# Optimizing a Trainium2 kernel written in Bass

```python
import math
import jax
import jax.numpy as jnp
from jax import lax
import numpy as np

D_MODEL = 1024
BATCH = 1
SEQ = 1024
DEPTH = 2

ROPE_THETA = 10000.0
NORM_EPS = 1e-6
Q_BLOCK = 128

DIFF_HEADS = 4
DIFF_HEAD_DIM = 64
DIFF_QK_WIDTH = DIFF_HEADS * 2 * DIFF_HEAD_DIM
DIFF_WIDTH = DIFF_HEADS * 2 * DIFF_HEAD_DIM
DIFF_SUBLN_EPS = 1e-5

MLA_HEADS = 4
MLA_NOPE_DIM = 64
MLA_ROPE_DIM = 32
MLA_V_DIM = 64
MLA_Q_RANK = 256
MLA_KV_RANK = 128
MLA_WIDTH = MLA_HEADS * MLA_V_DIM

RET_HEADS = 4
RET_QK_DIM = 64
RET_V_DIM = 64
RET_CHUNK = 128
RET_QK_WIDTH = RET_HEADS * RET_QK_DIM
RET_WIDTH = RET_HEADS * RET_V_DIM
RET_GN_EPS = 1e-6

MIX_WIDTH = DIFF_WIDTH + MLA_WIDTH + RET_WIDTH

IN_SIZES = (DIFF_QK_WIDTH, DIFF_QK_WIDTH, DIFF_WIDTH,
            MLA_Q_RANK, MLA_KV_RANK, MLA_ROPE_DIM,
            RET_QK_WIDTH, RET_QK_WIDTH, RET_WIDTH, RET_WIDTH)
IN_COLS = sum(IN_SIZES)

FFN_HIDDEN = -(-8 * D_MODEL // (3 * 256)) * 256

kernel_name = "hybrid_diff_mla_retention_block"

def _rms_norm(t, gain, eps=NORM_EPS):
    t32 = t.astype(jnp.float32)
    t32 = t32 * lax.rsqrt(jnp.mean(t32 * t32, axis=-1, keepdims=True) + eps)
    return t32.astype(t.dtype) * gain

def _rope_tables(positions, dim, dtype):
    inv_freq = 1.0 / (ROPE_THETA ** (jnp.arange(0, dim, 2, dtype=jnp.float32) / dim))
    ang = positions.astype(jnp.float32)[:, :, None] * inv_freq
    return (jnp.cos(ang)[:, :, None, :].astype(dtype),
            jnp.sin(ang)[:, :, None, :].astype(dtype))

def _apply_rope(t, cos, sin):
    t1, t2 = jnp.split(t, 2, axis=-1)
    return jnp.concatenate([t1 * cos - t2 * sin, t2 * cos + t1 * sin], axis=-1)

def _split_cols(t):
    out = []
    start = 0
    for n in IN_SIZES:
        out.append(t[..., start:start + n])
        start += n
    return out

def _sweep_query_blocks(block_fn, *qs):
    b, s = qs[0].shape[:2]
    nb = s // Q_BLOCK

    def to_blocks(t):
        return jnp.moveaxis(t.reshape((b, nb, Q_BLOCK) + t.shape[2:]), 1, 0)

    def body(args):
        return block_fn(args[0] * Q_BLOCK, *args[1:])

    out = lax.map(body, (jnp.arange(nb), *[to_blocks(t) for t in qs]))
    out = jnp.moveaxis(out, 0, 1)
    return out.reshape((b, s) + out.shape[3:])

def _causal_mask(q_start, s):
    q_pos = q_start + jnp.arange(Q_BLOCK)
    return jnp.arange(s)[None, :] <= q_pos[:, None]

def _masked_softmax(scores, mask):
    return jax.nn.softmax(jnp.where(mask, scores, -jnp.inf), axis=-1)

def _diff_attention(q, k, v, lam_q1, lam_k1, lam_q2, lam_k2, subln, lam_init, cos, sin):
    b, s, _ = q.shape
    q = q.reshape(b, s, DIFF_HEADS, 2, DIFF_HEAD_DIM)
    k = k.reshape(b, s, DIFF_HEADS, 2, DIFF_HEAD_DIM)
    q1 = _apply_rope(q[..., 0, :], cos, sin)
    q2 = _apply_rope(q[..., 1, :], cos, sin)
    k1 = _apply_rope(k[..., 0, :], cos, sin)
    k2 = _apply_rope(k[..., 1, :], cos, sin)
    v = v.reshape(b, s, DIFF_HEADS, 2 * DIFF_HEAD_DIM)
    f32 = jnp.float32
    lam = (jnp.exp(jnp.sum(lam_q1.astype(f32) * lam_k1.astype(f32)))
           - jnp.exp(jnp.sum(lam_q2.astype(f32) * lam_k2.astype(f32))) + lam_init)
    scale = DIFF_HEAD_DIM ** -0.5

    def block(q_start, q1b, q2b):
        mask = _causal_mask(q_start, s)
        a1 = _masked_softmax(jnp.einsum('bqhd,bkhd->bhqk', q1b, k1).astype(f32) * scale, mask)
        a2 = _masked_softmax(jnp.einsum('bqhd,bkhd->bhqk', q2b, k2).astype(f32) * scale, mask)
        return jnp.einsum('bhqk,bkhe->bqhe', (a1 - lam * a2).astype(v.dtype), v)

    o = _sweep_query_blocks(block, q1, q2)
    o = _rms_norm(o, subln, DIFF_SUBLN_EPS) * (1.0 - lam_init)
    return o.reshape(b, s, DIFF_WIDTH)

def _mla(c_q, c_kv, k_rope, q_norm, w_uq, kv_norm, w_ukv, cos, sin):
    b, s, _ = c_q.shape
    q = (_rms_norm(c_q, q_norm) @ w_uq).reshape(b, s, MLA_HEADS, MLA_NOPE_DIM + MLA_ROPE_DIM)
    q_nope = q[..., :MLA_NOPE_DIM]
    q_rope = _apply_rope(q[..., MLA_NOPE_DIM:], cos, sin)
    kv = (_rms_norm(c_kv, kv_norm) @ w_ukv).reshape(b, s, MLA_HEADS, MLA_NOPE_DIM + MLA_V_DIM)
    k_nope = kv[..., :MLA_NOPE_DIM]
    v = kv[..., MLA_NOPE_DIM:]
    k_rope = _apply_rope(k_rope[:, :, None, :], cos, sin)[:, :, 0, :]
    scale = (MLA_NOPE_DIM + MLA_ROPE_DIM) ** -0.5

    def block(q_start, qn, qr):
        mask = _causal_mask(q_start, s)
        scores = (jnp.einsum('bqhd,bkhd->bhqk', qn, k_nope)
                  + jnp.einsum('bqhr,bkr->bhqk', qr, k_rope))
        p = _masked_softmax(scores.astype(jnp.float32) * scale, mask)
        return jnp.einsum('bhqk,bkhe->bqhe', p.astype(v.dtype), v)

    o = _sweep_query_blocks(block, q_nope, q_rope)
    return o.reshape(b, s, MLA_WIDTH)

def _retention(q, k, v, g, gn_w, gn_b, cos, sin):
    b, s, _ = q.shape
    h, dk, dv, c = RET_HEADS, RET_QK_DIM, RET_V_DIM, RET_CHUNK
    nc = s // c
    dt = q.dtype
    q = _apply_rope(q.reshape(b, s, h, dk), cos, sin)
    k = _apply_rope(k.reshape(b, s, h, dk), cos, sin) * (dk ** -0.5)
    v = v.reshape(b, s, h, dv)
    log_gamma = jnp.log1p(-jnp.exp2(-5.0 - jnp.arange(h, dtype=jnp.float32)))
    pos = jnp.arange(c, dtype=jnp.float32)
    rel = pos[:, None] - pos[None, :]
    decay = jnp.where(rel[None] >= 0,
                      jnp.exp(jnp.maximum(rel, 0.0)[None] * log_gamma[:, None, None]),
                      0.0).astype(dt)
    xi = jnp.exp((pos[:, None] + 1.0) * log_gamma[None, :]).astype(dt)
    zeta = jnp.exp((c - 1.0 - pos)[:, None] * log_gamma[None, :]).astype(dt)
    chunk_decay = jnp.exp(c * log_gamma).astype(dt)
    qc = q.reshape(b, nc, c, h, dk)
    kc = k.reshape(b, nc, c, h, dk)
    vc = v.reshape(b, nc, c, h, dv)
    inner = jnp.einsum('bnihd,bnjhd->bnhij', qc, kc) * decay
    inner = jnp.einsum('bnhij,bnjhe->bnihe', inner, vc)

    def step(state, kv_chunk):
        k_i, v_i = kv_chunk
        new_state = (jnp.einsum('bjhd,bjhe->bhde', k_i * zeta[None, :, :, None], v_i)
                     + chunk_decay[None, :, None, None] * state)
        return new_state, state

    state0 = jnp.zeros((b, h, dk, dv), dt)
    _, prev_states = lax.scan(step, state0, (jnp.moveaxis(kc, 1, 0), jnp.moveaxis(vc, 1, 0)))
    cross = jnp.einsum('bnihd,nbhde->bnihe', qc, prev_states) * xi[None, None, :, :, None]
    o = (inner + cross).reshape(b, s, h, dv)
    o32 = o.astype(jnp.float32)
    mu = jnp.mean(o32, axis=-1, keepdims=True)
    var = jnp.mean(jnp.square(o32 - mu), axis=-1, keepdims=True)
    o = ((o32 - mu) * lax.rsqrt(var + RET_GN_EPS)).astype(dt).reshape(b, s, RET_WIDTH)
    o = o * gn_w + gn_b
    return jax.nn.silu(g) * o

def setup_inputs(seed: int = 0) -> dict:
    key = jax.random.key(seed)
    ks = jax.random.split(key, 24)
    f32 = jnp.float32
    L = DEPTH

    def dense(k, shape, fan_in):
        return jax.random.normal(k, shape, f32) * (fan_in ** -0.5)

    def gain(k, shape):
        return 1.0 + 0.01 * jax.random.normal(k, shape, f32)

    x = jax.random.normal(ks[0], (BATCH, SEQ, D_MODEL), f32)
    positions = (jnp.arange(SEQ, dtype=jnp.int32)[None, :]
                 + jax.random.randint(ks[1], (BATCH, 1), 0, 1024, dtype=jnp.int32))
    return {
        "x": x,
        "positions": positions,
        "attn_norm": gain(ks[2], (L, D_MODEL)),
        "w_in": dense(ks[3], (L, D_MODEL, IN_COLS), D_MODEL),
        "diff_lam_q1": 0.1 * jax.random.normal(ks[4], (L, DIFF_HEAD_DIM), f32),
        "diff_lam_k1": 0.1 * jax.random.normal(ks[5], (L, DIFF_HEAD_DIM), f32),
        "diff_lam_q2": 0.1 * jax.random.normal(ks[6], (L, DIFF_HEAD_DIM), f32),
        "diff_lam_k2": 0.1 * jax.random.normal(ks[7], (L, DIFF_HEAD_DIM), f32),
        "diff_subln": gain(ks[8], (L, 2 * DIFF_HEAD_DIM)),
        "mla_q_norm": gain(ks[9], (L, MLA_Q_RANK)),
        "mla_w_uq": dense(ks[10], (L, MLA_Q_RANK, MLA_HEADS * (MLA_NOPE_DIM + MLA_ROPE_DIM)), MLA_Q_RANK),
        "mla_kv_norm": gain(ks[11], (L, MLA_KV_RANK)),
        "mla_w_ukv": dense(ks[12], (L, MLA_KV_RANK, MLA_HEADS * (MLA_NOPE_DIM + MLA_V_DIM)), MLA_KV_RANK),
        "ret_gn_w": gain(ks[13], (L, RET_WIDTH)),
        "ret_gn_b": 0.01 * jax.random.normal(ks[14], (L, RET_WIDTH), f32),
        "w_out": dense(ks[15], (L, MIX_WIDTH, D_MODEL), MIX_WIDTH),
        "ffn_norm": gain(ks[16], (L, D_MODEL)),
        "w_gate": dense(ks[17], (L, D_MODEL, FFN_HIDDEN), D_MODEL),
        "w_up": dense(ks[18], (L, D_MODEL, FFN_HIDDEN), D_MODEL),
        "w_down": dense(ks[19], (L, FFN_HIDDEN, D_MODEL), FFN_HIDDEN),
        "final_norm": gain(ks[20], (D_MODEL,)),
    }

def reference(x, positions, attn_norm, w_in, diff_lam_q1, diff_lam_k1, diff_lam_q2,
              diff_lam_k2, diff_subln, mla_q_norm, mla_w_uq, mla_kv_norm, mla_w_ukv,
              ret_gn_w, ret_gn_b, w_out, ffn_norm, w_gate, w_up, w_down, final_norm):
    dt = x.dtype
    cos_d, sin_d = _rope_tables(positions, DIFF_HEAD_DIM, dt)
    cos_m, sin_m = _rope_tables(positions, MLA_ROPE_DIM, dt)
    cos_r, sin_r = _rope_tables(positions, RET_QK_DIM, dt)
    for layer in range(DEPTH):
        h = _rms_norm(x, attn_norm[layer])
        (d_q, d_k, d_v, m_cq, m_ckv, m_krope,
         r_q, r_k, r_v, r_g) = _split_cols(h @ w_in[layer])
        lam_init = 0.8 - 0.6 * math.exp(-0.3 * layer)
        o_diff = _diff_attention(d_q, d_k, d_v, diff_lam_q1[layer], diff_lam_k1[layer],
                                 diff_lam_q2[layer], diff_lam_k2[layer], diff_subln[layer],
                                 lam_init, cos_d, sin_d)
        o_mla = _mla(m_cq, m_ckv, m_krope, mla_q_norm[layer], mla_w_uq[layer],
                     mla_kv_norm[layer], mla_w_ukv[layer], cos_m, sin_m)
        o_ret = _retention(r_q, r_k, r_v, r_g, ret_gn_w[layer], ret_gn_b[layer], cos_r, sin_r)
        mixed = jnp.concatenate([o_diff, o_mla, o_ret], axis=-1)
        x = x + mixed @ w_out[layer]
        h = _rms_norm(x, ffn_norm[layer])
        x = x + (jax.nn.silu(h @ w_gate[layer]) * (h @ w_up[layer])) @ w_down[layer]
    return _rms_norm(x, final_norm)


_drawn_inputs = setup_inputs


def setup_inputs(seed=0):
    import zlib

    import numpy as np

    out = dict(_drawn_inputs(seed))
    spreads = {}
    factors = {'attn_norm': 3.706,
     'diff_subln': 7.842,
     'mla_q_norm': 8.0,
     'mla_kv_norm': 8.0,
     'ret_gn_w': 8.0,
     'ret_gn_b': 8.0,
     'ffn_norm': 6.233,
     'final_norm': 5.914}
    for name, (base, spread) in spreads.items():
        noise = np.random.default_rng([zlib.crc32(name.encode()), seed]).standard_normal(out[name].shape)
        drawn = base * np.exp(spread * noise) if base else spread * noise
        out[name] = jnp.asarray(drawn.astype(out[name].dtype))
    for name, factor in factors.items():
        out[name] = (out[name] * factor).astype(out[name].dtype)
    return out
```

```python
import math
from contextlib import ExitStack

import numpy as np

import concourse.bass as bass
from concourse import mybir

F32 = mybir.dt.float32
F32R = mybir.dt.float32r
I32 = mybir.dt.int32
ALU = mybir.AluOpType
ACT = mybir.ActivationFunctionType
AX_X = mybir.AxisListType.X

P = 128
DEPTH = 2
SEQ = 1024
D = 1024
T = SEQ // P
KD = D // P
DESC = range(T - 1, -1, -1)

DIFF_HEADS, DIFF_DIM = 4, 64
MLA_HEADS, NOPE, ROPE, MLA_V = 4, 64, 32, 64
MLA_QK = NOPE + ROPE
Q_RANK, KV_RANK = 256, 128
RET_HEADS, RET_DIM = 4, 64
RET_PAIRS = RET_HEADS // 2
FFN = 2816
GROUP = 256
GROUPS = FFN // GROUP
GM = GROUP // P

DIFF_W = DIFF_HEADS * 2 * DIFF_DIM
RET_W = RET_HEADS * RET_DIM
COL_DQ, COL_DK, COL_DV = 0, DIFF_W, 2 * DIFF_W
COL_MLA = 3 * DIFF_W
MLA_COLS = Q_RANK + KV_RANK + ROPE
COL_RET = COL_MLA + MLA_COLS
MIX_MLA = DIFF_W
MIX_RET = DIFF_W + MLA_HEADS * MLA_V

NORM_EPS, SUBLN_EPS, GN_EPS = 1e-6, 1e-5, 1e-6
DIFF_SCALE = DIFF_DIM ** -0.5
MLA_SCALE = MLA_QK ** -0.5
NEG = -1e30

CH_DIFF, CH_MLA, CH_UKV, CH_RET, CH_OUT, CHUNKS = 0, 4, 5, 6, 8, 10
Z_MLA, Z_RET, Z_UNITS = 4 * T, 5 * T, 7 * T
ROPE_RET = 4 * T
ATT_UNITS = DIFF_HEADS * T + MLA_HEADS * T


def groups_of_four(t):
    return (t + 4) // 4


PT_RINGS = sum(groups_of_four(t) for t in range(T))
RING = 2 * KD + 4 * (T + PT_RINGS) + (T + 4 * (T + PT_RINGS)) + 2 * T + 2 * 2 * KD

PER = dict(
    params_in=16 * 8, ret_in=16 * 3, x_saved=16, x_back=16, mix_in=16 * 2,
    w_in0=16 * (3 + 3 + 1 + 4 + 1), w_in1=16 * (3 + 3 + 4 + 4 + 1), w_gain=1, w_hi=CHUNKS, w_lo=CHUNKS,
    lam=5, n_sq=2 * T, n_ms=4, n_rstd=4, n_xn=2 * T, tr_done=RING, tr_hi=RING, tr_free=RING,
    z_done=Z_UNITS, z_free=Z_UNITS, rope_ab=6 * T, rope_sum=6 * T, v_hi=6 * T,
    s_done=2 * DIFF_HEADS * T + MLA_HEADS * T, s_max=2 * DIFF_HEADS * T + MLA_HEADS * T,
    s_exp=2 * DIFF_HEADS * T + MLA_HEADS * T,
    inv_sum=ATT_UNITS, lam_ratio=DIFF_HEADS * T, p_ready=DIFF_HEADS * T, pv_done=ATT_UNITS, o_free=ATT_UNITS,
    o_sq=DIFF_HEADS * T, o_ms=2 * DIFF_HEADS * T, o_rr=DIFF_HEADS * T,
    mix_out0=16 * (16 + 16 + 8), mix_out1=16 * (16 + 16 + 8),
    m_sq=T, m_sq2=T, m_ms=2 * T, m_rstd=T, m_kab=T, m_krope=T, u_done=T, m_nope=T, m_vhi=T, m_qab=T, u_free=T,
    m_qrope=T,
    r_xz=2 * T, r_kzhi=2 * T, r_kzlo=2 * T, ri_done=2 * T, r_at=2 * T, r_athi=2 * T, r_atlo=2 * T,
    ro_done=2 * T, rs_done=2 * (T - 1), r_st=2 * (T - 1), r_sthi=2 * (T - 1), r_stlo=2 * (T - 1),
    r_bn=2 * T, r_mv=2 * T, r_ms=2 * T, r_rstd=2 * T, r_on=2 * T, r_gw=2 * T, r_gb=2 * T, r_mx=2 * T,
    out_done=2 * T, out_add=2 * T,
    fg_in0=32 * GROUPS, fg_in1=32 * GROUPS, fd_in=16 * GROUPS, f_hi=3 * GROUPS, f_lo=3 * GROUPS,
    gu_done=4 * GROUPS, f_silu=4 * GROUPS, f_mul=4 * GROUPS, f_ahi=4 * GROUPS, f_act=4 * GROUPS,
    fd_done=2 * T * GROUPS, d_add=2 * T * GROUPS,
)
GU_CREDIT, D_CREDIT, ADD_CREDIT = 1, 1, 2 * T

C_IDENT, C_MASK, C_XZ, C_CD, C_INVF, C_LAM = 0, P, 2 * P, 2 * P + 8, 2 * P + 10, 2 * P + 58
C_COLS = C_LAM + 2 * DEPTH


def constants():
    c = np.zeros((P, C_COLS), np.float32)
    c[:, C_IDENT:C_IDENT + P] = np.eye(P)
    c[:, C_MASK:C_MASK + P] = np.triu(np.full((P, P), NEG), 1)
    log_gamma = np.log1p(-np.exp2(-5.0 - np.arange(RET_HEADS, dtype=np.float32))).astype(np.float32)
    pos = np.arange(P, dtype=np.float32)
    xi = np.exp((pos[:, None] + 1.0) * log_gamma[None, :])
    zeta = np.exp((P - 1.0 - pos)[:, None] * log_gamma[None, :]) * RET_DIM ** -0.5
    for p in range(RET_PAIRS):
        c[:, C_XZ + 4 * p:C_XZ + 4 * p + 2] = xi[:, 2 * p:2 * p + 2]
        c[:, C_XZ + 4 * p + 2:C_XZ + 4 * p + 4] = zeta[:, 2 * p:2 * p + 2]
        c[:64, C_CD + p] = np.exp(P * log_gamma[2 * p])
        c[64:, C_CD + p] = np.exp(P * log_gamma[2 * p + 1])
    for at, dim in ((0, DIFF_DIM), (32, ROPE)):
        freq = np.float32(1.0) / (np.float32(10000.0) ** (np.arange(0, dim, 2, dtype=np.float32) / np.float32(dim)))
        c[:, C_INVF + at:C_INVF + at + dim // 2] = freq
    for layer in range(DEPTH):
        init = 0.8 - 0.6 * math.exp(-0.3 * layer)
        c[:, C_LAM + 2 * layer:C_LAM + 2 * layer + 2] = (init, 1.0 - init)
    rel = pos[None, :] - pos[:, None]
    decay = np.where(rel[:, None, :] >= 0, np.exp(np.maximum(rel, 0.0)[:, None, :] * log_gamma[None, :, None]), 0.0)
    return c, (decay * RET_DIM ** -0.5).astype(np.float32).reshape(P, RET_HEADS * P)


def hybrid_block_kernel(nc, x, positions, attn_norm, w_in, diff_lam_q1, diff_lam_k1, diff_lam_q2, diff_lam_k2,
                        diff_subln, mla_q_norm, mla_w_uq, mla_kv_norm, mla_w_ukv, ret_gn_w, ret_gn_b, w_out,
                        ffn_norm, w_gate, w_up, w_down, final_norm, out):
    const_np, decay_np = constants()
    const_dram = nc.inline_tensor(const_np, name="const_table").ap()
    decay_dram = nc.inline_tensor(decay_np, name="decay_table").ap()
    mixed_dram = nc.dram_tensor("mixed_scratch", (SEQ, D), F32, kind="Internal").ap()
    x_dram = nc.dram_tensor("x_scratch", (SEQ, D), F32, kind="Internal").ap()

    base = 16512
    KB = 1024
    HT, WSLOT, XREG, EREG, MREG, CREG = 0, 64 * KB, 128 * KB, 160 * KB, 176 * KB, 200 * KB

    def sb(name, shape, dt, at):
        return nc.alloc_sbuf_tensor_at(name, shape, dt, offset=base + at)

    ht_hi = sb("ht_hi", [P, KD, SEQ], F32R, HT)
    ht_lo = sb("ht_lo", [P, KD, SEQ], F32R, HT + 32 * KB)

    def weight(name, shape, at):
        size = 4 * int(np.prod(shape[1:]))
        return (sb(name + "_hi", shape, F32R, at), sb(name + "_lo", shape, F32R, at + size),
                sb(name + "_raw", shape, F32, at + size))

    slots = [WSLOT, WSLOT + 32 * KB]
    w_diff = [weight(f"w_diff{i}", [P, KD, 3 * P], slots[i]) for i in range(2)]
    w_mla = weight("w_mla", [P, KD, MLA_COLS], slots[0])
    w_uq = weight("w_uq", [P, Q_RANK // P, MLA_HEADS * MLA_QK], slots[1])
    w_ukv = weight("w_ukv", [P, MLA_HEADS * (NOPE + MLA_V)], slots[1] + 8 * KB)
    w_ret = [weight(f"w_ret{i}", [P, KD, 4 * P], slots[i]) for i in range(2)]
    w_o = [weight(f"w_o{i}", [P, KD, 512], slots[i]) for i in range(2)]
    w_gu = [weight(f"w_gu{m}", [P, 2, KD, P], slots[0] + 16 * KB * m) for m in range(2)]
    w_dn = weight("w_dn", [P, GM, D], slots[1])

    X = sb("X", [P, T, D], F32, XREG)
    dq_hi = sb("dq_hi", [P, 2, SEQ], F32R, XREG)
    dq_lo = sb("dq_lo", [P, 2, SEQ], F32R, XREG + 8 * KB)
    dk = sb("dk", [P, 2, SEQ], F32R, XREG + 16 * KB)
    dv_hi = sb("dv_hi", [P, T, P], F32R, XREG + 24 * KB)
    dv_lo = sb("dv_lo", [P, T, P], F32R, XREG + 28 * KB)
    mq_hi = sb("mq_hi", [MLA_QK, SEQ], F32R, XREG)
    mq_lo = sb("mq_lo", [MLA_QK, SEQ], F32R, XREG + 4 * KB)
    mk_hi = sb("mk_hi", [MLA_QK, SEQ], F32R, XREG + 8 * KB)
    mk_lo = sb("mk_lo", [MLA_QK, SEQ], F32R, XREG + 12 * KB)
    mv_hi = sb("mv_hi", [P, T, MLA_HEADS, MLA_V], F32R, XREG + 16 * KB)
    mv_lo = sb("mv_lo", [P, T, MLA_HEADS, MLA_V], F32R, XREG + 24 * KB)

    pt_hi = sb("pt_hi", [P, T, P], F32R, EREG)
    pt_lo = sb("pt_lo", [P, T, P], F32R, EREG + 4 * KB)
    expo = [sb("expo0", [P, 2, SEQ], F32, EREG + 8 * KB), sb("expo1", [P, 2, SEQ], F32, MREG)]
    mexpo = [sb(f"mexpo{i}", [P, SEQ], F32, EREG + (8 + 4 * i) * KB) for i in range(2)]
    rope_a = [sb(f"rope_a{i}", [P, 4, 2, 32], F32, MREG + (8 + i) * KB) for i in range(2)]
    rope_b = [sb(f"rope_b{i}", [P, 4, 2, 32], F32, MREG + (10 + i) * KB) for i in range(2)]
    qk_rot = [sb(f"qk_rot{i}", [P, 4, 2, 64], F32, MREG + (12 + 2 * i) * KB) for i in range(2)]
    d_mx = [sb(f"d_mx{i}", [P, P], F32, MREG + 16 * KB + 512 * i) for i in range(2)]
    square_out = sb("square_out", [P, P], F32, MREG + 17 * KB)
    m_q = sb("m_q", [P, T, MLA_HEADS, MLA_QK], F32, MREG)
    m_k = sb("m_k", [P, T, MLA_HEADS, MLA_QK], F32, MREG + 12 * KB)
    cn = sb("cn", [P, 3, P], F32, EREG)
    ct_hi = sb("ct_hi", [P, 3, P], F32R, EREG + 1536)
    ct_lo = sb("ct_lo", [P, 3, P], F32R, EREG + 3072)
    mk_a = sb("mk_a", [P, 2, 16], F32, EREG + 4608)
    mk_b = sb("mk_b", [P, 2, 16], F32, EREG + 4736)
    mq_a = sb("mq_a", [P, MLA_HEADS, 2, 16], F32, EREG + 5120)
    mq_b = sb("mq_b", [P, MLA_HEADS, 2, 16], F32, EREG + 5632)
    m_square = sb("m_square", [P, Q_RANK], F32, EREG + 6144)
    decay = sb("decay", [P, RET_PAIRS, 2 * P], F32, EREG)
    gn_w = sb("gn_w", [P, RET_W], F32, EREG + 2 * KB)
    gn_b = sb("gn_b", [P, RET_W], F32, EREG + 3 * KB)
    rt_hi = [sb(f"rt_hi{i}", [P, 3, P], F32R, EREG + 4 * KB + 1536 * i) for i in range(2)]
    rt_lo = [sb(f"rt_lo{i}", [P, 3, P], F32R, EREG + 7 * KB + 1536 * i) for i in range(2)]
    rk_hi = [sb(f"rk_hi{i}", [P, P], F32R, EREG + 10 * KB + 512 * i) for i in range(2)]
    rk_lo = [sb(f"rk_lo{i}", [P, P], F32R, EREG + 11 * KB + 512 * i) for i in range(2)]
    rv_hi = [sb(f"rv_hi{i}", [P, P], F32R, EREG + 12 * KB + 512 * i) for i in range(3)]
    rv_lo = [sb(f"rv_lo{i}", [P, P], F32R, EREG + 12 * KB + 1536 + 512 * i) for i in range(3)]
    r_ab = [(sb(f"r_a{i}", [P, 4, 2, 32], F32, MREG + 2 * i * KB),
             sb(f"r_b{i}", [P, 4, 2, 32], F32, MREG + (2 * i + 1) * KB)) for i in range(2)]
    r_rot = [sb(f"r_rot{i}", [P, 4, 64], F32, MREG + (4 + i) * KB) for i in range(2)]
    r_xzt = [sb(f"r_xzt{i}", [P, 4, 64], F32, MREG + (6 + i) * KB) for i in range(2)]
    r_at = sb("r_at", [P, 2 * P], F32, MREG + 8 * KB)
    r_at_hi = sb("r_at_hi", [P, 2 * P], F32R, MREG + 9 * KB)
    r_at_lo = sb("r_at_lo", [P, 2 * P], F32R, MREG + 10 * KB)
    r_st = sb("r_st", [P, P], F32, MREG + 11 * KB)
    r_st_hi = [sb(f"r_st_hi{i}", [P, P], F32R, MREG + 12 * KB + 512 * i) for i in range(2)]
    r_st_lo = [sb(f"r_st_lo{i}", [P, P], F32R, MREG + 13 * KB + 512 * i) for i in range(2)]
    r_gate = [sb(f"r_gate{i}", [P, P], F32, MREG + 14 * KB + 512 * i) for i in range(3)]
    r_norm = [sb(f"r_norm{i}", [P, P], F32, MREG + 16 * KB + 512 * i) for i in range(2)]
    r_mx = [sb(f"r_mx{i}", [P, P], F32, MREG + 17 * KB + 512 * i) for i in range(2)]
    rows = sb("rows", [P, 4, D], F32, MREG)
    row_square = sb("row_square", [P, D], F32, MREG + 16 * KB)
    act_hi = sb("act_hi", [P, GM, SEQ], F32R, EREG)
    act_lo = sb("act_lo", [P, GM, SEQ], F32R, EREG + 8 * KB)
    f_gate = [sb(f"f_gate{i}", [P, 512], F32, MREG + 2 * i * KB) for i in range(2)]
    f_prod = [sb(f"f_prod{i}", [P, 512], F32, MREG + (4 + 2 * i) * KB) for i in range(2)]
    final_gain = sb("final_gain", [P, D], F32, EREG)
    ang, turns, red, cosarg = (sb(n, [P, T, 48], F32, EREG + 1536 * i) for i, n in
                               enumerate(("ang", "turns", "red", "cosarg")))
    pos_int = sb("pos_int", [P, T], I32, EREG + 6144)
    pos_f = sb("pos_f", [P, T], F32, EREG + 6400)
    consts = sb("consts", [P, C_COLS], F32, EREG + 7 * KB)
    at = [CREG]

    def keep(name, shape, dt=F32):
        size = -(-4 * int(np.prod(shape[1:])) // 32) * 32
        at[0] += size
        return sb(name, shape, dt, at[0] - size)

    ident = keep("ident", [P, P])
    ident_r = keep("ident_r", [P, P], F32R)
    mask_r = keep("mask_r", [P, P], F32R)
    subln = keep("subln", [P, P])
    cos_d = keep("cos_d", [P, T, 32])
    sin_d = keep("sin_d", [P, T, 2, 32])
    cos_m = keep("cos_m", [P, T, 16])
    sin_m = keep("sin_m", [P, T, 2, 16])
    stats = keep("stats", [P, 144])
    taken = [0]

    def small(*shape):
        size = int(np.prod(shape))
        taken[0] += size
        cols = stats[:, taken[0] - size:taken[0]]
        if len(shape) == 1:
            return cols
        names = "abc"[:len(shape)]
        return cols.rearrange(f"p ({' '.join(names)}) -> p {' '.join(names)}", **dict(zip(names, shape)))

    xz = small(2, 4)
    cd = small(2)
    lam_const = small(2)
    m_mx = [keep(f"m_mx{i}", [P, MLA_V]) for i in range(2)]
    attn_gain = small(KD)
    ffn_gain = small(KD)
    q_gain = small(2)
    kv_gain = small(1)
    lam_sum = small(2)
    lam_exp = small(2)
    neg_lam = small(1)
    row_ss = small(T)
    row_ms = small(T)
    row_rstd = small(T)
    neg_max = small(2, 2)
    exp_sum = small(2, 2)
    inv_sum = small(2, 2)
    ratio = small(2)
    o_ss = small(2)
    o_ms = small(2)
    o_rs = small(2)
    o_rr = small(2)
    m_ss = small(2, 2)
    m_msq = small(2, 2)
    m_rs = small(2, 2)
    bn = small(2, 2, 6)
    mv = small(2, 2, 2)
    r_rs = small(2, 2)
    r_ms = small(2, 2)
    minus_half = small(4)
    assert taken[0] <= 144, taken[0]
    assert base + at[0] <= nc.sbuf_usable_end, at[0] - CREG
    lam_vec = sb("lam_vec", [P, 4, DIFF_DIM], F32, MREG + 20 * KB)
    lam_prod = sb("lam_prod", [P, DIFF_DIM], F32, MREG + 21 * KB)

    ctx = ExitStack()
    with ctx:
        ctx.enter_context(nc.allow_non_contiguous_dma(reason="columns of gains and positions, a few KB"))
        banks = ctx.enter_context(nc.psum_tensor("banks", [P, 8, 512], F32))
        S = {name: ctx.enter_context(nc.semaphore(name)) for name in PER}
        S |= {name: ctx.enter_context(nc.semaphore(name)) for name in
              ("passed", "const_in", "x_in", "pos_in", "tab_dve", "tab_act", "ident_ok", "half_ok", "final_in", "f_sq", "f_ms", "f_rstd", "y_ready",
                 "y_out0", "y_out1", "y_out2", "y_out3")}

        SCORE = [banks[:, 0:2, :].rearrange("p b n -> p (b n)"), banks[:, 2:4, :].rearrange("p b n -> p (b n)")]
        Z_BANK, O_BANK = 4, 7
        TR_BANKS = (5, 6)
        NORM_BANKS = (4, 5, 6, 7)
        RET_INNER, RET_STATE, RET_OUT = (0, 1), 7, (2, 3)

        def tokens(t, n=1):
            return slice(t * P, (t + n) * P)

        STEPS = range(T + 2)

        block = ctx.enter_context(nc.Block())

        @block.sync
        def _(sp):
            sp.dma_start(consts[:], const_dram).then_inc(S["const_in"], 16)
            sp.dma_start(ident[:], const_dram[:, C_IDENT:C_IDENT + P]).then_inc(S["const_in"], 16)
            sp.dma_start(xz[:], const_dram[:, C_XZ:C_XZ + 8]).then_inc(S["const_in"], 16)
            sp.dma_start(cd[:], const_dram[:, C_CD:C_CD + 2]).then_inc(S["const_in"], 16)
            sp.dma_start(pos_int[:], positions.rearrange("b (t p) -> p (b t)", p=P)).then_inc(S["pos_in"], 16)
            sp.dma_start(X[:], x[0].rearrange("(t p) d -> p t d", p=P)).then_inc(S["x_in"], 16)
            const2 = const_dram[:, C_LAM:C_LAM + 2 * DEPTH].rearrange("p (l c) -> l p c", l=DEPTH)
            mixed = mixed_dram.rearrange("(t p) d -> t p d", p=P)

            with sp.Fori(0, DEPTH) as L:

                def arrives(dst, src, name):
                    sp.dma_start(dst, src).then_inc(S[name], 16)

                arrives(attn_gain[:], attn_norm[L].rearrange("(k p) -> p k", p=P), "params_in")
                arrives(lam_const[:], const2[L], "params_in")
                for i, v in enumerate((diff_lam_q1, diff_lam_k1, diff_lam_q2, diff_lam_k2)):
                    arrives(lam_vec[:, i, :], v[L].partition_broadcast(P), "params_in")
                arrives(subln[:], diff_subln[L].partition_broadcast(P), "params_in")
                arrives(ffn_gain[:], ffn_norm[L].rearrange("(k p) -> p k", p=P), "params_in")

                def load_columns(chunk, w, starts, width):
                    src = w_in[L].rearrange("(k p) n -> p k n", p=P)
                    for i, start in enumerate(starts):
                        arrives(w[:, :, i * width:(i + 1) * width], src[:, :, start:start + width],
                                f"w_in{chunk % 2}")

                def load_diff(h):
                    load_columns(h, w_diff[h % 2][2], [c + h * P for c in (COL_DQ, COL_DK, COL_DV)], P)

                def load_ret(p):
                    load_columns(CH_RET + p, w_ret[p][2], [COL_RET + i * RET_W + p * P for i in range(4)], P)

                def load_out(c):
                    arrives(w_o[c][2][:], w_out[L].rearrange("(k p) n -> p k n", p=P)[:, :, c * 512:(c + 1) * 512],
                            f"w_in{c}")

                sp.wait_ge(S["gu_done"], L * PER["gu_done"] + GU_CREDIT)
                load_diff(0)
                sp.wait_ge(S["fd_done"], L * PER["fd_done"] + D_CREDIT)
                load_diff(1)
                sp.wait_ge(S["x_in"], 16)
                sp.wait_ge(S["d_add"], L * PER["d_add"] + ADD_CREDIT)
                arrives(x_dram.rearrange("(t p) d -> p t d", p=P), X[:], "x_saved")

                def next_chunk(h):
                    sp.wait_ge(S["z_done"], L * PER["z_done"] + T * (h + 1))
                    if h + 2 < DIFF_HEADS:
                        load_diff(h + 2)
                    elif h + 2 == CH_MLA:
                        arrives(w_mla[2][:], w_in[L].rearrange("(k p) n -> p k n", p=P)[:, :, COL_MLA:COL_MLA + MLA_COLS],
                                "w_in0")
                    elif h + 2 == CH_UKV:
                        arrives(q_gain[:], mla_q_norm[L].rearrange("(k p) -> p k", p=P), "w_in1")
                        arrives(w_uq[2][:], mla_w_uq[L].rearrange("(k p) n -> p k n", p=P), "w_in1")
                        arrives(kv_gain[:], mla_kv_norm[L].rearrange("(k p) -> p k", p=P), "w_in1")
                        arrives(w_ukv[2][:], mla_w_ukv[L], "w_in1")

                def store_mixed(ready, n, t, col, width, tile, unit):
                    sp.wait_ge(S[ready], L * PER[ready] + n)
                    arrives(mixed[t][:, col:col + width], tile, f"mix_out{unit % 2}")

                next_chunk(0)
                for h in range(DIFF_HEADS):
                    for t in DESC:
                        a = h * T + (T - 1 - t)
                        store_mixed("o_free", a + 1, t, h * P, P, d_mx[a % 2][:], a)
                        if t == 0 and h + 1 < DIFF_HEADS:
                            next_chunk(h + 1)
                sp.wait_ge(S["z_done"], L * PER["z_done"] + Z_MLA + T)
                load_ret(0)
                for h in range(MLA_HEADS):
                    for t in DESC:
                        a = DIFF_HEADS * T + h * T + (T - 1 - t)
                        store_mixed("o_free", a + 1, t, MIX_MLA + h * MLA_V, MLA_V, m_mx[a % 2][:], a)
                        if h == 0 and t == T - 1:
                            sp.wait_ge(S["u_done"], L * PER["u_done"] + T)
                            load_ret(1)
                sp.wait_ge(S["pv_done"], L * PER["pv_done"] + ATT_UNITS)
                arrives(decay[:], decay_dram.rearrange("p (a n) -> p a n", a=RET_PAIRS), "ret_in")
                arrives(gn_w[:], ret_gn_w[L].partition_broadcast(P), "ret_in")
                arrives(gn_b[:], ret_gn_b[L].partition_broadcast(P), "ret_in")
                sp.wait_ge(S["x_saved"], L * PER["x_saved"] + 16)
                arrives(X[:], x_dram.rearrange("(t p) d -> p t d", p=P), "x_back")
                for p in range(RET_PAIRS):
                    for t in range(T):
                        n = p * T + t
                        if t == T - 2:
                            sp.wait_ge(S["z_done"], L * PER["z_done"] + Z_RET + (p + 1) * T)
                            load_out(p)
                        store_mixed("r_mx", n + 1, t, MIX_RET + p * P, P, r_mx[n % 2][:], n)
                sp.wait_ge(S["mix_out0"], L * PER["mix_out0"] + PER["mix_out0"])
                sp.wait_ge(S["mix_out1"], L * PER["mix_out1"] + PER["mix_out1"])
                for half in range(2):
                    if half:
                        sp.wait_ge(S["tr_done"], L * PER["tr_done"] + RING - 3 * 2 * KD + 2 * KD + KD)
                    arrives(rows[:], mixed_dram.rearrange("(t p) d -> p t d", p=P)[:, 4 * half:4 * half + 4, :], "mix_in")

                wgv = w_gate[L].rearrange("(k p) n -> p k n", p=P)
                wuv = w_up[L].rearrange("(k p) n -> p k n", p=P)
                wdv = w_down[L].rearrange("(g k p) n -> g p k n", p=P, k=GM)

                def load_gu(g, m):
                    arrives(w_gu[m][2][:, 0], wgv[:, :, bass.ds(g * GROUP + m * P, P)], f"fg_in{m}")
                    arrives(w_gu[m][2][:, 1], wuv[:, :, bass.ds(g * GROUP + m * P, P)], f"fg_in{m}")

                sp.wait_ge(S["out_done"], L * PER["out_done"] + T)
                load_gu(0, 0)
                load_gu(0, 1)
                sp.wait_ge(S["out_done"], L * PER["out_done"] + 2 * T)
                arrives(w_dn[2][:], wdv[0], "fd_in")
                with sp.Fori(1, GROUPS) as g:
                    for m in range(GM):
                        sp.wait_ge(S["gu_done"], L * PER["gu_done"] + g * 4 + (2 * (m + 1) - 4 + GU_CREDIT))
                        load_gu(g, m)
                    sp.wait_ge(S["fd_done"], L * PER["fd_done"] + g * 2 * T + D_CREDIT)
                    arrives(w_dn[2][:], wdv[g], "fd_in")

            sp.wait_ge(S["fd_done"], DEPTH * PER["fd_done"] + D_CREDIT)
            sp.dma_start(final_gain[:], final_norm.partition_broadcast(P)).then_inc(S["final_in"], 16)
            for t in range(T):
                sp.wait_ge(S["y_ready"], t + 1)
                sp.dma_start(out[0].rearrange("(t p) d -> t p d", p=P)[t], rows[:, t % 4, :]).then_inc(S[f"y_out{t % 4}"], 16)
            for i in range(4):
                sp.wait_ge(S[f"y_out{i}"], 16 * T // 4)

        @block.tensor
        def _(pe):
            pe.wait_ge(S["const_in"], 64)
            pe.wait_ge(S["ident_ok"], 2)
            pe.sem_inc(S["gu_done"], GU_CREDIT)
            pe.sem_inc(S["fd_done"], D_CREDIT)

            def products(bank, pairs, first=True, last=True):
                mm = None
                for i, (lhsT, rhs) in enumerate(pairs):
                    mm = pe.matmul(bank, lhsT, rhs, start=first and i == 0, stop=last and i == len(pairs) - 1)
                return mm

            def split(a, b):
                return [(a[0], b[0]), (a[0], b[1]), (a[1], b[0])]

            with pe.Fori(0, DEPTH) as L:
                ring, freed = [0], [0]

                def ring_empty():
                    if ring[0] > freed[0]:
                        pe.wait_ge(S["tr_free"], L * PER["tr_free"] + ring[0])
                    freed[0] = ring[0]

                def take_ring(n_banks=2):
                    r = ring[0]
                    if r - n_banks + 1 > freed[0]:
                        pe.wait_ge(S["tr_free"], L * PER["tr_free"] + r - n_banks + 1)
                    ring[0] += 1
                    return banks[:, (TR_BANKS if n_banks == 2 else NORM_BANKS)[r % n_banks], :]

                def transpose_rows(ready, counts):
                    for half in range(2):
                        pe.wait_ge(S[ready], L * PER[ready] + counts[half])
                        for k in range(KD):
                            bank = take_ring(4)
                            for j in range(4):
                                tr = pe.transpose(bank[:, tokens(j)], rows[:, j, tokens(k)], ident[:])
                            tr.then_inc(S["tr_done"], 1)

                def project(u, t, chunk, w, n):
                    pe.wait_ge(S["w_hi"], L * PER["w_hi"] + chunk + 1)
                    pe.wait_ge(S["w_lo"], L * PER["w_lo"] + chunk + 1)
                    if u >= 1:
                        pe.wait_ge(S["z_free"], L * PER["z_free"] + u)
                    bank = banks[:, Z_BANK, 0:n]
                    pairs = [pair for k in range(KD) for pair in
                             split((ht_hi[:, k, tokens(t)], ht_lo[:, k, tokens(t)]), (w[0][:, k, :], w[1][:, k, :]))]
                    products(bank, pairs).then_inc(S["z_done"], 1)

                transpose_rows("n_xn", (4, 8))
                ring_empty()

                qk_ready = {}

                def diff_transpose(h, t):
                    u = h * T + (T - 1 - t)
                    pe.wait_ge(S["rope_sum"], L * PER["rope_sum"] + u + 1)
                    bank = take_ring()
                    for v in range(4):
                        tr = pe.transpose(bank[:, tokens(v)], qk_rot[u % 2][:, v].rearrange("p c d -> p (c d)"), ident[:])
                    tr.then_inc(S["tr_done"], 1)
                    qk_ready[h] = ring[0]

                def diff_scores(h, t):
                    a = h * T + (T - 1 - t)
                    if t == T - 1:
                        pe.wait_ge(S["tr_free"], L * PER["tr_free"] + qk_ready[h])
                    for m in range(2):
                        j = 2 * a + m
                        if j >= 2:
                            pe.wait_ge(S["s_exp"], L * PER["s_exp"] + j - 1)
                        for c in range(0, (t + 1) * P, 512):
                            n = min(512, (t + 1) * P - c)
                            diagonal = c + n == (t + 1) * P
                            keys = dk[:, m, c:c + n]
                            mm = products(SCORE[m][:, c:c + n], [(dq_hi[:, m, tokens(t)], keys), (dq_lo[:, m, tokens(t)], keys)],
                                          last=not diagonal)
                        mm = pe.matmul(SCORE[m][:, tokens(t)], ident_r[:], mask_r[:], start=False, stop=True)
                        mm.then_inc(S["s_done"], 1)

                def transpose_probs(tile, t):
                    for b in range(0, t + 1, 4):
                        bank = take_ring()
                        for kb in range(b, min(b + 4, t + 1)):
                            tr = pe.transpose(bank[:, tokens(kb - b)], tile[:, tokens(kb)], ident[:])
                        tr.then_inc(S["tr_done"], 1)

                def diff_output(h, t):
                    a = h * T + (T - 1 - t)
                    pe.wait_ge(S["p_ready"], L * PER["p_ready"] + a + 1)
                    transpose_probs(expo[a % 2][:, 0, :], t)
                    pe.wait_ge(S["z_free"], L * PER["z_free"] + (h + 1) * T)
                    if a >= 1:
                        pe.wait_ge(S["o_free"], L * PER["o_free"] + a)
                    ring_empty()
                    pairs = [pair for kb in range(t + 1) for pair in
                             split((pt_hi[:, kb, :], pt_lo[:, kb, :]), (dv_hi[:, kb, :], dv_lo[:, kb, :]))]
                    products(banks[:, O_BANK, 0:P], pairs).then_inc(S["pv_done"], 1)

                for h in range(-1, DIFF_HEADS):
                    for s in STEPS:
                        t = T - 1 - s
                        if h >= 0 and s < T:
                            diff_scores(h, t)
                        if h + 1 < DIFF_HEADS and 1 <= s <= T:
                            project((h + 1) * T + s - 1, t + 1, h + 1, w_diff[(h + 1) % 2], 3 * P)
                        if h + 1 < DIFF_HEADS and 2 <= s:
                            diff_transpose(h + 1, t + 2)
                        if h >= 0 and 1 <= s <= T:
                            diff_output(h, t + 1)

                def mla_latents(t):
                    u = T - 1 - t
                    project(Z_MLA + u, t, CH_MLA, w_mla, MLA_COLS)

                def mla_up(t):
                    u = T - 1 - t
                    pe.wait_ge(S["z_free"], L * PER["z_free"] + Z_MLA + u + 1)
                    bank = take_ring()
                    for b in range(3):
                        tr = pe.transpose(bank[:, tokens(b)], cn[:, b, :], ident[:])
                    tr.then_inc(S["tr_done"], 1)
                    pe.wait_ge(S["w_hi"], L * PER["w_hi"] + CH_UKV + 1)
                    pe.wait_ge(S["w_lo"], L * PER["w_lo"] + CH_UKV + 1)
                    if u >= 2:
                        pe.wait_ge(S["u_free"], L * PER["u_free"] + u - 1)
                        pe.wait_ge(S["m_nope"], L * PER["m_nope"] + u - 1)
                    if u == 0:
                        pe.wait_ge(S["s_exp"], L * PER["s_exp"] + 2 * DIFF_HEADS * T)
                    ring_empty()
                    pairs = [pair for k in range(2) for pair in
                             split((ct_hi[:, k, :], ct_lo[:, k, :]), (w_uq[0][:, k, :], w_uq[1][:, k, :]))]
                    products(banks[:, 2 * (u % 2), 0:MLA_HEADS * MLA_QK], pairs)
                    products(banks[:, 2 * (u % 2) + 1, :], split((ct_hi[:, 2, :], ct_lo[:, 2, :]), (w_ukv[0][:], w_ukv[1][:])))\
                        .then_inc(S["u_done"], 1)

                mqk_ready = {}

                def mla_transpose(h, t):
                    if h == 0:
                        pe.wait_ge(S["m_qrope"], L * PER["m_qrope"] + T - t)
                        pe.wait_ge(S["m_krope"], L * PER["m_krope"] + T - t)
                    bank = take_ring()
                    pe.transpose(bank[0:MLA_QK, 0:P], m_q[:, t, h, :], ident[:])
                    pe.transpose(bank[0:MLA_QK, P:2 * P], m_k[:, t, h, :], ident[:]).then_inc(S["tr_done"], 1)
                    mqk_ready[h] = ring[0]

                def mla_scores(h, t):
                    a = h * T + (T - 1 - t)
                    j = 2 * DIFF_HEADS * T + a
                    if t == T - 1:
                        pe.wait_ge(S["tr_free"], L * PER["tr_free"] + mqk_ready[h])
                    pe.wait_ge(S["s_exp"], L * PER["s_exp"] + j - 1)
                    for c in range(0, (t + 1) * P, 512):
                        n = min(512, (t + 1) * P - c)
                        products(SCORE[j % 2][:, c:c + n],
                                 split((mq_hi[:, tokens(t)], mq_lo[:, tokens(t)]), (mk_hi[:, c:c + n], mk_lo[:, c:c + n])),
                                 last=c + n != (t + 1) * P)
                    pe.matmul(SCORE[j % 2][:, tokens(t)], ident_r[:], mask_r[:], start=False, stop=True)\
                        .then_inc(S["s_done"], 1)

                def mla_output(h, t):
                    a = h * T + (T - 1 - t)
                    j = 2 * DIFF_HEADS * T + a
                    pe.wait_ge(S["s_exp"], L * PER["s_exp"] + j + 1)
                    transpose_probs(mexpo[a % 2], t)
                    pe.wait_ge(S["o_free"], L * PER["o_free"] + DIFF_HEADS * T + a)
                    pe.wait_ge(S["u_free"], L * PER["u_free"] + T)
                    ring_empty()
                    pairs = [pair for kb in range(t + 1) for pair in
                             split((pt_hi[:, kb, :], pt_lo[:, kb, :]), (mv_hi[:, kb, h, :], mv_lo[:, kb, h, :]))]
                    products(banks[:, O_BANK, 0:MLA_V], pairs).then_inc(S["pv_done"], 1)

                for s in range(T + 1):
                    if s < T:
                        mla_latents(T - 1 - s)
                    if s >= 1:
                        mla_up(T - s)
                pe.wait_ge(S["u_free"], L * PER["u_free"] + T)
                pe.wait_ge(S["m_nope"], L * PER["m_nope"] + T)
                for h in range(-1, MLA_HEADS):
                    for s in STEPS:
                        t = T - 1 - s
                        if h >= 0 and s < T:
                            mla_scores(h, t)
                        if h + 1 < MLA_HEADS and 1 <= s <= T:
                            mla_transpose(h + 1, t + 1)
                        if h >= 0 and 1 <= s <= T:
                            mla_output(h, t + 1)

                def ret_transpose(p, t):
                    n = p * T + t
                    pe.wait_ge(S["r_xz"], L * PER["r_xz"] + n + 1)
                    bank = take_ring()
                    pe.transpose(bank[:, tokens(0)], r_rot[n % 2][:, 0:2, :].rearrange("p a d -> p (a d)"), ident[:])
                    pe.transpose(bank[:, tokens(1)], r_rot[n % 2][:, 2:4, :].rearrange("p a d -> p (a d)"), ident[:])
                    pe.transpose(bank[:, tokens(2)], r_xzt[n % 2][:, 0:2, :].rearrange("p a d -> p (a d)"), ident[:])\
                        .then_inc(S["tr_done"], 1)
                    ret_ready[n] = ring[0]

                ret_ready = {}

                def ret_inner(p, t):
                    n = p * T + t
                    pe.wait_ge(S["tr_free"], L * PER["tr_free"] + ret_ready[n])
                    if n >= 1:
                        pe.wait_ge(S["r_at"], L * PER["r_at"] + n)
                    hi, lo = rt_hi[n % 2], rt_lo[n % 2]
                    for j in range(2):
                        at_ = slice(64 * j, 64 * j + 64)
                        mm = products(banks[:, RET_INNER[j], 0:P], split((hi[at_, 1, :], lo[at_, 1, :]), (hi[at_, 0, :], lo[at_, 0, :])))
                    mm.then_inc(S["ri_done"], 1)
                    if t < T - 1:
                        n_s = p * (T - 1) + t
                        pe.wait_ge(S["r_kzhi"], L * PER["r_kzhi"] + n + 1)
                        pe.wait_ge(S["r_kzlo"], L * PER["r_kzlo"] + n + 1)
                        pe.wait_ge(S["z_free"], L * PER["z_free"] + Z_RET + n + 1)
                        if n_s >= 1:
                            pe.wait_ge(S["r_st"], L * PER["r_st"] + n_s)
                        products(banks[:, RET_STATE, 0:P], split((rk_hi[n % 2][:], rk_lo[n % 2][:]), (rv_hi[n % 3][:], rv_lo[n % 3][:])))\
                            .then_inc(S["rs_done"], 1)

                def ret_output(p, t):
                    n = p * T + t
                    pe.wait_ge(S["r_athi"], L * PER["r_athi"] + n + 1)
                    pe.wait_ge(S["r_atlo"], L * PER["r_atlo"] + n + 1)
                    pe.wait_ge(S["z_free"], L * PER["z_free"] + Z_RET + n + 1)
                    if n >= 1:
                        pe.wait_ge(S["r_on"], L * PER["r_on"] + n)
                    if t >= 1:
                        pe.wait_ge(S["r_sthi"], L * PER["r_sthi"] + p * (T - 1) + t)
                        pe.wait_ge(S["r_stlo"], L * PER["r_stlo"] + p * (T - 1) + t)
                    for j in range(2):
                        at_ = slice(64 * j, 64 * j + 64)
                        pairs = split((r_at_hi[:, tokens(j)], r_at_lo[:, tokens(j)]), (rv_hi[n % 3][:, at_], rv_lo[n % 3][:, at_]))
                        if t >= 1:
                            pairs += split((rt_hi[n % 2][at_, 2, :], rt_lo[n % 2][at_, 2, :]),
                                           (r_st_hi[(t - 1) % 2][at_, at_], r_st_lo[(t - 1) % 2][at_, at_]))
                        mm = products(banks[:, RET_OUT[j], 0:64], pairs)
                    mm.then_inc(S["ro_done"], 1)

                for n in range(2 * T + 2):
                    if 1 <= n <= 2 * T:
                        ret_transpose((n - 1) // T, (n - 1) % T)
                    if n >= 2:
                        ret_inner((n - 2) // T, (n - 2) % T)
                    if n < 2 * T:
                        if n == 0:
                            pe.wait_ge(S["s_exp"], L * PER["s_exp"] + PER["s_exp"])
                        project(Z_RET + n, n % T, CH_RET + n // T, w_ret[n // T], 512)
                    if n >= 2:
                        ret_output((n - 2) // T, (n - 2) % T)

                pe.wait_ge(S["z_free"], L * PER["z_free"] + Z_UNITS)
                ring_empty()
                transpose_rows("mix_in", (16, 32))
                ring_empty()
                pe.wait_ge(S["r_on"], L * PER["r_on"] + 2 * T)
                for c in range(2):
                    pe.wait_ge(S["w_hi"], L * PER["w_hi"] + CH_OUT + c + 1)
                    pe.wait_ge(S["w_lo"], L * PER["w_lo"] + CH_OUT + c + 1)
                    for t in range(T):
                        q = c * T + t
                        if q >= 4:
                            pe.wait_ge(S["out_add"], L * PER["out_add"] + q - 3)
                        pairs = [pair for k in range(KD) for pair in
                                 split((ht_hi[:, k, tokens(t)], ht_lo[:, k, tokens(t)]), (w_o[c][0][:, k, :], w_o[c][1][:, k, :]))]
                        products(banks[:, q % 4, :], pairs).then_inc(S["out_done"], 1)

                transpose_rows("n_xn", (T + 4, 2 * T))
                assert ring[0] == RING
                pe.wait_ge(S["tr_free"], L * PER["tr_free"] + RING)
                pe.wait_ge(S["out_add"], L * PER["out_add"] + 2 * T)
                pe.sem_inc(S["passed"], 1)

                with pe.Fori(0, GROUPS) as g:
                    for m in range(GM):
                        pe.wait_ge(S["f_hi"], L * PER["f_hi"] + g * 3 + (m + 1))
                        pe.wait_ge(S["f_lo"], L * PER["f_lo"] + g * 3 + (m + 1))
                        for half in range(2):
                            v = 2 * m + half
                            if v >= 2:
                                pe.wait_ge(S["f_mul"], L * PER["f_mul"] + g * 4 + (v - 1))
                            for gate_or_up in range(2):
                                pairs = []
                                for k in range(KD):
                                    w = (w_gu[m][0][:, gate_or_up, k, :], w_gu[m][1][:, gate_or_up, k, :])
                                    h_ = (ht_hi[:, k, tokens(4 * half, 4)], ht_lo[:, k, tokens(4 * half, 4)])
                                    pairs += split(w, h_)
                                mm = products(banks[:, 2 * (v % 2) + gate_or_up, :], pairs)
                            mm.then_inc(S["gu_done"], 1)
                    pe.wait_ge(S["f_hi"], L * PER["f_hi"] + g * 3 + 3)
                    pe.wait_ge(S["f_lo"], L * PER["f_lo"] + g * 3 + 3)
                    for t in range(T):
                        if t % 4 == 0:
                            pe.wait_ge(S["f_act"], L * PER["f_act"] + g * 4 + (3 + t // 4))
                        for c in range(2):
                            q = 2 * t + c
                            pe.wait_ge(S["d_add"], L * PER["d_add"] + g * 2 * T + (q - 3 + ADD_CREDIT))
                            pairs = [pair for m in range(GM) for pair in
                                     split((act_hi[:, m, tokens(t)], act_lo[:, m, tokens(t)]),
                                           (w_dn[0][:, m, c * 512:(c + 1) * 512], w_dn[1][:, m, c * 512:(c + 1) * 512]))]
                            products(banks[:, 4 + q % 4, :], pairs).then_inc(S["fd_done"], 1)

        @block.scalar
        def _(act):
            act.wait_ge(S["tab_dve"], 11)
            act.activation(sin_d[:, :, 1, :], red[:, :, 0:32], ACT.Sin)
            act.activation(sin_d[:, :, 0, :], red[:, :, 0:32], ACT.Sin, scale=-1.0)
            act.activation(sin_m[:, :, 1, :], red[:, :, 32:48], ACT.Sin)
            act.activation(sin_m[:, :, 0, :], red[:, :, 32:48], ACT.Sin, scale=-1.0)
            act.activation(cos_d[:], cosarg[:, :, 0:32], ACT.Sin)
            act.activation(cos_m[:], cosarg[:, :, 32:48], ACT.Sin).then_inc(S["tab_act"], 1)

            with act.Fori(0, DEPTH) as L:
                ring = [0]

                def round_ring():
                    ring[0] += 1
                    act.wait_ge(S["tr_done"], L * PER["tr_done"] + ring[0])
                    return ring[0] - 1

                def round_weights(chunk, n_in, parts):
                    act.wait_ge(S[f"w_in{chunk % 2}"], L * PER[f"w_in{chunk % 2}"] + n_in)
                    for hi, raw in parts[:-1]:
                        act.activation(hi, raw, ACT.Copy)
                    act.activation(*parts[-1], ACT.Copy).then_inc(S["w_hi"], 1)

                def square_rows(norm, t, ready, n):
                    act.wait_ge(S[ready], L * PER[ready] + n)
                    if norm * T + t:
                        act.wait_ge(S["n_sq"], L * PER["n_sq"] + norm * T + t)
                    act.activation(row_square[:], X[:, t, :], ACT.Square, accum_out=row_ss[:, t:t + 1])\
                        .then_inc(S["n_sq"], 1)

                def high_rows(gain):
                    for half in range(2):
                        for k in range(KD):
                            r = round_ring()
                            act.activation(ht_hi[:, k, tokens(4 * half, 4)], banks[:, NORM_BANKS[r % 4], :], ACT.Copy,
                                           scale=gain[:, k:k + 1] if gain is not None else 1.0).then_inc(S["tr_hi"], 1)

                act.wait_ge(S["x_in"], 16)
                for t in range(T):
                    square_rows(0, t, "d_add", 2 * (t + 1))
                act.wait_ge(S["params_in"], L * PER["params_in"] + PER["params_in"])
                high_rows(attn_gain)
                act.wait_ge(S["lam"], L * PER["lam"] + 2)
                act.activation(lam_exp[:], lam_sum[:], ACT.Exp).then_inc(S["lam"], 1)

                def weights(chunk):
                    if chunk < CH_MLA:
                        w, n = w_diff[chunk % 2], 3 * (chunk // 2 + 1)
                    elif chunk == CH_MLA:
                        w, n = w_mla, 7
                    elif chunk == CH_UKV:
                        act.wait_ge(S["w_gain"], L * PER["w_gain"] + 1)
                        return round_weights(chunk, 16 * 10, [(w_uq[0][:], w_uq[2][:]), (w_ukv[0][:], w_ukv[2][:])])
                    elif chunk < CH_OUT:
                        w, n = w_ret[chunk % 2], (11, 14)[chunk % 2]
                    else:
                        w, n = w_o[chunk % 2], (12, 15)[chunk % 2]
                    round_weights(chunk, 16 * n, [(w[0][:, 0:4, :], w[2][:, 0:4, :]), (w[0][:, 4:8, :], w[2][:, 4:8, :])])

                def diff_v(h, t):
                    u = h * T + (T - 1 - t)
                    act.wait_ge(S["z_done"], L * PER["z_done"] + u + 1)
                    if u >= T:
                        act.wait_ge(S["pv_done"], L * PER["pv_done"] + u - T + 1)
                    act.activation(dv_hi[:, t, :], banks[:, Z_BANK, 2 * P:3 * P], ACT.Copy).then_inc(S["v_hi"], 1)

                def diff_qk(h, t):
                    r = round_ring()
                    bank = banks[:, TR_BANKS[r % 2], :].rearrange("p (a m n) -> p a m n", a=2, m=2)
                    act.activation(dq_hi[:, :, tokens(t)], bank[:, 0], ACT.Copy, scale=DIFF_SCALE)
                    act.activation(dk[:, :, tokens(t)], bank[:, 1], ACT.Copy).then_inc(S["tr_hi"], 1)

                def exponentials(j, dst, a, m, t):
                    act.wait_ge(S["s_max"], L * PER["s_max"] + j + 1)
                    act.activation(dst, SCORE[j % 2][:, 0:(t + 1) * P], ACT.Exp, bias=neg_max[:, a % 2, m:m + 1],
                                   accum_out=exp_sum[:, a % 2, m:m + 1]).then_inc(S["s_exp"], 1)

                def high_probs(a, t):
                    for b in range(0, t + 1, 4):
                        r = round_ring()
                        n = min(4, t + 1 - b)
                        if a >= 1:
                            act.wait_ge(S["pv_done"], L * PER["pv_done"] + a)
                        act.activation(pt_hi[:, b:b + n, :], banks[:, TR_BANKS[r % 2], 0:n * P].rearrange("p (b n) -> p b n", n=P),
                                       ACT.Copy).then_inc(S["tr_hi"], 1)

                def diff_square(h, t):
                    a = h * T + (T - 1 - t)
                    act.wait_ge(S["pv_done"], L * PER["pv_done"] + a + 1)
                    if a >= 1:
                        act.wait_ge(S["o_sq"], L * PER["o_sq"] + a)
                    act.activation(square_out[:], banks[:, O_BANK, 0:P], ACT.Square, scale=inv_sum[:, a % 2, 0:1],
                                   accum_out=o_ss[:, a % 2:a % 2 + 1]).then_inc(S["o_sq"], 1)

                weights(0)
                act.wait_ge(S["x_saved"], L * PER["x_saved"] + 16)
                for h in range(-1, DIFF_HEADS):
                    for s in STEPS:
                        t = T - 1 - s
                        if s == 4:
                            weights(h + 2)
                        if h >= 0 and s < T:
                            a = h * T + s
                            for m in range(2):
                                if a >= 2:
                                    act.wait_ge(S["pv_done"], L * PER["pv_done"] + a - 1)
                                exponentials(2 * a + m, expo[a % 2][:, m, 0:(t + 1) * P], a, m, t)
                        if h + 1 < DIFF_HEADS and 2 <= s:
                            diff_qk(h + 1, t + 2)
                        if h >= 0 and 1 <= s <= T:
                            high_probs(h * T + s - 1, t + 1)
                            diff_square(h, t + 1)
                        if h + 1 < DIFF_HEADS and 1 <= s <= T:
                            diff_v(h + 1, t + 1)

                def mla_squares(t):
                    u = T - 1 - t
                    act.wait_ge(S["z_done"], L * PER["z_done"] + Z_MLA + u + 1)
                    if u == 0:
                        act.wait_ge(S["pv_done"], L * PER["pv_done"] + DIFF_HEADS * T)
                    else:
                        act.wait_ge(S["m_sq"], L * PER["m_sq"] + u)
                    act.activation(m_square[:], banks[:, Z_BANK, 0:Q_RANK], ACT.Square, accum_out=m_ss[:, u % 2, 0:1]).then_inc(S["m_sq2"], 1)
                    act.wait_ge(S["m_sq2"], L * PER["m_sq2"] + u + 1)
                    act.activation(m_square[:, 0:KV_RANK], banks[:, Z_BANK, Q_RANK:Q_RANK + KV_RANK], ACT.Square,
                                   accum_out=m_ss[:, u % 2, 1:2]).then_inc(S["m_sq"], 1)

                def mla_up(t):
                    u = T - 1 - t
                    r = round_ring()
                    if u >= 1:
                        act.wait_ge(S["u_done"], L * PER["u_done"] + u)
                    act.activation(ct_hi[:].rearrange("p b n -> p (b n)"), banks[:, TR_BANKS[r % 2], 0:3 * P], ACT.Copy).then_inc(S["tr_hi"], 1)
                    act.wait_ge(S["u_done"], L * PER["u_done"] + u + 1)
                    if u == 0:
                        act.wait_ge(S["mix_out0"], L * PER["mix_out0"] + 16 * DIFF_HEADS * T // 2)
                        act.wait_ge(S["mix_out1"], L * PER["mix_out1"] + 16 * DIFF_HEADS * T // 2)
                    qb = banks[:, 2 * (u % 2), 0:MLA_HEADS * MLA_QK].rearrange("p (h d) -> p h d", h=MLA_HEADS)
                    kvb = banks[:, 2 * (u % 2) + 1, :].rearrange("p (h d) -> p h d", h=MLA_HEADS)
                    act.activation(mv_hi[:, t], kvb[:, :, NOPE:], ACT.Copy).then_inc(S["m_vhi"], 1)
                    act.activation(m_q[:, t, :, 0:NOPE], qb[:, :, 0:NOPE], ACT.Copy)
                    act.activation(m_k[:, t, :, 0:NOPE], kvb[:, :, 0:NOPE], ACT.Copy).then_inc(S["m_nope"], 1)

                def mla_qk(h, t):
                    r = round_ring()
                    bank = banks[0:MLA_QK, TR_BANKS[r % 2], :]
                    act.activation(mq_hi[:, tokens(t)], bank[:, 0:P], ACT.Copy, scale=MLA_SCALE)
                    act.activation(mk_hi[:, tokens(t)], bank[:, P:2 * P], ACT.Copy).then_inc(S["tr_hi"], 1)

                for s in range(T + 1):
                    if s < T:
                        mla_squares(T - 1 - s)
                    if s >= 1:
                        mla_up(T - s)
                for h in range(-1, MLA_HEADS):
                    for s in STEPS:
                        t = T - 1 - s
                        a = DIFF_HEADS * T + h * T + s
                        if h >= 0 and s < T:
                            act.wait_ge(S["pv_done"], L * PER["pv_done"] + a - 1)
                            exponentials(2 * DIFF_HEADS * T + h * T + s, mexpo[a % 2][:, 0:(t + 1) * P], a, 0, t)
                        if h + 1 < MLA_HEADS and 1 <= s <= T:
                            mla_qk(h + 1, t + 1)
                        if h >= 0 and 1 <= s <= T:
                            high_probs(a - 1, t + 1)
                        if h in (0, 1) and s == 4:
                            weights(CH_RET + h)

                def ret_gate_and_v(n):
                    act.wait_ge(S["z_done"], L * PER["z_done"] + Z_RET + n + 1)
                    bank = banks[:, Z_BANK, :]
                    if n == 0:
                        act.wait_ge(S["pv_done"], L * PER["pv_done"] + ATT_UNITS)
                    if n >= 3:
                        act.wait_ge(S["r_mx"], L * PER["r_mx"] + n - 2)
                        act.wait_ge(S["ro_done"], L * PER["ro_done"] + n - 2)
                    act.activation(r_gate[n % 3][:], bank[:, 3 * P:4 * P], ACT.Silu)
                    act.activation(rv_hi[n % 3][:], bank[:, 2 * P:3 * P], ACT.Copy).then_inc(S["v_hi"], 1)
                    act.wait_ge(S["r_xz"], L * PER["r_xz"] + n + 1)
                    if n >= 2:
                        act.wait_ge(S["ri_done"], L * PER["ri_done"] + n - 1)
                        if rs_count(n - 1):
                            act.wait_ge(S["rs_done"], L * PER["rs_done"] + rs_count(n - 1))
                    act.activation(rk_hi[n % 2][:], r_xzt[n % 2][:, 2:4, :].rearrange("p a d -> p (a d)"), ACT.Copy)\
                        .then_inc(S["r_kzhi"], 1)

                def rs_count(n):
                    return n - n // T

                def ret_high(n):
                    r = round_ring()
                    if n >= 2:
                        act.wait_ge(S["ro_done"], L * PER["ro_done"] + n - 1)
                    act.activation(rt_hi[n % 2][:].rearrange("p b n -> p (b n)"), banks[:, TR_BANKS[r % 2], 0:3 * P], ACT.Copy)\
                        .then_inc(S["tr_hi"], 1)

                def ret_inner(n):
                    act.wait_ge(S["r_at"], L * PER["r_at"] + n + 1)
                    if n >= 1:
                        act.wait_ge(S["ro_done"], L * PER["ro_done"] + n)
                    act.activation(r_at_hi[:], r_at[:], ACT.Copy).then_inc(S["r_athi"], 1)
                    if n % T < T - 1:
                        i = rs_count(n)
                        act.wait_ge(S["r_st"], L * PER["r_st"] + i + 1)
                        act.activation(r_st_hi[n % T % 2][:], r_st[:], ACT.Copy).then_inc(S["r_sthi"], 1)

                for n in range(2 * T + 2):
                    if 1 <= n <= 2 * T:
                        ret_high(n - 1)
                    if n >= 2:
                        ret_inner(n - 2)
                    if n < 2 * T:
                        ret_gate_and_v(n)
                    if n == T + 1:
                        weights(CH_OUT)
                weights(CH_OUT + 1)

                high_rows(None)
                for t in range(T):
                    square_rows(1, t, "out_add", T + t + 1)
                high_rows(ffn_gain)

                with act.Fori(0, GROUPS) as g:
                    for m in range(GM):
                        act.wait_ge(S[f"fg_in{m}"], L * PER[f"fg_in{m}"] + g * 32 + 32)
                        act.activation(w_gu[m][0][:], w_gu[m][2][:], ACT.Copy).then_inc(S["f_hi"], 1)
                    act.wait_ge(S["fd_in"], L * PER["fd_in"] + g * 16 + 16)
                    act.activation(w_dn[0][:], w_dn[2][:], ACT.Copy).then_inc(S["f_hi"], 1)
                    for v in range(4):
                        m, half = v // 2, v % 2
                        act.wait_ge(S["gu_done"], L * PER["gu_done"] + g * 4 + (v + 1 + GU_CREDIT))
                        act.activation(f_gate[v % 2][:], banks[:, 2 * (v % 2), :], ACT.Silu).then_inc(S["f_silu"], 1)
                        act.wait_ge(S["f_mul"], L * PER["f_mul"] + g * 4 + (v + 1))
                        act.activation(act_hi[:, m, tokens(4 * half, 4)], f_prod[v % 2][:], ACT.Copy).then_inc(S["f_ahi"], 1)

            for t in range(T):
                act.wait_ge(S["d_add"], DEPTH * PER["d_add"] + 2 * (t + 1))
                if t:
                    act.wait_ge(S["f_sq"], t)
                act.activation(row_square[:], X[:, t, :], ACT.Square, accum_out=row_ss[:, t:t + 1]).then_inc(S["f_sq"], 1)

        @block.vector
        def _(dve):
            dve.sem_inc(S["d_add"], ADD_CREDIT)
            tab = [0]

            def table_step(ins):
                tab[0] += 1
                ins.then_inc(S["tab_dve"], 1)
                dve.wait_ge(S["tab_dve"], tab[0])

            dve.wait_ge(S["const_in"], 64)
            dve.tensor_copy(ident_r[:], consts[:, C_IDENT:C_IDENT + P]).then_inc(S["ident_ok"], 1)
            dve.tensor_copy(mask_r[:], consts[:, C_MASK:C_MASK + P]).then_inc(S["ident_ok"], 1)
            dve.wait_ge(S["pos_in"], 16)
            table_step(dve.tensor_copy(pos_f[:], pos_int[:]))
            table_step(dve.tensor_tensor(ang[:], pos_f[:].unsqueeze(2).to_broadcast([P, T, 48]),
                                         consts[:, C_INVF:C_INVF + 48].unsqueeze(1).to_broadcast([P, T, 48]), ALU.mult))
            magic = 1.5 * 2.0 ** 23
            table_step(dve.tensor_scalar(turns[:], ang[:], 1.0 / (2 * math.pi), magic, ALU.mult, ALU.add))
            table_step(dve.tensor_scalar(turns[:], turns[:], magic, None, ALU.subtract))
            left = 2 * math.pi
            for bits in (5, 13, 30, 50):
                part = round(left * 2.0 ** bits) / 2.0 ** bits
                left -= part
                table_step(dve.scalar_tensor_tensor(red[:], turns[:], -part, ang[:] if bits == 5 else red[:], ALU.mult, ALU.add))
            top = float(np.nextafter(np.float32(math.pi), np.float32(0)))
            table_step(dve.tensor_scalar(red[:], red[:], top, -top, ALU.min, ALU.max))
            table_step(dve.scalar_tensor_tensor(cosarg[:], red[:], -1.0, red[:], ALU.mult, ALU.max))
            table_step(dve.tensor_scalar(cosarg[:], cosarg[:], -1.0, math.pi / 2, ALU.mult, ALU.add))
            dve.wait_ge(S["tab_act"], 1)

            with dve.Fori(0, DEPTH) as L:
                ring = [0]

                def low_ring():
                    ring[0] += 1
                    dve.wait_ge(S["tr_hi"], L * PER["tr_hi"] + ring[0])
                    return ring[0] - 1

                def scale_rows(norm, half):
                    for j in range(4):
                        t = 4 * half + j
                        dve.wait_ge(S["n_rstd"], L * PER["n_rstd"] + 2 * norm + half + 1)
                        dve.tensor_scalar(rows[:, j, :], X[:, t, :], row_rstd[:, t:t + 1], None, ALU.mult)\
                            .then_inc(S["n_xn"], 1)

                def low_rows(half, gain):
                    for k in range(KD):
                        r = low_ring()
                        at_ = tokens(4 * half, 4)
                        bank = banks[:, NORM_BANKS[r % 4], :]
                        hi = ht_hi[:, k, at_].bitcast(F32)
                        if gain is None:
                            lo = dve.tensor_tensor(ht_lo[:, k, at_], bank, hi, ALU.subtract)
                        else:
                            lo = dve.scalar_tensor_tensor(ht_lo[:, k, at_], bank, gain[:, k:k + 1], hi, ALU.mult, ALU.subtract)
                        lo.then_inc(S["tr_free"], 1)

                def norm_rows(norm, gain):
                    for half in range(2):
                        if half:
                            dve.wait_ge(S["tr_done"], L * PER["tr_done"] + ring[0])
                        scale_rows(norm, half)
                        low_rows(half, gain)

                dve.wait_ge(S["params_in"], L * PER["params_in"] + PER["params_in"])
                norm_rows(0, attn_gain)
                for m in range(2):
                    if m:
                        dve.wait_ge(S["lam"], L * PER["lam"] + 1)
                    dve.tensor_tensor_reduce(lam_prod[:], lam_vec[:, 2 * m, :], lam_vec[:, 2 * m + 1, :], 1.0, 0.0, ALU.mult,
                                             ALU.add, lam_sum[:, m:m + 1]).then_inc(S["lam"], 1)
                dve.wait_ge(S["lam"], L * PER["lam"] + 3)
                dve.tensor_tensor(neg_lam[:], lam_exp[:, 1:2], lam_exp[:, 0:1], ALU.subtract).then_inc(S["lam"], 1)
                dve.wait_ge(S["lam"], L * PER["lam"] + 4)
                dve.tensor_tensor(neg_lam[:], neg_lam[:], lam_const[:, 0:1], ALU.subtract)
                dve.tensor_scalar(subln[:], subln[:], lam_const[:, 1:2], None, ALU.mult).then_inc(S["lam"], 1)
                dve.wait_ge(S["lam"], L * PER["lam"] + 5)

                def rotate(z, a, b, t):
                    dve.tensor_tensor(a[:].rearrange("p v s d -> p (v s) d"), z.rearrange("p (v d) -> p v d", d=32),
                                      cos_d[:, t, :].unsqueeze(1).to_broadcast([P, 8, 32]), ALU.mult)
                    return dve.tensor_tensor(b[:], z.rearrange("p (v s d) -> p v s d", v=4, s=2)[:, :, ::-1, :],
                                             sin_d[:, t].unsqueeze(1).to_broadcast([P, 4, 2, 32]), ALU.mult)

                def diff_rotate(h, t):
                    u = h * T + (T - 1 - t)
                    dve.wait_ge(S["v_hi"], L * PER["v_hi"] + u + 1)
                    if u >= 2:
                        dve.wait_ge(S["rope_sum"], L * PER["rope_sum"] + u - 1)
                    rotate(banks[:, Z_BANK, 0:2 * P], rope_a[u % 2], rope_b[u % 2], t).then_inc(S["rope_ab"], 1)
                    dve.tensor_tensor(dv_lo[:, t, :], banks[:, Z_BANK, 2 * P:3 * P], dv_hi[:, t, :].bitcast(F32), ALU.subtract)\
                        .then_inc(S["z_free"], 1)

                def diff_low(h, t):
                    r = low_ring()
                    bank = banks[:, TR_BANKS[r % 2], :].rearrange("p (a m n) -> p a m n", a=2, m=2)
                    dve.scalar_tensor_tensor(dq_lo[:, :, tokens(t)], bank[:, 0], DIFF_SCALE, dq_hi[:, :, tokens(t)].bitcast(F32),
                                             ALU.mult, ALU.subtract)
                    low = dk[64:P, :, tokens(t)]
                    dve.tensor_tensor(low, bank[64:P, 1], low.bitcast(F32), ALU.subtract).then_inc(S["tr_free"], 1)

                def negated_max(j, a, m, t):
                    dve.wait_ge(S["s_done"], L * PER["s_done"] + j + 1)
                    dve.tensor_reduce(neg_max[:, a % 2, m:m + 1], SCORE[j % 2][:, 0:(t + 1) * P], AX_X, ALU.max, negate=True)\
                        .then_inc(S["s_max"], 1)

                def combine(h, t):
                    a = h * T + (T - 1 - t)
                    b = a % 2
                    dve.wait_ge(S["s_exp"], L * PER["s_exp"] + 2 * a + 2)
                    dve.reciprocal(inv_sum[:, b, :], exp_sum[:, b, :]).then_inc(S["inv_sum"], 1)
                    dve.wait_ge(S["inv_sum"], L * PER["inv_sum"] + a + 1)
                    dve.scalar_tensor_tensor(ratio[:, b:b + 1], exp_sum[:, b, 0:1], neg_lam[:], inv_sum[:, b, 1:2],
                                             ALU.mult, ALU.mult).then_inc(S["lam_ratio"], 1)
                    dve.wait_ge(S["lam_ratio"], L * PER["lam_ratio"] + a + 1)
                    e = expo[b]
                    n = (t + 1) * P
                    dve.scalar_tensor_tensor(e[:, 0, 0:n], e[:, 1, 0:n], ratio[:, b:b + 1], e[:, 0, 0:n], ALU.mult, ALU.add)\
                        .then_inc(S["p_ready"], 1)

                def low_probs(t):
                    for b in range(0, t + 1, 4):
                        r = low_ring()
                        n = min(4, t + 1 - b)
                        dve.tensor_tensor(pt_lo[:, b:b + n, :], banks[:, TR_BANKS[r % 2], 0:n * P].rearrange("p (b n) -> p b n", n=P),
                                          pt_hi[:, b:b + n, :].bitcast(F32), ALU.subtract).then_inc(S["tr_free"], 1)

                def diff_finish(h, t):
                    a = h * T + (T - 1 - t)
                    dve.wait_ge(S["o_rr"], L * PER["o_rr"] + a + 1)
                    if a >= 2:
                        dve.wait_ge(S[f"mix_out{a % 2}"], L * PER[f"mix_out{a % 2}"] + 16 * (a // 2))
                    dve.scalar_tensor_tensor(d_mx[a % 2][:], banks[:, O_BANK, 0:P], o_rr[:, a % 2:a % 2 + 1], subln[:],
                                             ALU.mult, ALU.mult).then_inc(S["o_free"], 1)

                for h in range(-1, DIFF_HEADS):
                    for s in STEPS:
                        t = T - 1 - s
                        if h >= 0 and s < T:
                            for m in range(2):
                                negated_max(2 * (h * T + s) + m, h * T + s, m, t)
                            combine(h, t)
                        if h + 1 < DIFF_HEADS and 2 <= s:
                            diff_low(h + 1, t + 2)
                        if h >= 0 and 1 <= s <= T:
                            low_probs(t + 1)
                            diff_finish(h, t + 1)
                        if h + 1 < DIFF_HEADS and 1 <= s <= T:
                            diff_rotate(h + 1, t + 1)

                def mla_latents(t):
                    u = T - 1 - t
                    z = banks[:, Z_BANK, 0:MLA_COLS]
                    dve.wait_ge(S["m_sq"], L * PER["m_sq"] + u + 1)
                    zr = z[:, Q_RANK + KV_RANK:MLA_COLS].rearrange("p (s d) -> p s d", s=2)
                    if u >= 1:
                        dve.wait_ge(S["m_krope"], L * PER["m_krope"] + u)
                    dve.tensor_tensor(mk_a[:], zr, cos_m[:, t, :].unsqueeze(1).to_broadcast([P, 2, 16]), ALU.mult)
                    dve.tensor_tensor(mk_b[:], zr[:, ::-1, :], sin_m[:, t], ALU.mult).then_inc(S["m_kab"], 1)
                    dve.wait_ge(S["m_rstd"], L * PER["m_rstd"] + u + 1)
                    if u >= 1:
                        dve.wait_ge(S["tr_done"], L * PER["tr_done"] + ring[0] + 1)
                    dve.tensor_scalar(cn[:, 0:2, :].rearrange("p b n -> p (b n)"), z[:, 0:Q_RANK], m_rs[:, u % 2, 0:1], None, ALU.mult)
                    dve.tensor_scalar(cn[:, 2, :], z[:, Q_RANK:Q_RANK + KV_RANK], m_rs[:, u % 2, 1:2], None, ALU.mult)\
                        .then_inc(S["z_free"], 1)

                def mla_up(t):
                    u = T - 1 - t
                    r = low_ring()
                    dve.tensor_tensor(ct_lo[:].rearrange("p b n -> p (b n)"), banks[:, TR_BANKS[r % 2], 0:3 * P],
                                      ct_hi[:].rearrange("p b n -> p (b n)").bitcast(F32), ALU.subtract).then_inc(S["tr_free"], 1)
                    dve.wait_ge(S["m_nope"], L * PER["m_nope"] + u + 1)
                    qb = banks[:, 2 * (u % 2), 0:MLA_HEADS * MLA_QK].rearrange("p (h d) -> p h d", h=MLA_HEADS)
                    kvb = banks[:, 2 * (u % 2) + 1, :].rearrange("p (h d) -> p h d", h=MLA_HEADS)
                    qr = qb[:, :, NOPE:].rearrange("p h (s d) -> p h s d", s=2)
                    if u >= 1:
                        dve.wait_ge(S["m_qrope"], L * PER["m_qrope"] + u)
                    dve.tensor_tensor(mq_a[:], qr, cos_m[:, t, :].unsqueeze(1).unsqueeze(1).to_broadcast([P, MLA_HEADS, 2, 16]), ALU.mult)
                    dve.tensor_tensor(mq_b[:], qr[:, :, ::-1, :], sin_m[:, t].unsqueeze(1).to_broadcast([P, MLA_HEADS, 2, 16]),
                                      ALU.mult).then_inc(S["m_qab"], 1)
                    dve.tensor_tensor(mv_lo[:, t], kvb[:, :, NOPE:], mv_hi[:, t].bitcast(F32), ALU.subtract).then_inc(S["u_free"], 1)

                def mla_low(h, t):
                    r = low_ring()
                    bank = banks[0:MLA_QK, TR_BANKS[r % 2], :]
                    dve.scalar_tensor_tensor(mq_lo[:, tokens(t)], bank[:, 0:P], MLA_SCALE, mq_hi[:, tokens(t)].bitcast(F32),
                                             ALU.mult, ALU.subtract)
                    dve.tensor_tensor(mk_lo[:, tokens(t)], bank[:, P:2 * P], mk_hi[:, tokens(t)].bitcast(F32), ALU.subtract)\
                        .then_inc(S["tr_free"], 1)

                def mla_finish(a):
                    b = a % 2
                    dve.wait_ge(S["pv_done"], L * PER["pv_done"] + a + 1)
                    dve.wait_ge(S["inv_sum"], L * PER["inv_sum"] + a + 1)
                    n = a
                    dve.wait_ge(S[f"mix_out{a % 2}"], L * PER[f"mix_out{a % 2}"] + 16 * (n // 2))
                    dve.tensor_scalar(m_mx[b][:], banks[:, O_BANK, 0:MLA_V], inv_sum[:, b, 0:1], None, ALU.mult)\
                        .then_inc(S["o_free"], 1)

                for s in range(T + 1):
                    if s < T:
                        mla_latents(T - 1 - s)
                    if s >= 1:
                        mla_up(T - s)
                for h in range(-1, MLA_HEADS):
                    for s in STEPS:
                        t = T - 1 - s
                        a = DIFF_HEADS * T + h * T + s
                        if h >= 0 and s < T:
                            j = 2 * DIFF_HEADS * T + h * T + s
                            negated_max(j, a, 0, t)
                        if h + 1 < MLA_HEADS and 1 <= s <= T:
                            mla_low(h + 1, t + 1)
                        if h >= 0 and 1 <= s <= T:
                            low_probs(t + 1)
                            dve.wait_ge(S["s_exp"], L * PER["s_exp"] + 2 * DIFF_HEADS * T + h * T + s)
                            dve.reciprocal(inv_sum[:, (a - 1) % 2, 0:1], exp_sum[:, (a - 1) % 2, 0:1]).then_inc(S["inv_sum"], 1)
                            mla_finish(a - 1)

                def ret_rotate(n):
                    t = n % T
                    dve.wait_ge(S["v_hi"], L * PER["v_hi"] + ROPE_RET + n + 1)
                    bank = banks[:, Z_BANK, :]
                    if n >= 2:
                        dve.wait_ge(S["rope_sum"], L * PER["rope_sum"] + ROPE_RET + n - 1)
                    rotate(bank[:, 0:2 * P], r_ab[n % 2][0], r_ab[n % 2][1], t).then_inc(S["rope_ab"], 1)
                    dve.tensor_tensor(rv_lo[n % 3][:], bank[:, 2 * P:3 * P], rv_hi[n % 3][:].bitcast(F32), ALU.subtract)\
                        .then_inc(S["z_free"], 1)

                def rs_count(n):
                    return n - n // T

                def ret_low(n):
                    r = low_ring()
                    dve.tensor_tensor(rt_lo[n % 2][:].rearrange("p b n -> p (b n)"), banks[:, TR_BANKS[r % 2], 0:3 * P],
                                      rt_hi[n % 2][:].rearrange("p b n -> p (b n)").bitcast(F32), ALU.subtract).then_inc(S["tr_free"], 1)

                def ret_inner(n):
                    p = n // T
                    if n == 0:
                        dve.wait_ge(S["ret_in"], L * PER["ret_in"] + PER["ret_in"])
                    dve.wait_ge(S["ri_done"], L * PER["ri_done"] + n + 1)
                    if n >= 1:
                        dve.wait_ge(S["r_atlo"], L * PER["r_atlo"] + n)
                    dve.tensor_tensor(r_at[:].rearrange("p (j n) -> p j n", j=2), banks[:, 0:2, 0:P], decay[:, p, :].rearrange("p (j n) -> p j n", j=2), ALU.mult).then_inc(S["r_at"], 1)
                    if n % T < T - 1:
                        i = rs_count(n)
                        dve.wait_ge(S["rs_done"], L * PER["rs_done"] + i + 1)
                        if i:
                            dve.wait_ge(S["r_sthi"], L * PER["r_sthi"] + i)
                            dve.wait_ge(S["r_stlo"], L * PER["r_stlo"] + i)
                        if n % T == 0:
                            st = dve.tensor_copy(r_st[:], banks[:, RET_STATE, 0:P])
                        else:
                            st = dve.scalar_tensor_tensor(r_st[:], r_st[:], cd[:, p:p + 1], banks[:, RET_STATE, 0:P], ALU.mult, ALU.add)
                        st.then_inc(S["r_st"], 1)

                def ret_norm(n):
                    b = n % 2
                    dve.wait_ge(S["ro_done"], L * PER["ro_done"] + n + 1)
                    for j in range(2):
                        st = dve.bn_stats(bn[:, b, j, :], banks[:, RET_OUT[j], 0:64])
                    st.then_inc(S["r_bn"], 1)
                    dve.wait_ge(S["r_bn"], L * PER["r_bn"] + n + 1)
                    dve.sem_inc(S["passed"], 1)
                    for j in range(2):
                        st = dve.bn_aggr(mv[:, b, j, :], bn[:, b, j, :])
                    st.then_inc(S["r_mv"], 1)
                    dve.wait_ge(S["r_rstd"], L * PER["r_rstd"] + n + 1)
                    if n >= 2:
                        dve.wait_ge(S["r_gw"], L * PER["r_gw"] + n - 1)
                    for j in range(2):
                        st = dve.tensor_scalar(r_norm[b][:, 64 * j:64 * j + 64], banks[:, RET_OUT[j], 0:64],
                                               mv[:, b, j, 0:1], r_rs[:, b, j:j + 1], ALU.subtract, ALU.mult)
                    st.then_inc(S["r_on"], 1)

                for n in range(2 * T + 2):
                    if 1 <= n <= 2 * T:
                        ret_low(n - 1)
                    if n >= 2:
                        ret_inner(n - 2)
                    if n < 2 * T:
                        ret_rotate(n)
                    if n >= 2:
                        ret_norm(n - 2)

                for half in range(2):
                    low_rows(half, None)
                dve.wait_ge(S["x_back"], L * PER["x_back"] + 16)
                for q in range(2 * T):
                    c, t = q // T, q % T
                    cols = slice(c * 512, (c + 1) * 512)
                    dve.wait_ge(S["out_done"], L * PER["out_done"] + q + 1)
                    dve.tensor_tensor(X[:, t, cols], X[:, t, cols], banks[:, q % 4, :], ALU.add).then_inc(S["out_add"], 1)
                dve.wait_ge(S["out_add"], L * PER["out_add"] + 2 * T)
                norm_rows(1, ffn_gain)

                with dve.Fori(0, GROUPS) as g:
                    for v in range(4):
                        m, half = v // 2, v % 2
                        dve.wait_ge(S["f_silu"], L * PER["f_silu"] + g * 4 + (v + 1))
                        if v >= 2:
                            dve.wait_ge(S["f_act"], L * PER["f_act"] + g * 4 + (v - 1))
                        dve.tensor_tensor(f_prod[v % 2][:], banks[:, 2 * (v % 2) + 1, :], f_gate[v % 2][:], ALU.mult)\
                            .then_inc(S["f_mul"], 1)
                        dve.wait_ge(S["f_ahi"], L * PER["f_ahi"] + g * 4 + (v + 1))
                        dve.tensor_tensor(act_lo[:, m, tokens(4 * half, 4)], f_prod[v % 2][:],
                                          act_hi[:, m, tokens(4 * half, 4)].bitcast(F32), ALU.subtract).then_inc(S["f_act"], 1)
                    for q in range(2 * T):
                        t, c = q // 2, q % 2
                        cols = slice(c * 512, (c + 1) * 512)
                        dve.wait_ge(S["fd_done"], L * PER["fd_done"] + g * 2 * T + (q + 1 + D_CREDIT))
                        dve.tensor_tensor(X[:, t, cols], X[:, t, cols], banks[:, 4 + q % 4, :], ALU.add).then_inc(S["d_add"], 1)
                    dve.wait_ge(S["d_add"], L * PER["d_add"] + g * 2 * T + (2 * T + ADD_CREDIT))

            dve.wait_ge(S["final_in"], 16)
            for t in range(T):
                dve.wait_ge(S["f_rstd"], t // 4 + 1)
                if t >= 4:
                    dve.wait_ge(S[f"y_out{t % 4}"], 16)
                dve.scalar_tensor_tensor(rows[:, t % 4, :], X[:, t, :], row_rstd[:, t:t + 1], final_gain[:], ALU.mult, ALU.mult)\
                    .then_inc(S["y_ready"], 1)

        @block.gpsimd
        def _(pool):
            pool.memset(minus_half, -0.5).then_inc(S["half_ok"], 1)
            pool.wait_ge(S["half_ok"], 1)

            def inverse_root(out_, in_):
                return pool.tensor_tensor(out_, in_, minus_half[:, 0:in_.shape[1]], ALU.pow)

            with pool.Fori(0, DEPTH) as L:

                def inverse_roots(norm):
                    for half in range(2):
                        i = 2 * norm + half
                        cols = slice(4 * half, 4 * half + 4)
                        if norm:
                            pool.wait_ge(S["n_xn"], L * PER["n_xn"] + T)
                        pool.wait_ge(S["n_sq"], L * PER["n_sq"] + norm * T + 4 * half + 4)
                        pool.sem_inc(S["passed"], 1)
                        pool.tensor_scalar(row_ms[:, cols], row_ss[:, cols], 1.0 / D, NORM_EPS, ALU.mult, ALU.add).then_inc(S["n_ms"], 1)
                        pool.wait_ge(S["n_ms"], L * PER["n_ms"] + i + 1)
                        inverse_root(row_rstd[:, cols], row_ms[:, cols]).then_inc(S["n_rstd"], 1)

                def low_weights(chunk, parts):
                    pool.wait_ge(S["w_hi"], L * PER["w_hi"] + chunk + 1)
                    for lo, raw, hi in parts:
                        st = pool.tensor_tensor(lo, raw, hi.bitcast(F32), ALU.subtract)
                    st.then_inc(S["w_lo"], 1)

                def weights(chunk):
                    if chunk == CH_UKV:
                        return low_weights(chunk, [(w_uq[1][:], w_uq[2][:], w_uq[0][:]), (w_ukv[1][:], w_ukv[2][:], w_ukv[0][:])])
                    w = (w_diff[chunk % 2] if chunk < CH_MLA else w_mla if chunk == CH_MLA else
                         w_ret[chunk % 2] if chunk < CH_OUT else w_o[chunk % 2])
                    low_weights(chunk, [(w[1][:], w[2][:], w[0][:])])

                inverse_roots(0)
                weights(0)

                def rotation(n, a, b, dst, copies):
                    pool.wait_ge(S["rope_ab"], L * PER["rope_ab"] + n + 1)
                    a, b = (x[:].rearrange("p v s d -> p v (s d)").unsqueeze(2).to_broadcast([P, 4, copies, 64]) for x in (a, b))
                    return pool.tensor_tensor(dst[:] if copies > 1 else dst[:].unsqueeze(2), a, b, ALU.add)

                def diff_rotation(h, t):
                    u = h * T + (T - 1 - t)
                    if u >= 2:
                        pool.wait_ge(S["tr_done"], L * PER["tr_done"] + diff_ring[u - 2])
                    rotation(u, rope_a[u % 2], rope_b[u % 2], qk_rot[u % 2], 2).then_inc(S["rope_sum"], 1)

                def diff_root(h, t):
                    a = h * T + (T - 1 - t)
                    b = slice(a % 2, a % 2 + 1)
                    pool.wait_ge(S["o_sq"], L * PER["o_sq"] + a + 1)
                    pool.sem_inc(S["passed"], 1)
                    pool.tensor_scalar(o_ms[:, b], o_ss[:, b], 1.0 / (2 * DIFF_DIM), SUBLN_EPS, ALU.mult, ALU.add).then_inc(S["o_ms"], 1)
                    pool.wait_ge(S["o_ms"], L * PER["o_ms"] + 2 * a + 1)
                    inverse_root(o_rs[:, b], o_ms[:, b]).then_inc(S["o_ms"], 1)
                    pool.wait_ge(S["o_ms"], L * PER["o_ms"] + 2 * a + 2)
                    pool.tensor_tensor(o_rr[:, b], o_rs[:, b], inv_sum[:, a % 2, 0:1], ALU.mult).then_inc(S["o_rr"], 1)

                diff_ring, ring = {}, 2 * KD
                for h in range(-1, DIFF_HEADS):
                    for s in STEPS:
                        t = T - 1 - s
                        if s == 1 and h + 2 == CH_UKV:
                            pool.wait_ge(S["w_in1"], L * PER["w_in1"] + 16 * 10)
                            pool.sem_inc(S["passed"], 1)
                            for k in range(2):
                                pool.tensor_scalar(w_uq[2][:, k, :], w_uq[2][:, k, :], q_gain[:, k:k + 1], None, ALU.mult)
                            pool.tensor_scalar(w_ukv[2][:], w_ukv[2][:], kv_gain[:], None, ALU.mult).then_inc(S["w_gain"], 1)
                        if h + 1 < DIFF_HEADS and 2 <= s:
                            ring += 1
                            diff_ring[(h + 1) * T + s - 2] = ring
                        if h >= 0 and 1 <= s <= T:
                            ring += groups_of_four(t + 1)
                            diff_root(h, t + 1)
                        if h + 1 < DIFF_HEADS and 1 <= s <= T:
                            diff_rotation(h + 1, t + 1)
                        if s == 4:
                            weights(h + 2)

                def mla_roots(t):
                    u = T - 1 - t
                    b = u % 2
                    pool.wait_ge(S["m_sq"], L * PER["m_sq"] + u + 1)
                    pool.sem_inc(S["passed"], 1)
                    pool.tensor_scalar(m_msq[:, b, 0:1], m_ss[:, b, 0:1], 1.0 / Q_RANK, NORM_EPS, ALU.mult, ALU.add)
                    pool.tensor_scalar(m_msq[:, b, 1:2], m_ss[:, b, 1:2], 1.0 / KV_RANK, NORM_EPS, ALU.mult, ALU.add).then_inc(S["m_ms"], 2)
                    pool.wait_ge(S["m_ms"], L * PER["m_ms"] + 2 * u + 2)
                    inverse_root(m_rs[:, b, :], m_msq[:, b, :]).then_inc(S["m_rstd"], 1)
                    pool.wait_ge(S["m_kab"], L * PER["m_kab"] + u + 1)
                    if u == 0:
                        pool.wait_ge(S["pv_done"], L * PER["pv_done"] + DIFF_HEADS * T)
                        pool.wait_ge(S["mix_out0"], L * PER["mix_out0"] + 16 * DIFF_HEADS * T // 2)
                        pool.wait_ge(S["mix_out1"], L * PER["mix_out1"] + 16 * DIFF_HEADS * T // 2)
                    pool.tensor_tensor(m_k[:, t, :, NOPE:], mk_a[:].rearrange("p s d -> p (s d)").unsqueeze(1).to_broadcast([P, MLA_HEADS, ROPE]),
                                       mk_b[:].rearrange("p s d -> p (s d)").unsqueeze(1).to_broadcast([P, MLA_HEADS, ROPE]), ALU.add)\
                        .then_inc(S["m_krope"], 1)

                def mla_q_rotation(t):
                    u = T - 1 - t
                    pool.wait_ge(S["m_qab"], L * PER["m_qab"] + u + 1)
                    pool.tensor_tensor(m_q[:, t, :, NOPE:], mq_a[:].rearrange("p h s d -> p h (s d)"), mq_b[:].rearrange("p h s d -> p h (s d)"),
                                       ALU.add).then_inc(S["m_qrope"], 1)

                for s in range(T + 1):
                    if s < T:
                        mla_roots(T - 1 - s)
                    if s >= 1:
                        mla_q_rotation(T - s)
                weights(CH_RET)
                weights(CH_RET + 1)

                def rs_count(n):
                    return n - n // T

                def ret_scaled(n):
                    b = n % 2
                    if n == 0:
                        pool.wait_ge(S["pv_done"], L * PER["pv_done"] + ATT_UNITS)
                    if n >= 2:
                        pool.wait_ge(S["tr_done"], L * PER["tr_done"] + ret_ring + n - 1)
                        pool.wait_ge(S["r_kzhi"], L * PER["r_kzhi"] + n - 1)
                    rotation(ROPE_RET + n, r_ab[b][0], r_ab[b][1], r_rot[b], 1).then_inc(S["rope_sum"], 1)
                    pool.wait_ge(S["rope_sum"], L * PER["rope_sum"] + ROPE_RET + n + 1)
                    pool.tensor_tensor(r_xzt[b][:], r_rot[b][:], xz[:, n // T, :].unsqueeze(2).to_broadcast([P, 4, 64]), ALU.mult)\
                        .then_inc(S["r_xz"], 1)
                    pool.wait_ge(S["r_kzhi"], L * PER["r_kzhi"] + n + 1)
                    pool.tensor_tensor(rk_lo[b][:], r_xzt[b][:, 2:4, :].rearrange("p a d -> p (a d)"), rk_hi[b][:].bitcast(F32), ALU.subtract)\
                        .then_inc(S["r_kzlo"], 1)

                def ret_inner(n):
                    pool.wait_ge(S["r_athi"], L * PER["r_athi"] + n + 1)
                    pool.tensor_tensor(r_at_lo[:], r_at[:], r_at_hi[:].bitcast(F32), ALU.subtract).then_inc(S["r_atlo"], 1)
                    if n % T < T - 1:
                        i = rs_count(n)
                        pool.wait_ge(S["r_sthi"], L * PER["r_sthi"] + i + 1)
                        b = n % T % 2
                        pool.tensor_tensor(r_st_lo[b][:], r_st[:], r_st_hi[b][:].bitcast(F32), ALU.subtract).then_inc(S["r_stlo"], 1)

                def ret_norm(n):
                    b = n % 2
                    p = n // T
                    pool.wait_ge(S["r_mv"], L * PER["r_mv"] + n + 1)
                    pool.sem_inc(S["passed"], 1)
                    pool.tensor_scalar(r_ms[:, b, :], mv[:, b, :, 1], GN_EPS, None, ALU.add).then_inc(S["r_ms"], 1)
                    pool.wait_ge(S["r_ms"], L * PER["r_ms"] + n + 1)
                    inverse_root(r_rs[:, b, :], r_ms[:, b, :]).then_inc(S["r_rstd"], 1)
                    pool.wait_ge(S["r_on"], L * PER["r_on"] + n + 1)
                    cols = slice(p * P, (p + 1) * P)
                    if n == 0:
                        pool.wait_ge(S["ret_in"], L * PER["ret_in"] + PER["ret_in"])
                    if n >= 2:
                        pool.wait_ge(S[f"mix_out{b}"], L * PER[f"mix_out{b}"] + 16 * (ATT_UNITS // 2 + n // 2))
                    pool.tensor_tensor(r_mx[b][:], r_norm[b][:], gn_w[:, cols], ALU.mult).then_inc(S["r_gw"], 1)
                    pool.wait_ge(S["r_gw"], L * PER["r_gw"] + n + 1)
                    pool.tensor_tensor(r_mx[b][:], r_mx[b][:], gn_b[:, cols], ALU.add).then_inc(S["r_gb"], 1)
                    pool.wait_ge(S["r_gb"], L * PER["r_gb"] + n + 1)
                    pool.tensor_tensor(r_mx[b][:], r_mx[b][:], r_gate[n % 3][:], ALU.mult).then_inc(S["r_mx"], 1)

                ret_ring = RING - 2 * 2 * KD - 2 * T
                for n in range(2 * T + 2):
                    if n >= 2:
                        ret_inner(n - 2)
                    if n < 2 * T:
                        ret_scaled(n)
                    if n >= 2:
                        ret_norm(n - 2)
                    if n == T + 1:
                        weights(CH_OUT)
                weights(CH_OUT + 1)
                inverse_roots(1)

                with pool.Fori(0, GROUPS) as g:
                    for i, w in enumerate((w_gu[0], w_gu[1], w_dn)):
                        pool.wait_ge(S["f_hi"], L * PER["f_hi"] + g * 3 + (i + 1))
                        pool.tensor_tensor(w[1][:], w[2][:], w[0][:].bitcast(F32), ALU.subtract).then_inc(S["f_lo"], 1)

            for half in range(2):
                cols = slice(4 * half, 4 * half + 4)
                pool.wait_ge(S["f_sq"], 4 * half + 4)
                pool.tensor_scalar(row_ms[:, cols], row_ss[:, cols], 1.0 / D, NORM_EPS, ALU.mult, ALU.add).then_inc(S["f_ms"], 1)
                pool.wait_ge(S["f_ms"], half + 1)
                inverse_root(row_rstd[:, cols], row_ms[:, cols]).then_inc(S["f_rstd"], 1)


_INS = ["x", "positions", "attn_norm", "w_in", "diff_lam_q1", "diff_lam_k1", "diff_lam_q2", "diff_lam_k2", "diff_subln",
        "mla_q_norm", "mla_w_uq", "mla_kv_norm", "mla_w_ukv", "ret_gn_w", "ret_gn_b", "w_out", "ffn_norm", "w_gate",
        "w_up", "w_down", "final_norm"]
_OUTS = [((1, SEQ, D), "float32")]


def kernel(**inputs):
    import numpy as _np
    import concourse.bacc as _bacc
    from concourse import mybir as _mybir
    from concourse.bass_utils import run_bass_kernel_spmd as _run

    nc = _bacc.Bacc("TRN2", target_bir_lowering=False, num_devices=1)
    arrays, args = {}, []
    for name in _INS:
        a = _np.ascontiguousarray(inputs[name])
        arrays[f"in_{name}_dram"] = a
        args.append(nc.dram_tensor(f"in_{name}_dram", a.shape, _mybir.dt.from_np(a.dtype), kind="ExternalInput").ap())
    for i, (shape, dtype) in enumerate(_OUTS):
        dt = _mybir.dt.from_np(_np.dtype(dtype))
        args.append(nc.dram_tensor(f"out_{i}_dram", shape, dt, kind="ExternalOutput").ap())
    hybrid_block_kernel(nc, *args)
    r = _run(nc, [arrays], core_ids=[0])
    got = tuple(r.results[0][f"out_{i}_dram"] for i in range(len(_OUTS)))
    return got[0]
```

```python
import math
from contextlib import ExitStack

import numpy as np

import concourse.bass as bass
from concourse import mybir

F32 = mybir.dt.float32
F32R = mybir.dt.float32r
I32 = mybir.dt.int32
ALU = mybir.AluOpType
ACT = mybir.ActivationFunctionType
AX_X = mybir.AxisListType.X

P = 128
DEPTH = 2
SEQ = 1024
D = 1024
T = SEQ // P
KD = D // P
DESC = range(T - 1, -1, -1)

DIFF_HEADS, DIFF_DIM = 4, 64
MLA_HEADS, NOPE, ROPE, MLA_V = 4, 64, 32, 64
MLA_QK = NOPE + ROPE
Q_RANK, KV_RANK = 256, 128
RET_HEADS, RET_DIM = 4, 64
RET_PAIRS = RET_HEADS // 2
FFN = 2816
GROUP = 256
GROUPS = FFN // GROUP
GM = GROUP // P

DIFF_W = DIFF_HEADS * 2 * DIFF_DIM
RET_W = RET_HEADS * RET_DIM
COL_DQ, COL_DK, COL_DV = 0, DIFF_W, 2 * DIFF_W
COL_MLA = 3 * DIFF_W
MLA_COLS = Q_RANK + KV_RANK + ROPE
COL_RET = COL_MLA + MLA_COLS
MIX_MLA = DIFF_W
MIX_RET = DIFF_W + MLA_HEADS * MLA_V

NORM_EPS, SUBLN_EPS, GN_EPS = 1e-6, 1e-5, 1e-6
DIFF_SCALE = DIFF_DIM ** -0.5
MLA_SCALE = MLA_QK ** -0.5
NEG = -1e30

CH_DIFF, CH_MLA, CH_UKV, CH_RET, CH_OUT, CHUNKS = 0, 4, 5, 6, 8, 10
Z_MLA, Z_RET, Z_UNITS = 4 * T, 5 * T, 7 * T
ROPE_RET = 4 * T
ATT_UNITS = DIFF_HEADS * T + MLA_HEADS * T


def groups_of_four(t):
    return (t + 4) // 4


PT_RINGS = sum(groups_of_four(t) for t in range(T))
RING = 2 * KD + 4 * (T + PT_RINGS) + (T + 4 * (T + PT_RINGS)) + 2 * T + 2 * 2 * KD

PARTS = 4
V_SLOTS = T + 2


def diff_transposes(a):
    units = {0: (a + 6, a + 7), 1: ()}.get(a % T, (a + 6,))
    return [u for u in units if 0 <= u < DIFF_HEADS * T]


DIFF_STEPS = range(-T, DIFF_HEADS * T + 2)


def diff_rings():
    ring, after = 2 * KD, {}
    for a in DIFF_STEPS:
        early = diff_transposes(a)[:1] if a % T == 0 else []
        for u in early:
            ring += 1
            after[u] = ring
        if 0 <= a - 1 < DIFF_HEADS * T:
            ring += groups_of_four(T - 1 - (a - 1) % T)
        for u in diff_transposes(a)[len(early):]:
            ring += 1
            after[u] = ring
    return after


PER = dict(
    params_in=16 * 8, ret_in=16 * 3, x_saved=16, x_back=16, mix_in=16 * 2,
    w_in0=16 * (3 + 3 + 1 + 4 + 1), w_in1=16 * (3 + 3 + 4 + 4 + 1), w_gain=1, w_hi=PARTS * CHUNKS, w_lo=CHUNKS,
    lam=5, n_sq=2 * T, n_ms=4, n_rstd=4, n_xn=2 * T, tr_done=RING, tr_hi=RING, tr_free=RING,
    z_done=Z_UNITS, z_free=Z_UNITS, rope_ab=6 * T, rope_sum=6 * T, v_hi=6 * T,
    s_done=2 * DIFF_HEADS * T + MLA_HEADS * T, s_max=2 * DIFF_HEADS * T + MLA_HEADS * T,
    s_exp=2 * DIFF_HEADS * T + MLA_HEADS * T,
    inv_sum=ATT_UNITS, lam_ratio=DIFF_HEADS * T, p_ready=DIFF_HEADS * T, pv_done=ATT_UNITS, o_free=ATT_UNITS,
    o_sq=DIFF_HEADS * T, o_ms=3 * DIFF_HEADS * T, o_rr=DIFF_HEADS * T, o_out=ATT_UNITS,
    mix_out0=16 * (16 + 16 + 8), mix_out1=16 * (16 + 16 + 8),
    m_sq=T, m_sq2=T, m_ms=2 * T, m_rstd=T, m_kab=T, m_krope=T, u_done=T, m_nope=T, m_vhi=T, m_qab=T, u_free=T,
    m_qrope=T,
    r_xz=2 * T, r_kzhi=2 * T, r_kzlo=2 * T, ri_done=2 * T, r_at=2 * T, r_athi=2 * T, r_atlo=2 * T,
    ro_done=2 * T, rs_done=2 * (T - 1), r_st=2 * (T - 1), r_sthi=2 * (T - 1), r_stlo=2 * (T - 1),
    r_bn=2 * T, r_mv=2 * T, r_ms=2 * T, r_rstd=2 * T, r_on=2 * T, r_gw=2 * T, r_gb=2 * T, r_mx=2 * T,
    out_done=2 * T, out_add=2 * T,
    fg_in0=32 * GROUPS, fg_in1=32 * GROUPS, fd_in=16 * GROUPS, f_hi=3 * GROUPS, f_lo=3 * GROUPS,
    gu_done=4 * GROUPS, f_silu=4 * GROUPS, f_mul=4 * GROUPS, f_ahi=4 * GROUPS, f_act=4 * GROUPS,
    fd_done=2 * T * GROUPS, d_add=2 * T * GROUPS,
)
GU_CREDIT, D_CREDIT, ADD_CREDIT = 1, 1, 2 * T

C_IDENT, C_MASK, C_XZ, C_CD, C_INVF, C_LAM = 0, P, 2 * P, 2 * P + 8, 2 * P + 10, 2 * P + 58
C_COLS = C_LAM + 2 * DEPTH


def constants():
    c = np.zeros((P, C_COLS), np.float32)
    c[:, C_IDENT:C_IDENT + P] = np.eye(P)
    c[:, C_MASK:C_MASK + P] = np.triu(np.full((P, P), NEG), 1)
    log_gamma = np.log1p(-np.exp2(-5.0 - np.arange(RET_HEADS, dtype=np.float32))).astype(np.float32)
    pos = np.arange(P, dtype=np.float32)
    xi = np.exp((pos[:, None] + 1.0) * log_gamma[None, :])
    zeta = np.exp((P - 1.0 - pos)[:, None] * log_gamma[None, :]) * RET_DIM ** -0.5
    for p in range(RET_PAIRS):
        c[:, C_XZ + 4 * p:C_XZ + 4 * p + 2] = xi[:, 2 * p:2 * p + 2]
        c[:, C_XZ + 4 * p + 2:C_XZ + 4 * p + 4] = zeta[:, 2 * p:2 * p + 2]
        c[:64, C_CD + p] = np.exp(P * log_gamma[2 * p])
        c[64:, C_CD + p] = np.exp(P * log_gamma[2 * p + 1])
    for at, dim in ((0, DIFF_DIM), (32, ROPE)):
        freq = np.float32(1.0) / (np.float32(10000.0) ** (np.arange(0, dim, 2, dtype=np.float32) / np.float32(dim)))
        c[:, C_INVF + at:C_INVF + at + dim // 2] = freq
    for layer in range(DEPTH):
        init = 0.8 - 0.6 * math.exp(-0.3 * layer)
        c[:, C_LAM + 2 * layer:C_LAM + 2 * layer + 2] = (init, 1.0 - init)
    rel = pos[None, :] - pos[:, None]
    decay = np.where(rel[:, None, :] >= 0, np.exp(np.maximum(rel, 0.0)[:, None, :] * log_gamma[None, :, None]), 0.0)
    return c, (decay * RET_DIM ** -0.5).astype(np.float32).reshape(P, RET_HEADS * P)


def hybrid_block_kernel(nc, x, positions, attn_norm, w_in, diff_lam_q1, diff_lam_k1, diff_lam_q2, diff_lam_k2,
                        diff_subln, mla_q_norm, mla_w_uq, mla_kv_norm, mla_w_ukv, ret_gn_w, ret_gn_b, w_out,
                        ffn_norm, w_gate, w_up, w_down, final_norm, out):
    const_np, decay_np = constants()
    const_dram = nc.inline_tensor(const_np, name="const_table").ap()
    decay_dram = nc.inline_tensor(decay_np, name="decay_table").ap()
    mixed_dram = nc.dram_tensor("mixed_scratch", (SEQ, D), F32, kind="Internal").ap()
    x_dram = nc.dram_tensor("x_scratch", (SEQ, D), F32, kind="Internal").ap()

    base = 16512
    KB = 1024
    HT, WSLOT, XREG, EREG, MREG, CREG = 0, 64 * KB, 128 * KB, 160 * KB, 176 * KB, 200 * KB

    def sb(name, shape, dt, at):
        return nc.alloc_sbuf_tensor_at(name, shape, dt, offset=base + at)

    ht_hi = sb("ht_hi", [P, KD, SEQ], F32R, HT)
    ht_lo = sb("ht_lo", [P, KD, SEQ], F32R, HT + 32 * KB)

    def weight(name, shape, at):
        size = 4 * int(np.prod(shape[1:]))
        return (sb(name + "_hi", shape, F32R, at), sb(name + "_lo", shape, F32R, at + size),
                sb(name + "_raw", shape, F32, at + size))

    slots = [WSLOT, WSLOT + 32 * KB]
    w_diff = [weight(f"w_diff{i}", [P, KD, 3 * P], slots[i]) for i in range(2)]
    w_mla = weight("w_mla", [P, KD, MLA_COLS], slots[0])
    w_uq = weight("w_uq", [P, Q_RANK // P, MLA_HEADS * MLA_QK], slots[1])
    w_ukv = weight("w_ukv", [P, MLA_HEADS * (NOPE + MLA_V)], slots[1] + 8 * KB)
    w_ret = [weight(f"w_ret{i}", [P, KD, 4 * P], slots[i]) for i in range(2)]
    w_o = [weight(f"w_o{i}", [P, KD, 512], slots[i]) for i in range(2)]
    w_gu = [weight(f"w_gu{m}", [P, 2, KD, P], slots[0] + 16 * KB * m) for m in range(2)]
    w_dn = weight("w_dn", [P, GM, D], slots[1])

    X = sb("X", [P, T, D], F32, XREG)
    dq_hi = sb("dq_hi", [P, 2, SEQ], F32R, XREG)
    dq_lo = sb("dq_lo", [P, 2, SEQ], F32R, XREG + 8 * KB)
    dk = sb("dk", [P, 2, SEQ], F32R, XREG + 16 * KB)
    dv = [sb(f"dv{i}", [P, 2, P], F32R, XREG + (24 + i) * KB if i < T else MREG + (18 + i - T) * KB) for i in range(V_SLOTS)]
    mq_hi = sb("mq_hi", [MLA_QK, SEQ], F32R, XREG)
    mq_lo = sb("mq_lo", [MLA_QK, SEQ], F32R, XREG + 4 * KB)
    mk_hi = sb("mk_hi", [MLA_QK, SEQ], F32R, XREG + 8 * KB)
    mk_lo = sb("mk_lo", [MLA_QK, SEQ], F32R, XREG + 12 * KB)
    m_v = sb("m_v", [P, T, MLA_HEADS, 2, MLA_V], F32R, XREG + 16 * KB)

    pt_hi = sb("pt_hi", [P, T, P], F32R, EREG)
    pt_lo = sb("pt_lo", [P, T, P], F32R, EREG + 4 * KB)
    expo = [sb("expo0", [P, 2, SEQ], F32, EREG + 8 * KB), sb("expo1", [P, 2, SEQ], F32, MREG)]
    mexpo = [sb(f"mexpo{i}", [P, SEQ], F32, EREG + (8 + 4 * i) * KB) for i in range(2)]
    mpt_hi = [pt_hi, sb("mpt_hi1", [P, T, P], F32R, slots[1])]
    mpt_lo = [pt_lo, sb("mpt_lo1", [P, T, P], F32R, slots[1] + 4 * KB)]
    rope_a = [sb(f"rope_a{i}", [P, 4, 2, 32], F32, MREG + (8 + i) * KB) for i in range(2)]
    rope_b = [sb(f"rope_b{i}", [P, 4, 2, 32], F32, MREG + (10 + i) * KB) for i in range(2)]
    qk_rot = [sb(f"qk_rot{i}", [P, 4, 2, 64], F32, MREG + (12 + 2 * i) * KB) for i in range(2)]
    d_mx = [sb(f"d_mx{i}", [P, P], F32, MREG + 16 * KB + 512 * i) for i in range(2)]
    d_sum = [sb(f"d_sum{i}", [P, P], F32, MREG + 22 * KB + 512 * i) for i in range(2)]
    m_sum = [sb(f"m_sum{i}", [P, MLA_V], F32, slots[1] + 16 * KB + 256 * i) for i in range(2)]
    square_out = sb("square_out", [P, P], F32, MREG + 17 * KB)
    m_q = sb("m_q", [P, T, MLA_HEADS, MLA_QK], F32, MREG)
    m_k = sb("m_k", [P, T, MLA_HEADS, MLA_QK], F32, MREG + 12 * KB)
    cn = sb("cn", [P, 3, P], F32, EREG)
    ct_hi = sb("ct_hi", [P, 3, P], F32R, EREG + 1536)
    ct_lo = sb("ct_lo", [P, 3, P], F32R, EREG + 3072)
    mk_a = sb("mk_a", [P, 2, 16], F32, EREG + 4608)
    mk_b = sb("mk_b", [P, 2, 16], F32, EREG + 4736)
    mq_a = sb("mq_a", [P, MLA_HEADS, 2, 16], F32, EREG + 5120)
    mq_b = sb("mq_b", [P, MLA_HEADS, 2, 16], F32, EREG + 5632)
    m_square = sb("m_square", [P, Q_RANK], F32, EREG + 6144)
    decay = sb("decay", [P, RET_PAIRS, 2 * P], F32, EREG)
    gn_w = sb("gn_w", [P, RET_W], F32, EREG + 2 * KB)
    gn_b = sb("gn_b", [P, RET_W], F32, EREG + 3 * KB)
    rt_hi = [sb(f"rt_hi{i}", [P, 3, P], F32R, EREG + 4 * KB + 1536 * i) for i in range(2)]
    rt_lo = [sb(f"rt_lo{i}", [P, 3, P], F32R, EREG + 7 * KB + 1536 * i) for i in range(2)]
    rk_hi = [sb(f"rk_hi{i}", [P, P], F32R, EREG + 10 * KB + 512 * i) for i in range(2)]
    rk_lo = [sb(f"rk_lo{i}", [P, P], F32R, EREG + 11 * KB + 512 * i) for i in range(2)]
    rv_hi = [sb(f"rv_hi{i}", [P, P], F32R, EREG + 12 * KB + 512 * i) for i in range(3)]
    rv_lo = [sb(f"rv_lo{i}", [P, P], F32R, EREG + 12 * KB + 1536 + 512 * i) for i in range(3)]
    r_ab = [(sb(f"r_a{i}", [P, 4, 2, 32], F32, MREG + 2 * i * KB),
             sb(f"r_b{i}", [P, 4, 2, 32], F32, MREG + (2 * i + 1) * KB)) for i in range(2)]
    r_rot = [sb(f"r_rot{i}", [P, 4, 64], F32, MREG + (4 + i) * KB) for i in range(2)]
    r_xzt = [sb(f"r_xzt{i}", [P, 4, 64], F32, MREG + (6 + i) * KB) for i in range(2)]
    r_at = sb("r_at", [P, 2 * P], F32, MREG + 8 * KB)
    r_at_hi = sb("r_at_hi", [P, 2 * P], F32R, MREG + 9 * KB)
    r_at_lo = sb("r_at_lo", [P, 2 * P], F32R, MREG + 10 * KB)
    r_st = sb("r_st", [P, P], F32, MREG + 11 * KB)
    r_st_hi = [sb(f"r_st_hi{i}", [P, P], F32R, MREG + 12 * KB + 512 * i) for i in range(2)]
    r_st_lo = [sb(f"r_st_lo{i}", [P, P], F32R, MREG + 13 * KB + 512 * i) for i in range(2)]
    r_gate = [sb(f"r_gate{i}", [P, P], F32, MREG + 14 * KB + 512 * i) for i in range(3)]
    r_norm = [sb(f"r_norm{i}", [P, P], F32, MREG + 16 * KB + 512 * i) for i in range(2)]
    r_mx = [sb(f"r_mx{i}", [P, P], F32, MREG + 17 * KB + 512 * i) for i in range(2)]
    rows = sb("rows", [P, 4, D], F32, MREG)
    row_square = sb("row_square", [P, D], F32, MREG + 16 * KB)
    act_hi = sb("act_hi", [P, GM, SEQ], F32R, EREG)
    act_lo = sb("act_lo", [P, GM, SEQ], F32R, EREG + 8 * KB)
    f_gate = [sb(f"f_gate{i}", [P, 512], F32, MREG + 2 * i * KB) for i in range(2)]
    f_prod = [sb(f"f_prod{i}", [P, 512], F32, MREG + (4 + 2 * i) * KB) for i in range(2)]
    final_gain = sb("final_gain", [P, D], F32, EREG)
    ang, turns, red, cosarg = (sb(n, [P, T, 48], F32, EREG + 1536 * i) for i, n in
                               enumerate(("ang", "turns", "red", "cosarg")))
    pos_int = sb("pos_int", [P, T], I32, EREG + 6144)
    pos_f = sb("pos_f", [P, T], F32, EREG + 6400)
    consts = sb("consts", [P, C_COLS], F32, EREG + 7 * KB)
    at = [CREG]

    def keep(name, shape, dt=F32):
        size = -(-4 * int(np.prod(shape[1:])) // 32) * 32
        at[0] += size
        return sb(name, shape, dt, at[0] - size)

    ident = keep("ident", [P, P])
    ident_r = keep("ident_r", [P, P], F32R)
    mask_r = keep("mask_r", [P, P], F32R)
    subln = keep("subln", [P, P])
    cos_d = keep("cos_d", [P, T, 32])
    sin_d = keep("sin_d", [P, T, 2, 32])
    cos_m = keep("cos_m", [P, T, 16])
    sin_m = keep("sin_m", [P, T, 2, 16])
    stats = keep("stats", [P, 148])
    taken = [0]

    def small(*shape):
        size = int(np.prod(shape))
        taken[0] += size
        cols = stats[:, taken[0] - size:taken[0]]
        if len(shape) == 1:
            return cols
        names = "abc"[:len(shape)]
        return cols.rearrange(f"p ({' '.join(names)}) -> p {' '.join(names)}", **dict(zip(names, shape)))

    xz = small(2, 4)
    cd = small(2)
    lam_const = small(2)
    m_mx = [keep(f"m_mx{i}", [P, MLA_V]) for i in range(2)]
    attn_gain = small(KD)
    ffn_gain = small(KD)
    q_gain = small(2)
    kv_gain = small(1)
    lam_sum = small(2)
    lam_exp = small(2)
    neg_lam = small(1)
    row_ss = small(T)
    row_ms = small(T)
    row_rstd = small(T)
    neg_max = small(2, 2)
    exp_sum = small(2, 2)
    inv_sum = small(4, 2)
    ratio = small(2)
    o_ss = small(2)
    o_ms = small(2)
    o_rs = small(2)
    o_rr = small(2)
    m_ss = small(2, 2)
    m_msq = small(2, 2)
    m_rs = small(2, 2)
    bn = small(2, 2, 6)
    mv = small(2, 2, 2)
    r_rs = small(2, 2)
    r_ms = small(2, 2)
    minus_half = small(4)
    assert taken[0] <= 148, taken[0]
    assert base + at[0] <= nc.sbuf_usable_end, at[0] - CREG
    lam_vec = sb("lam_vec", [P, 4, DIFF_DIM], F32, MREG + 20 * KB)
    lam_prod = sb("lam_prod", [P, DIFF_DIM], F32, MREG + 21 * KB)

    ctx = ExitStack()
    with ctx:
        ctx.enter_context(nc.allow_non_contiguous_dma(reason="columns of gains and positions, a few KB"))
        banks = ctx.enter_context(nc.psum_tensor("banks", [P, 8, 512], F32))
        S = {name: ctx.enter_context(nc.semaphore(name)) for name in PER}
        S |= {name: ctx.enter_context(nc.semaphore(name)) for name in
              ("passed", "const_in", "x_in", "pos_in", "tab_dve", "tab_act", "ident_ok", "half_ok", "final_in", "f_sq", "f_ms", "f_rstd", "y_ready",
                 "y_out0", "y_out1", "y_out2", "y_out3")}

        SCORE = [banks[:, 0:2, :].rearrange("p b n -> p (b n)"), banks[:, 2:4, :].rearrange("p b n -> p (b n)")]
        Z_BANK, O_BANK = 4, 7

        def z_bank(u):
            return O_BANK if (u < T or Z_MLA <= u < Z_MLA + T) and u % 2 else Z_BANK

        TR_BANKS = (5, 6)
        NORM_BANKS = (4, 5, 6, 7)
        RET_INNER, RET_STATE, RET_OUT = (0, 1), 7, (2, 3)

        def tokens(t, n=1):
            return slice(t * P, (t + n) * P)

        def tile_of(unit):
            return T - 1 - unit % T

        DIFF_UNITS = DIFF_HEADS * T
        qk_ring = diff_rings()
        MLA_UNITS = MLA_HEADS * T
        MLA_STEPS = range(-T, MLA_UNITS + 3)

        RET_UNITS = RET_PAIRS * T

        def o_bank(a):
            return (Z_BANK, O_BANK)[a % 2]


        block = ctx.enter_context(nc.Block())

        @block.sync
        def _(sp):
            sp.dma_start(consts[:], const_dram).then_inc(S["const_in"], 16)
            sp.dma_start(ident[:], const_dram[:, C_IDENT:C_IDENT + P]).then_inc(S["const_in"], 16)
            sp.dma_start(xz[:], const_dram[:, C_XZ:C_XZ + 8]).then_inc(S["const_in"], 16)
            sp.dma_start(cd[:], const_dram[:, C_CD:C_CD + 2]).then_inc(S["const_in"], 16)
            sp.dma_start(pos_int[:], positions.rearrange("b (t p) -> p (b t)", p=P)).then_inc(S["pos_in"], 16)
            sp.dma_start(X[:], x[0].rearrange("(t p) d -> p t d", p=P)).then_inc(S["x_in"], 16)
            const2 = const_dram[:, C_LAM:C_LAM + 2 * DEPTH].rearrange("p (l c) -> l p c", l=DEPTH)
            mixed = mixed_dram.rearrange("(t p) d -> t p d", p=P)

            with sp.Fori(0, DEPTH) as L:

                def arrives(dst, src, name):
                    sp.dma_start(dst, src).then_inc(S[name], 16)

                arrives(attn_gain[:], attn_norm[L].rearrange("(k p) -> p k", p=P), "params_in")
                arrives(lam_const[:], const2[L], "params_in")
                for i, v in enumerate((diff_lam_q1, diff_lam_k1, diff_lam_q2, diff_lam_k2)):
                    arrives(lam_vec[:, i, :], v[L].partition_broadcast(P), "params_in")
                arrives(subln[:], diff_subln[L].partition_broadcast(P), "params_in")
                arrives(ffn_gain[:], ffn_norm[L].rearrange("(k p) -> p k", p=P), "params_in")

                def load_columns(chunk, w, starts, width):
                    src = w_in[L].rearrange("(k p) n -> p k n", p=P)
                    for i, start in enumerate(starts):
                        arrives(w[:, :, i * width:(i + 1) * width], src[:, :, start:start + width],
                                f"w_in{chunk % 2}")

                def load_diff(h):
                    load_columns(h, w_diff[h % 2][2], [c + h * P for c in (COL_DQ, COL_DK, COL_DV)], P)

                def load_ret(p):
                    load_columns(CH_RET + p, w_ret[p][2], [COL_RET + i * RET_W + p * P for i in range(4)], P)

                def load_out(c):
                    arrives(w_o[c][2][:], w_out[L].rearrange("(k p) n -> p k n", p=P)[:, :, c * 512:(c + 1) * 512],
                            f"w_in{c}")

                sp.wait_ge(S["gu_done"], L * PER["gu_done"] + GU_CREDIT)
                load_diff(0)
                sp.wait_ge(S["fd_done"], L * PER["fd_done"] + D_CREDIT)
                load_diff(1)
                sp.wait_ge(S["x_in"], 16)
                sp.wait_ge(S["d_add"], L * PER["d_add"] + ADD_CREDIT)
                arrives(x_dram.rearrange("(t p) d -> p t d", p=P), X[:], "x_saved")

                def next_chunk(h):
                    sp.wait_ge(S["z_done"], L * PER["z_done"] + T * (h + 1))
                    if h + 2 < DIFF_HEADS:
                        load_diff(h + 2)
                    elif h + 2 == CH_MLA:
                        arrives(w_mla[2][:], w_in[L].rearrange("(k p) n -> p k n", p=P)[:, :, COL_MLA:COL_MLA + MLA_COLS],
                                "w_in0")
                    elif h + 2 == CH_UKV:
                        arrives(q_gain[:], mla_q_norm[L].rearrange("(k p) -> p k", p=P), "w_in1")
                        arrives(w_uq[2][:], mla_w_uq[L].rearrange("(k p) n -> p k n", p=P), "w_in1")
                        arrives(kv_gain[:], mla_kv_norm[L].rearrange("(k p) -> p k", p=P), "w_in1")
                        arrives(w_ukv[2][:], mla_w_ukv[L], "w_in1")

                def store_mixed(ready, n, t, col, width, tile, unit):
                    sp.wait_ge(S[ready], L * PER[ready] + n)
                    arrives(mixed[t][:, col:col + width], tile, f"mix_out{unit % 2}")

                next_chunk(0)
                for h in range(DIFF_HEADS):
                    for t in DESC:
                        a = h * T + (T - 1 - t)
                        store_mixed("o_out", a + 1, t, h * P, P, d_mx[a % 2][:], a)
                        if t == 2 and h + 1 < DIFF_HEADS:
                            next_chunk(h + 1)
                sp.wait_ge(S["z_done"], L * PER["z_done"] + Z_MLA + T)
                load_ret(0)
                for h in range(MLA_HEADS):
                    for t in DESC:
                        a = DIFF_HEADS * T + h * T + (T - 1 - t)
                        store_mixed("o_out", a + 1, t, MIX_MLA + h * MLA_V, MLA_V, m_mx[a % 2][:], a)
                sp.wait_ge(S["pv_done"], L * PER["pv_done"] + ATT_UNITS)
                load_ret(1)
                arrives(decay[:], decay_dram.rearrange("p (a n) -> p a n", a=RET_PAIRS), "ret_in")
                arrives(gn_w[:], ret_gn_w[L].partition_broadcast(P), "ret_in")
                arrives(gn_b[:], ret_gn_b[L].partition_broadcast(P), "ret_in")
                sp.wait_ge(S["x_saved"], L * PER["x_saved"] + 16)
                arrives(X[:], x_dram.rearrange("(t p) d -> p t d", p=P), "x_back")
                for p in range(RET_PAIRS):
                    for t in range(T):
                        n = p * T + t
                        if t == T - 2:
                            sp.wait_ge(S["z_done"], L * PER["z_done"] + Z_RET + (p + 1) * T)
                            load_out(p)
                        store_mixed("r_mx", n + 1, t, MIX_RET + p * P, P, r_mx[n % 2][:], n)
                sp.wait_ge(S["mix_out0"], L * PER["mix_out0"] + PER["mix_out0"])
                sp.wait_ge(S["mix_out1"], L * PER["mix_out1"] + PER["mix_out1"])
                for half in range(2):
                    if half:
                        sp.wait_ge(S["tr_done"], L * PER["tr_done"] + RING - 3 * 2 * KD + 2 * KD + KD)
                    arrives(rows[:], mixed_dram.rearrange("(t p) d -> p t d", p=P)[:, 4 * half:4 * half + 4, :], "mix_in")

                wgv = w_gate[L].rearrange("(k p) n -> p k n", p=P)
                wuv = w_up[L].rearrange("(k p) n -> p k n", p=P)
                wdv = w_down[L].rearrange("(g k p) n -> g p k n", p=P, k=GM)

                def load_gu(g, m):
                    arrives(w_gu[m][2][:, 0], wgv[:, :, bass.ds(g * GROUP + m * P, P)], f"fg_in{m}")
                    arrives(w_gu[m][2][:, 1], wuv[:, :, bass.ds(g * GROUP + m * P, P)], f"fg_in{m}")

                sp.wait_ge(S["out_done"], L * PER["out_done"] + T)
                load_gu(0, 0)
                load_gu(0, 1)
                sp.wait_ge(S["out_done"], L * PER["out_done"] + 2 * T)
                arrives(w_dn[2][:], wdv[0], "fd_in")
                with sp.Fori(1, GROUPS) as g:
                    for m in range(GM):
                        sp.wait_ge(S["gu_done"], L * PER["gu_done"] + g * 4 + (2 * (m + 1) - 4 + GU_CREDIT))
                        load_gu(g, m)
                    sp.wait_ge(S["fd_done"], L * PER["fd_done"] + g * 2 * T + D_CREDIT)
                    arrives(w_dn[2][:], wdv[g], "fd_in")

            sp.wait_ge(S["fd_done"], DEPTH * PER["fd_done"] + D_CREDIT)
            sp.dma_start(final_gain[:], final_norm.partition_broadcast(P)).then_inc(S["final_in"], 16)
            for t in range(T):
                sp.wait_ge(S["y_ready"], t + 1)
                sp.dma_start(out[0].rearrange("(t p) d -> t p d", p=P)[t], rows[:, t % 4, :]).then_inc(S[f"y_out{t % 4}"], 16)
            for i in range(4):
                sp.wait_ge(S[f"y_out{i}"], 16 * T // 4)

        @block.tensor
        def _(pe):
            pe.wait_ge(S["const_in"], 64)
            pe.wait_ge(S["ident_ok"], 2)
            pe.sem_inc(S["gu_done"], GU_CREDIT)
            pe.sem_inc(S["fd_done"], D_CREDIT)

            def products(bank, pairs, first=True, last=True):
                mm = None
                for i, (lhsT, rhs) in enumerate(pairs):
                    mm = pe.matmul(bank, lhsT, rhs, start=first and i == 0, stop=last and i == len(pairs) - 1)
                return mm

            def split(a, b):
                return [(a[0], b[0]), (a[0], b[1]), (a[1], b[0])]

            with pe.Fori(0, DEPTH) as L:
                ring, freed = [0], [0]

                def ring_empty():
                    if ring[0] > freed[0]:
                        pe.wait_ge(S["tr_free"], L * PER["tr_free"] + ring[0])
                    freed[0] = ring[0]

                def take_ring(n_banks=2):
                    r = ring[0]
                    if r - n_banks + 1 > freed[0]:
                        pe.wait_ge(S["tr_free"], L * PER["tr_free"] + r - n_banks + 1)
                    ring[0] += 1
                    return banks[:, (TR_BANKS if n_banks == 2 else NORM_BANKS)[r % n_banks], :]

                def transpose_rows(ready, counts):
                    for half in range(2):
                        pe.wait_ge(S[ready], L * PER[ready] + counts[half])
                        for k in range(KD):
                            bank = take_ring(4)
                            for j in range(4):
                                tr = pe.transpose(bank[:, tokens(j)], rows[:, j, tokens(k)], ident[:])
                            tr.then_inc(S["tr_done"], 1)

                def project(u, t, chunk, w, n, parts=(0, 1)):
                    if 0 in parts:
                        pe.wait_ge(S["w_hi"], L * PER["w_hi"] + PARTS * (chunk + 1))
                        pe.wait_ge(S["w_lo"], L * PER["w_lo"] + chunk + 1)
                        if u == Z_MLA:
                            pe.wait_ge(S["o_free"], L * PER["o_free"] + DIFF_UNITS)
                        if T < u <= Z_MLA or u >= Z_MLA + T:
                            pe.wait_ge(S["z_free"], L * PER["z_free"] + u)
                        elif u >= 2:
                            pe.wait_ge(S["z_free"], L * PER["z_free"] + u - 1)
                    bank = banks[:, z_bank(u), 0:n]
                    for part in parts:
                        pairs = [pair for k in range(part * KD // 2, (part + 1) * KD // 2) for pair in
                                 split((ht_hi[:, k, tokens(t)], ht_lo[:, k, tokens(t)]), (w[0][:, k, :], w[1][:, k, :]))]
                        mm = products(bank, pairs, first=part == 0, last=part == 1)
                    if 1 in parts:
                        mm.then_inc(S["z_done"], 1)

                transpose_rows("n_xn", (4, 8))
                ring_empty()

                def diff_project(u, part):
                    if 0 <= u < DIFF_UNITS:
                        project(u, tile_of(u), u // T, w_diff[u // T % 2], 3 * P, (part,))

                def diff_transpose(u):
                    pe.wait_ge(S["rope_sum"], L * PER["rope_sum"] + u + 1)
                    bank = take_ring()
                    for v in range(4):
                        tr = pe.transpose(bank[:, tokens(v)], qk_rot[u % 2][:, v].rearrange("p c d -> p (c d)"), ident[:])
                    tr.then_inc(S["tr_done"], 1)
                    assert qk_ring[u] == ring[0]

                def diff_scores(a):
                    t = tile_of(a)
                    if a % T == 0:
                        pe.wait_ge(S["tr_free"], L * PER["tr_free"] + qk_ring[a + T - 1])
                    for m in range(2):
                        j = 2 * a + m
                        if j >= 2:
                            pe.wait_ge(S["s_exp"], L * PER["s_exp"] + j - 1)
                        for c in range(0, (t + 1) * P, 512):
                            n = min(512, (t + 1) * P - c)
                            diagonal = c + n == (t + 1) * P
                            keys = dk[:, m, c:c + n]
                            mm = products(SCORE[m][:, c:c + n], [(dq_hi[:, m, tokens(t)], keys), (dq_lo[:, m, tokens(t)], keys)],
                                          last=not diagonal)
                        mm = pe.matmul(SCORE[m][:, tokens(t)], ident_r[:], mask_r[:], start=False, stop=True)
                        mm.then_inc(S["s_done"], 1)

                def weighted(bank, hi, lo, v, width):
                    for kb, v_kb in enumerate(v):
                        pe.matmul(bank[:, 0:2 * width], hi[:, kb, :], v_kb.rearrange("p c d -> p (c d)"), start=kb == 0, stop=False)
                        mm = pe.matmul(bank[:, 0:width], lo[:, kb, :], v_kb[:, 0, :], start=False, stop=kb == len(v) - 1)
                    mm.then_inc(S["pv_done"], 1)

                def transpose_probs(tile, t):
                    for b in range(0, t + 1, 4):
                        bank = take_ring()
                        for kb in range(b, min(b + 4, t + 1)):
                            tr = pe.transpose(bank[:, tokens(kb - b)], tile[:, tokens(kb)], ident[:])
                        tr.then_inc(S["tr_done"], 1)

                def diff_probs(a):
                    if 0 <= a < DIFF_UNITS:
                        pe.wait_ge(S["p_ready"], L * PER["p_ready"] + a + 1)
                        transpose_probs(expo[a % 2][:, 0, :], tile_of(a))
                        p_ring[a] = ring[0]

                p_ring = {}

                def diff_output(a):
                    if not 0 <= a < DIFF_UNITS:
                        return
                    t = tile_of(a)
                    if a >= 1:
                        pe.wait_ge(S["o_free"], L * PER["o_free"] + a)
                    if p_ring[a] > freed[0]:
                        pe.wait_ge(S["tr_free"], L * PER["tr_free"] + p_ring[a])
                        freed[0] = p_ring[a]
                    weighted(banks[:, O_BANK, :], pt_hi, pt_lo,
                             [dv[(a // T * T + T - 1 - kb) % V_SLOTS][:] for kb in range(t + 1)], P)

                for a in DIFF_STEPS:
                    if a % T == 0:
                        for u in diff_transposes(a)[:1]:
                            diff_transpose(u)
                    elif 0 <= a < DIFF_UNITS:
                        diff_scores(a)
                    diff_project(a + T, 0)
                    diff_probs(a - 1)
                    for u in diff_transposes(a)[0 if a % T else 1:]:
                        diff_transpose(u)
                    diff_project(a + T, 1)
                    if a >= T:
                        pe.wait_ge(S["z_free"], L * PER["z_free"] + min(DIFF_UNITS, a + T - 1))
                    diff_output(a - 1)
                    if a % T == 0 and 0 <= a < DIFF_UNITS:
                        diff_scores(a)

                def mla_latents(u, part):
                    project(Z_MLA + u, tile_of(u), CH_MLA, w_mla, MLA_COLS, (part,))

                def mla_transpose_latents(u):
                    pe.wait_ge(S["z_free"], L * PER["z_free"] + Z_MLA + u + 1)
                    bank = take_ring()
                    for b in range(3):
                        tr = pe.transpose(bank[:, tokens(b)], cn[:, b, :], ident[:])
                    tr.then_inc(S["tr_done"], 1)

                def mla_up(u):
                    pe.wait_ge(S["w_hi"], L * PER["w_hi"] + CH_UKV + 1)
                    pe.wait_ge(S["w_lo"], L * PER["w_lo"] + CH_UKV + 1)
                    if u >= 2:
                        pe.wait_ge(S["u_free"], L * PER["u_free"] + u - 1)
                        pe.wait_ge(S["m_nope"], L * PER["m_nope"] + u - 1)
                    if u == 0:
                        pe.wait_ge(S["s_exp"], L * PER["s_exp"] + 2 * DIFF_HEADS * T)
                    ring_empty()
                    pairs = [pair for k in range(2) for pair in
                             split((ct_hi[:, k, :], ct_lo[:, k, :]), (w_uq[0][:, k, :], w_uq[1][:, k, :]))]
                    products(banks[:, 2 * (u % 2), 0:MLA_HEADS * MLA_QK], pairs)
                    products(banks[:, 2 * (u % 2) + 1, :], split((ct_hi[:, 2, :], ct_lo[:, 2, :]), (w_ukv[0][:], w_ukv[1][:])))\
                        .then_inc(S["u_done"], 1)

                def mla_transpose(u):
                    h, t = u // T, tile_of(u)
                    if h == 0:
                        pe.wait_ge(S["m_qrope"], L * PER["m_qrope"] + u + 1)
                        pe.wait_ge(S["m_krope"], L * PER["m_krope"] + u + 1)
                    bank = take_ring()
                    pe.transpose(bank[0:MLA_QK, 0:P], m_q[:, t, h, :], ident[:])
                    pe.transpose(bank[0:MLA_QK, P:2 * P], m_k[:, t, h, :], ident[:]).then_inc(S["tr_done"], 1)
                    mqk_ring[u] = ring[0]

                mqk_ring, mp_ring = {}, {}

                def mla_scores(a):
                    t = tile_of(a)
                    j = 2 * DIFF_UNITS + a
                    if a % T == 0:
                        pe.wait_ge(S["tr_free"], L * PER["tr_free"] + mqk_ring[a + T - 1])
                    pe.wait_ge(S["s_exp"], L * PER["s_exp"] + j - 1)
                    for c in range(0, (t + 1) * P, 512):
                        n = min(512, (t + 1) * P - c)
                        products(SCORE[j % 2][:, c:c + n],
                                 split((mq_hi[:, tokens(t)], mq_lo[:, tokens(t)]), (mk_hi[:, c:c + n], mk_lo[:, c:c + n])),
                                 last=c + n != (t + 1) * P)
                    pe.matmul(SCORE[j % 2][:, tokens(t)], ident_r[:], mask_r[:], start=False, stop=True)\
                        .then_inc(S["s_done"], 1)

                def mla_probs(a):
                    if 0 <= a < MLA_UNITS:
                        pe.wait_ge(S["s_exp"], L * PER["s_exp"] + 2 * DIFF_UNITS + a + 1)
                        transpose_probs(mexpo[a % 2], tile_of(a))
                        mp_ring[a] = ring[0]

                def mla_output(a):
                    if not 0 <= a < MLA_UNITS:
                        return
                    h, t = a // T, tile_of(a)
                    pe.wait_ge(S["o_free"], L * PER["o_free"] + DIFF_UNITS + a - 1)
                    if mp_ring[a] > freed[0]:
                        pe.wait_ge(S["tr_free"], L * PER["tr_free"] + mp_ring[a])
                        freed[0] = mp_ring[a]
                    weighted(banks[:, o_bank(a), :], mpt_hi[a % 2], mpt_lo[a % 2], [m_v[:, kb, h] for kb in range(t + 1)], MLA_V)

                for u in range(T + 1):
                    if u < T:
                        mla_latents(u, 0)
                    if u >= 1:
                        mla_transpose_latents(u - 1)
                    if u < T:
                        mla_latents(u, 1)
                    if u >= 1:
                        mla_up(u - 1)
                pe.wait_ge(S["u_free"], L * PER["u_free"] + T)
                pe.wait_ge(S["m_nope"], L * PER["m_nope"] + T)
                for a in MLA_STEPS:
                    if 0 <= a < MLA_UNITS and a % T:
                        mla_scores(a)
                    mla_probs(a - 1)
                    if a + T < MLA_UNITS:
                        mla_transpose(a + T)
                    mla_output(a - 2)
                    if 0 <= a < MLA_UNITS and a % T == 0:
                        mla_scores(a)

                def ret_transpose(p, t):
                    n = p * T + t
                    pe.wait_ge(S["r_xz"], L * PER["r_xz"] + n + 1)
                    bank = take_ring()
                    pe.transpose(bank[:, tokens(0)], r_rot[n % 2][:, 0:2, :].rearrange("p a d -> p (a d)"), ident[:])
                    pe.transpose(bank[:, tokens(1)], r_rot[n % 2][:, 2:4, :].rearrange("p a d -> p (a d)"), ident[:])
                    pe.transpose(bank[:, tokens(2)], r_xzt[n % 2][:, 0:2, :].rearrange("p a d -> p (a d)"), ident[:])\
                        .then_inc(S["tr_done"], 1)
                    ret_ready[n] = ring[0]

                ret_ready = {}

                def ret_inner(p, t):
                    n = p * T + t
                    pe.wait_ge(S["tr_free"], L * PER["tr_free"] + ret_ready[n])
                    if n >= 1:
                        pe.wait_ge(S["r_at"], L * PER["r_at"] + n)
                    hi, lo = rt_hi[n % 2], rt_lo[n % 2]
                    for j in range(2):
                        at_ = slice(64 * j, 64 * j + 64)
                        mm = products(banks[:, RET_INNER[j], 0:P], split((hi[at_, 1, :], lo[at_, 1, :]), (hi[at_, 0, :], lo[at_, 0, :])))
                    mm.then_inc(S["ri_done"], 1)
                    if t < T - 1:
                        n_s = p * (T - 1) + t
                        pe.wait_ge(S["r_kzhi"], L * PER["r_kzhi"] + n + 1)
                        pe.wait_ge(S["r_kzlo"], L * PER["r_kzlo"] + n + 1)
                        pe.wait_ge(S["z_free"], L * PER["z_free"] + Z_RET + n + 1)
                        if n_s >= 1:
                            pe.wait_ge(S["r_st"], L * PER["r_st"] + n_s)
                        products(banks[:, RET_STATE, 0:P], split((rk_hi[n % 2][:], rk_lo[n % 2][:]), (rv_hi[n % 3][:], rv_lo[n % 3][:])))\
                            .then_inc(S["rs_done"], 1)

                def ret_output(p, t):
                    n = p * T + t
                    pe.wait_ge(S["r_athi"], L * PER["r_athi"] + n + 1)
                    pe.wait_ge(S["r_atlo"], L * PER["r_atlo"] + n + 1)
                    pe.wait_ge(S["z_free"], L * PER["z_free"] + Z_RET + n + 1)
                    if n >= 1:
                        pe.wait_ge(S["r_on"], L * PER["r_on"] + n)
                    if t >= 1:
                        pe.wait_ge(S["r_sthi"], L * PER["r_sthi"] + p * (T - 1) + t)
                        pe.wait_ge(S["r_stlo"], L * PER["r_stlo"] + p * (T - 1) + t)
                    for j in range(2):
                        at_ = slice(64 * j, 64 * j + 64)
                        pairs = split((r_at_hi[:, tokens(j)], r_at_lo[:, tokens(j)]), (rv_hi[n % 3][:, at_], rv_lo[n % 3][:, at_]))
                        if t >= 1:
                            pairs += split((rt_hi[n % 2][at_, 2, :], rt_lo[n % 2][at_, 2, :]),
                                           (r_st_hi[(t - 1) % 2][at_, at_], r_st_lo[(t - 1) % 2][at_, at_]))
                        mm = products(banks[:, RET_OUT[j], 0:64], pairs)
                    mm.then_inc(S["ro_done"], 1)

                pe.wait_ge(S["s_exp"], L * PER["s_exp"] + PER["s_exp"])
                pe.wait_ge(S["o_free"], L * PER["o_free"] + PER["o_free"])
                for n in range(RET_UNITS + 2):
                    if n >= 2:
                        ret_inner((n - 2) // T, (n - 2) % T)
                    if n < RET_UNITS:
                        project(Z_RET + n, n % T, CH_RET + n // T, w_ret[n // T], 512, (0,))
                    if 1 <= n <= RET_UNITS:
                        ret_transpose((n - 1) // T, (n - 1) % T)
                    if n < RET_UNITS:
                        project(Z_RET + n, n % T, CH_RET + n // T, w_ret[n // T], 512, (1,))
                    if n >= 2:
                        ret_output((n - 2) // T, (n - 2) % T)

                pe.wait_ge(S["z_free"], L * PER["z_free"] + Z_UNITS)
                ring_empty()
                transpose_rows("mix_in", (16, 32))
                ring_empty()
                pe.wait_ge(S["r_on"], L * PER["r_on"] + 2 * T)
                for c in range(2):
                    pe.wait_ge(S["w_hi"], L * PER["w_hi"] + CH_OUT + c + 1)
                    pe.wait_ge(S["w_lo"], L * PER["w_lo"] + CH_OUT + c + 1)
                    for t in range(T):
                        q = c * T + t
                        if q >= 4:
                            pe.wait_ge(S["out_add"], L * PER["out_add"] + q - 3)
                        pairs = [pair for k in range(KD) for pair in
                                 split((ht_hi[:, k, tokens(t)], ht_lo[:, k, tokens(t)]), (w_o[c][0][:, k, :], w_o[c][1][:, k, :]))]
                        products(banks[:, q % 4, :], pairs).then_inc(S["out_done"], 1)

                transpose_rows("n_xn", (T + 4, 2 * T))
                assert ring[0] == RING
                pe.wait_ge(S["tr_free"], L * PER["tr_free"] + RING)
                pe.wait_ge(S["out_add"], L * PER["out_add"] + 2 * T)
                pe.sem_inc(S["passed"], 1)

                with pe.Fori(0, GROUPS) as g:
                    for m in range(GM):
                        pe.wait_ge(S["f_hi"], L * PER["f_hi"] + g * 3 + (m + 1))
                        pe.wait_ge(S["f_lo"], L * PER["f_lo"] + g * 3 + (m + 1))
                        for half in range(2):
                            v = 2 * m + half
                            if v >= 2:
                                pe.wait_ge(S["f_mul"], L * PER["f_mul"] + g * 4 + (v - 1))
                            for gate_or_up in range(2):
                                pairs = []
                                for k in range(KD):
                                    w = (w_gu[m][0][:, gate_or_up, k, :], w_gu[m][1][:, gate_or_up, k, :])
                                    h_ = (ht_hi[:, k, tokens(4 * half, 4)], ht_lo[:, k, tokens(4 * half, 4)])
                                    pairs += split(w, h_)
                                mm = products(banks[:, 2 * (v % 2) + gate_or_up, :], pairs)
                            mm.then_inc(S["gu_done"], 1)
                    pe.wait_ge(S["f_hi"], L * PER["f_hi"] + g * 3 + 3)
                    pe.wait_ge(S["f_lo"], L * PER["f_lo"] + g * 3 + 3)
                    for t in range(T):
                        if t % 4 == 0:
                            pe.wait_ge(S["f_act"], L * PER["f_act"] + g * 4 + (3 + t // 4))
                        for c in range(2):
                            q = 2 * t + c
                            pe.wait_ge(S["d_add"], L * PER["d_add"] + g * 2 * T + (q - 3 + ADD_CREDIT))
                            pairs = [pair for m in range(GM) for pair in
                                     split((act_hi[:, m, tokens(t)], act_lo[:, m, tokens(t)]),
                                           (w_dn[0][:, m, c * 512:(c + 1) * 512], w_dn[1][:, m, c * 512:(c + 1) * 512]))]
                            products(banks[:, 4 + q % 4, :], pairs).then_inc(S["fd_done"], 1)

        @block.scalar
        def _(act):
            act.wait_ge(S["tab_dve"], 11)
            act.activation(sin_d[:, :, 1, :], red[:, :, 0:32], ACT.Sin)
            act.activation(sin_d[:, :, 0, :], red[:, :, 0:32], ACT.Sin, scale=-1.0)
            act.activation(sin_m[:, :, 1, :], red[:, :, 32:48], ACT.Sin)
            act.activation(sin_m[:, :, 0, :], red[:, :, 32:48], ACT.Sin, scale=-1.0)
            act.activation(cos_d[:], cosarg[:, :, 0:32], ACT.Sin)
            act.activation(cos_m[:], cosarg[:, :, 32:48], ACT.Sin).then_inc(S["tab_act"], 1)

            with act.Fori(0, DEPTH) as L:
                ring = [0]

                def round_ring():
                    ring[0] += 1
                    act.wait_ge(S["tr_done"], L * PER["tr_done"] + ring[0])
                    return ring[0] - 1

                def round_weights(chunk, n_in, parts, whole=PARTS):
                    act.wait_ge(S[f"w_in{chunk % 2}"], L * PER[f"w_in{chunk % 2}"] + n_in)
                    for hi, raw in parts:
                        act.activation(hi, raw, ACT.Copy).then_inc(S["w_hi"], PARTS // whole)

                def square_rows(norm, t, ready, n):
                    act.wait_ge(S[ready], L * PER[ready] + n)
                    if norm * T + t:
                        act.wait_ge(S["n_sq"], L * PER["n_sq"] + norm * T + t)
                    act.activation(row_square[:], X[:, t, :], ACT.Square, accum_out=row_ss[:, t:t + 1])\
                        .then_inc(S["n_sq"], 1)

                def high_rows(gain):
                    for half in range(2):
                        for k in range(KD):
                            r = round_ring()
                            act.activation(ht_hi[:, k, tokens(4 * half, 4)], banks[:, NORM_BANKS[r % 4], :], ACT.Copy,
                                           scale=gain[:, k:k + 1] if gain is not None else 1.0).then_inc(S["tr_hi"], 1)

                act.wait_ge(S["x_in"], 16)
                for t in range(T):
                    square_rows(0, t, "d_add", 2 * (t + 1))
                act.wait_ge(S["params_in"], L * PER["params_in"] + PER["params_in"])
                high_rows(attn_gain)
                act.wait_ge(S["lam"], L * PER["lam"] + 2)
                act.activation(lam_exp[:], lam_sum[:], ACT.Exp).then_inc(S["lam"], 1)

                def weights(chunk, parts=range(PARTS)):
                    if chunk < CH_MLA:
                        w, n = w_diff[chunk % 2], 3 * (chunk // 2 + 1)
                    elif chunk == CH_MLA:
                        w, n = w_mla, 7
                    elif chunk == CH_UKV:
                        act.wait_ge(S["w_gain"], L * PER["w_gain"] + 1)
                        return round_weights(chunk, 16 * 10, [(w_uq[0][:], w_uq[2][:]), (w_ukv[0][:], w_ukv[2][:])], 2)
                    elif chunk < CH_OUT:
                        w, n = w_ret[chunk % 2], (11, 14)[chunk % 2]
                    else:
                        w, n = w_o[chunk % 2], (12, 15)[chunk % 2]
                    step = KD // PARTS
                    round_weights(chunk, 16 * n, [(w[0][:, i * step:(i + 1) * step, :], w[2][:, i * step:(i + 1) * step, :])
                                                  for i in parts])

                def diff_v(u):
                    if 0 <= u < DIFF_UNITS:
                        act.wait_ge(S["z_done"], L * PER["z_done"] + u + 1)
                        if u >= V_SLOTS:
                            act.wait_ge(S["pv_done"], L * PER["pv_done"] + u - V_SLOTS + 1)
                        act.activation(dv[u % V_SLOTS][:, 0, :], banks[:, z_bank(u), 2 * P:3 * P], ACT.Copy).then_inc(S["v_hi"], 1)

                def diff_qk(u):
                    t = tile_of(u)
                    r = round_ring()
                    bank = banks[:, TR_BANKS[r % 2], :].rearrange("p (a m n) -> p a m n", a=2, m=2)
                    act.activation(dq_hi[:, :, tokens(t)], bank[:, 0], ACT.Copy, scale=DIFF_SCALE)
                    act.activation(dk[:, :, tokens(t)], bank[:, 1], ACT.Copy).then_inc(S["tr_hi"], 1)

                def exponentials(j, dst, a, m, t):
                    act.wait_ge(S["s_max"], L * PER["s_max"] + j + 1)
                    act.activation(dst, SCORE[j % 2][:, 0:(t + 1) * P], ACT.Exp, bias=neg_max[:, a % 2, m:m + 1],
                                   accum_out=exp_sum[:, a % 2, m:m + 1]).then_inc(S["s_exp"], 1)

                def high_probs(a, t, hi=pt_hi, behind=0):
                    for b in range(0, t + 1, 4):
                        r = round_ring()
                        n = min(4, t + 1 - b)
                        if a >= 1:
                            act.wait_ge(S["pv_done"], L * PER["pv_done"] + a - behind)
                        act.activation(hi[:, b:b + n, :], banks[:, TR_BANKS[r % 2], 0:n * P].rearrange("p (b n) -> p b n", n=P),
                                       ACT.Copy).then_inc(S["tr_hi"], 1)

                def diff_square(a):
                    if not 0 <= a < DIFF_UNITS:
                        return
                    act.wait_ge(S["o_free"], L * PER["o_free"] + a + 1)
                    if a >= 1:
                        act.wait_ge(S["o_sq"], L * PER["o_sq"] + a)
                    act.activation(square_out[:], d_sum[a % 2][:], ACT.Square, scale=inv_sum[:, a % 4, 0:1],
                                   accum_out=o_ss[:, a % 2:a % 2 + 1]).then_inc(S["o_sq"], 1)

                def diff_exponentials(a):
                    if 0 <= a < DIFF_UNITS:
                        for m in range(2):
                            if a >= 2:
                                act.wait_ge(S["pv_done"], L * PER["pv_done"] + a - 1)
                            exponentials(2 * a + m, expo[a % 2][:, m, 0:(tile_of(a) + 1) * P], a, m, tile_of(a))

                weights(0)
                act.wait_ge(S["x_saved"], L * PER["x_saved"] + 16)
                for a in DIFF_STEPS:
                    if a % T == 0:
                        for u in diff_transposes(a)[:1]:
                            diff_qk(u)
                    if 0 <= a - 1 < DIFF_UNITS:
                        high_probs(a - 1, tile_of(a - 1))
                    for u in diff_transposes(a)[0 if a % T else 1:]:
                        diff_qk(u)
                    if a % T:
                        diff_exponentials(a)
                    diff_square(a - 2)
                    diff_v(a + T)
                    if a % T == 0:
                        diff_exponentials(a)
                    if a < DIFF_UNITS and 3 <= a % T < 3 + PARTS:
                        if a // T + 2 < CH_UKV:
                            weights(a // T + 2, [a % T - 3])
                        elif a % T == 3:
                            weights(CH_UKV)

                def mla_squares(u):
                    z = banks[:, z_bank(Z_MLA + u), :]
                    act.wait_ge(S["z_done"], L * PER["z_done"] + Z_MLA + u + 1)
                    if u == 0:
                        act.wait_ge(S["pv_done"], L * PER["pv_done"] + DIFF_HEADS * T)
                    else:
                        act.wait_ge(S["m_sq"], L * PER["m_sq"] + u)
                    act.activation(m_square[:], z[:, 0:Q_RANK], ACT.Square, accum_out=m_ss[:, u % 2, 0:1]).then_inc(S["m_sq2"], 1)
                    act.wait_ge(S["m_sq2"], L * PER["m_sq2"] + u + 1)
                    act.activation(m_square[:, 0:KV_RANK], z[:, Q_RANK:Q_RANK + KV_RANK], ACT.Square,
                                   accum_out=m_ss[:, u % 2, 1:2]).then_inc(S["m_sq"], 1)

                def mla_high(u):
                    r = round_ring()
                    if u >= 1:
                        act.wait_ge(S["u_done"], L * PER["u_done"] + u)
                    act.activation(ct_hi[:].rearrange("p b n -> p (b n)"), banks[:, TR_BANKS[r % 2], 0:3 * P], ACT.Copy).then_inc(S["tr_hi"], 1)

                def mla_up(u):
                    t = tile_of(u)
                    act.wait_ge(S["u_done"], L * PER["u_done"] + u + 1)
                    if u == 0:
                        act.wait_ge(S["mix_out0"], L * PER["mix_out0"] + 16 * DIFF_HEADS * T // 2)
                        act.wait_ge(S["mix_out1"], L * PER["mix_out1"] + 16 * DIFF_HEADS * T // 2)
                    qb = banks[:, 2 * (u % 2), 0:MLA_HEADS * MLA_QK].rearrange("p (h d) -> p h d", h=MLA_HEADS)
                    kvb = banks[:, 2 * (u % 2) + 1, :].rearrange("p (h d) -> p h d", h=MLA_HEADS)
                    act.activation(m_v[:, t, :, 0, :], kvb[:, :, NOPE:], ACT.Copy).then_inc(S["m_vhi"], 1)
                    act.activation(m_q[:, t, :, 0:NOPE], qb[:, :, 0:NOPE], ACT.Copy)
                    act.activation(m_k[:, t, :, 0:NOPE], kvb[:, :, 0:NOPE], ACT.Copy).then_inc(S["m_nope"], 1)

                def mla_qk(u):
                    t = tile_of(u)
                    r = round_ring()
                    if u >= T:
                        act.wait_ge(S["s_done"], L * PER["s_done"] + 2 * DIFF_UNITS + u - T + 1)
                    bank = banks[0:MLA_QK, TR_BANKS[r % 2], :]
                    act.activation(mq_hi[:, tokens(t)], bank[:, 0:P], ACT.Copy, scale=MLA_SCALE)
                    act.activation(mk_hi[:, tokens(t)], bank[:, P:2 * P], ACT.Copy).then_inc(S["tr_hi"], 1)

                for u in range(T + 1):
                    if u >= 1:
                        mla_high(u - 1)
                    if u < T:
                        mla_squares(u)
                    if u >= 1:
                        mla_up(u - 1)
                for a in MLA_STEPS:
                    if 0 <= a - 1 < MLA_UNITS:
                        high_probs(DIFF_UNITS + a - 1, tile_of(a - 1), mpt_hi[(a - 1) % 2], 1)
                    if a + T < MLA_UNITS:
                        mla_qk(a + T)
                    if 0 <= a < MLA_UNITS:
                        exponentials(2 * DIFF_UNITS + a, mexpo[a % 2][:, 0:(tile_of(a) + 1) * P], a, 0, tile_of(a))
                    if T <= a < T + PARTS:
                        weights(CH_RET, [a - T])

                def ret_gate_and_v(n):
                    act.wait_ge(S["z_done"], L * PER["z_done"] + Z_RET + n + 1)
                    bank = banks[:, Z_BANK, :]
                    if n == 0:
                        act.wait_ge(S["pv_done"], L * PER["pv_done"] + ATT_UNITS)
                    if n >= 3:
                        act.wait_ge(S["r_mx"], L * PER["r_mx"] + n - 2)
                        act.wait_ge(S["ro_done"], L * PER["ro_done"] + n - 2)
                    act.activation(r_gate[n % 3][:], bank[:, 3 * P:4 * P], ACT.Silu)
                    act.activation(rv_hi[n % 3][:], bank[:, 2 * P:3 * P], ACT.Copy).then_inc(S["v_hi"], 1)

                def ret_high_k(n):
                    act.wait_ge(S["r_xz"], L * PER["r_xz"] + n + 1)
                    if n >= 2:
                        act.wait_ge(S["ri_done"], L * PER["ri_done"] + n - 1)
                        if rs_count(n - 1):
                            act.wait_ge(S["rs_done"], L * PER["rs_done"] + rs_count(n - 1))
                    act.activation(rk_hi[n % 2][:], r_xzt[n % 2][:, 2:4, :].rearrange("p a d -> p (a d)"), ACT.Copy)\
                        .then_inc(S["r_kzhi"], 1)

                def rs_count(n):
                    return n - n // T

                def ret_high(n):
                    r = round_ring()
                    if n >= 2:
                        act.wait_ge(S["ro_done"], L * PER["ro_done"] + n - 1)
                    act.activation(rt_hi[n % 2][:].rearrange("p b n -> p (b n)"), banks[:, TR_BANKS[r % 2], 0:3 * P], ACT.Copy)\
                        .then_inc(S["tr_hi"], 1)

                def ret_inner(n):
                    act.wait_ge(S["r_at"], L * PER["r_at"] + n + 1)
                    if n >= 1:
                        act.wait_ge(S["ro_done"], L * PER["ro_done"] + n)
                    act.activation(r_at_hi[:], r_at[:], ACT.Copy).then_inc(S["r_athi"], 1)
                    if n % T < T - 1:
                        i = rs_count(n)
                        act.wait_ge(S["r_st"], L * PER["r_st"] + i + 1)
                        act.activation(r_st_hi[n % T % 2][:], r_st[:], ACT.Copy).then_inc(S["r_sthi"], 1)

                for n in range(RET_UNITS + 2):
                    if n >= 2:
                        ret_inner(n - 2)
                    if 1 <= n <= RET_UNITS:
                        ret_high_k(n - 1)
                        ret_high(n - 1)
                    if n < RET_UNITS:
                        ret_gate_and_v(n)
                    if 2 <= n < 2 + PARTS:
                        weights(CH_RET + 1, [n - 2])
                    if T + 2 <= n < T + 2 + PARTS:
                        weights(CH_OUT, [n - T - 2])
                weights(CH_OUT + 1)

                high_rows(None)
                for t in range(T):
                    square_rows(1, t, "out_add", T + t + 1)
                high_rows(ffn_gain)

                with act.Fori(0, GROUPS) as g:
                    for m in range(GM):
                        act.wait_ge(S[f"fg_in{m}"], L * PER[f"fg_in{m}"] + g * 32 + 32)
                        act.activation(w_gu[m][0][:], w_gu[m][2][:], ACT.Copy).then_inc(S["f_hi"], 1)
                    act.wait_ge(S["fd_in"], L * PER["fd_in"] + g * 16 + 16)
                    act.activation(w_dn[0][:], w_dn[2][:], ACT.Copy).then_inc(S["f_hi"], 1)
                    for v in range(4):
                        m, half = v // 2, v % 2
                        act.wait_ge(S["gu_done"], L * PER["gu_done"] + g * 4 + (v + 1 + GU_CREDIT))
                        act.activation(f_gate[v % 2][:], banks[:, 2 * (v % 2), :], ACT.Silu).then_inc(S["f_silu"], 1)
                        act.wait_ge(S["f_mul"], L * PER["f_mul"] + g * 4 + (v + 1))
                        act.activation(act_hi[:, m, tokens(4 * half, 4)], f_prod[v % 2][:], ACT.Copy).then_inc(S["f_ahi"], 1)

            for t in range(T):
                act.wait_ge(S["d_add"], DEPTH * PER["d_add"] + 2 * (t + 1))
                if t:
                    act.wait_ge(S["f_sq"], t)
                act.activation(row_square[:], X[:, t, :], ACT.Square, accum_out=row_ss[:, t:t + 1]).then_inc(S["f_sq"], 1)

        @block.vector
        def _(dve):
            dve.sem_inc(S["d_add"], ADD_CREDIT)
            tab = [0]

            def table_step(ins):
                tab[0] += 1
                ins.then_inc(S["tab_dve"], 1)
                dve.wait_ge(S["tab_dve"], tab[0])

            dve.wait_ge(S["const_in"], 64)
            dve.tensor_copy(ident_r[:], consts[:, C_IDENT:C_IDENT + P]).then_inc(S["ident_ok"], 1)
            dve.tensor_copy(mask_r[:], consts[:, C_MASK:C_MASK + P]).then_inc(S["ident_ok"], 1)
            dve.wait_ge(S["pos_in"], 16)
            table_step(dve.tensor_copy(pos_f[:], pos_int[:]))
            table_step(dve.tensor_tensor(ang[:], pos_f[:].unsqueeze(2).to_broadcast([P, T, 48]),
                                         consts[:, C_INVF:C_INVF + 48].unsqueeze(1).to_broadcast([P, T, 48]), ALU.mult))
            magic = 1.5 * 2.0 ** 23
            table_step(dve.tensor_scalar(turns[:], ang[:], 1.0 / (2 * math.pi), magic, ALU.mult, ALU.add))
            table_step(dve.tensor_scalar(turns[:], turns[:], magic, None, ALU.subtract))
            left = 2 * math.pi
            for bits in (5, 13, 30, 50):
                part = round(left * 2.0 ** bits) / 2.0 ** bits
                left -= part
                table_step(dve.scalar_tensor_tensor(red[:], turns[:], -part, ang[:] if bits == 5 else red[:], ALU.mult, ALU.add))
            top = float(np.nextafter(np.float32(math.pi), np.float32(0)))
            table_step(dve.tensor_scalar(red[:], red[:], top, -top, ALU.min, ALU.max))
            table_step(dve.scalar_tensor_tensor(cosarg[:], red[:], -1.0, red[:], ALU.mult, ALU.max))
            table_step(dve.tensor_scalar(cosarg[:], cosarg[:], -1.0, math.pi / 2, ALU.mult, ALU.add))
            dve.wait_ge(S["tab_act"], 1)

            with dve.Fori(0, DEPTH) as L:
                ring = [0]

                def low_ring():
                    ring[0] += 1
                    dve.wait_ge(S["tr_hi"], L * PER["tr_hi"] + ring[0])
                    return ring[0] - 1

                def scale_rows(norm, half):
                    for j in range(4):
                        t = 4 * half + j
                        dve.wait_ge(S["n_rstd"], L * PER["n_rstd"] + 2 * norm + half + 1)
                        dve.tensor_scalar(rows[:, j, :], X[:, t, :], row_rstd[:, t:t + 1], None, ALU.mult)\
                            .then_inc(S["n_xn"], 1)

                def low_rows(half, gain):
                    for k in range(KD):
                        r = low_ring()
                        at_ = tokens(4 * half, 4)
                        bank = banks[:, NORM_BANKS[r % 4], :]
                        hi = ht_hi[:, k, at_].bitcast(F32)
                        if gain is None:
                            lo = dve.tensor_tensor(ht_lo[:, k, at_], bank, hi, ALU.subtract)
                        else:
                            lo = dve.scalar_tensor_tensor(ht_lo[:, k, at_], bank, gain[:, k:k + 1], hi, ALU.mult, ALU.subtract)
                        lo.then_inc(S["tr_free"], 1)

                def norm_rows(norm, gain):
                    for half in range(2):
                        if half:
                            dve.wait_ge(S["tr_done"], L * PER["tr_done"] + ring[0])
                        scale_rows(norm, half)
                        low_rows(half, gain)

                dve.wait_ge(S["params_in"], L * PER["params_in"] + PER["params_in"])
                norm_rows(0, attn_gain)
                for m in range(2):
                    if m:
                        dve.wait_ge(S["lam"], L * PER["lam"] + 1)
                    dve.tensor_tensor_reduce(lam_prod[:], lam_vec[:, 2 * m, :], lam_vec[:, 2 * m + 1, :], 1.0, 0.0, ALU.mult,
                                             ALU.add, lam_sum[:, m:m + 1]).then_inc(S["lam"], 1)
                dve.wait_ge(S["lam"], L * PER["lam"] + 3)
                dve.tensor_tensor(neg_lam[:], lam_exp[:, 1:2], lam_exp[:, 0:1], ALU.subtract).then_inc(S["lam"], 1)
                dve.wait_ge(S["lam"], L * PER["lam"] + 4)
                dve.tensor_tensor(neg_lam[:], neg_lam[:], lam_const[:, 0:1], ALU.subtract)
                dve.tensor_scalar(subln[:], subln[:], lam_const[:, 1:2], None, ALU.mult).then_inc(S["lam"], 1)
                dve.wait_ge(S["lam"], L * PER["lam"] + 5)

                def rotate(z, a, b, t):
                    dve.tensor_tensor(a[:].rearrange("p v s d -> p (v s) d"), z.rearrange("p (v d) -> p v d", d=32),
                                      cos_d[:, t, :].unsqueeze(1).to_broadcast([P, 8, 32]), ALU.mult)
                    return dve.tensor_tensor(b[:], z.rearrange("p (v s d) -> p v s d", v=4, s=2)[:, :, ::-1, :],
                                             sin_d[:, t].unsqueeze(1).to_broadcast([P, 4, 2, 32]), ALU.mult)

                def diff_rotate(u):
                    if not 0 <= u < DIFF_UNITS:
                        return
                    bank = banks[:, z_bank(u), :]
                    dve.wait_ge(S["v_hi"], L * PER["v_hi"] + u + 1)
                    if u >= 2:
                        dve.wait_ge(S["rope_sum"], L * PER["rope_sum"] + u - 1)
                    rotate(bank[:, 0:2 * P], rope_a[u % 2], rope_b[u % 2], tile_of(u)).then_inc(S["rope_ab"], 1)
                    v = u % V_SLOTS
                    dve.tensor_tensor(dv[v][:, 1, :], bank[:, 2 * P:3 * P], dv[v][:, 0, :].bitcast(F32), ALU.subtract)\
                        .then_inc(S["z_free"], 1)

                def diff_low(u):
                    t = tile_of(u)
                    r = low_ring()
                    bank = banks[:, TR_BANKS[r % 2], :].rearrange("p (a m n) -> p a m n", a=2, m=2)
                    dve.scalar_tensor_tensor(dq_lo[:, :, tokens(t)], bank[:, 0], DIFF_SCALE, dq_hi[:, :, tokens(t)].bitcast(F32),
                                             ALU.mult, ALU.subtract)
                    low = dk[64:P, :, tokens(t)]
                    dve.tensor_tensor(low, bank[64:P, 1], low.bitcast(F32), ALU.subtract).then_inc(S["tr_free"], 1)

                def negated_max(j, a, m, t):
                    dve.wait_ge(S["s_done"], L * PER["s_done"] + j + 1)
                    dve.tensor_reduce(neg_max[:, a % 2, m:m + 1], SCORE[j % 2][:, 0:(t + 1) * P], AX_X, ALU.max, negate=True)\
                        .then_inc(S["s_max"], 1)

                def combine(a):
                    t = tile_of(a)
                    b = a % 2
                    dve.wait_ge(S["s_exp"], L * PER["s_exp"] + 2 * a + 2)
                    if a >= 4:
                        dve.wait_ge(S["o_out"], L * PER["o_out"] + a - 3)
                    dve.reciprocal(inv_sum[:, a % 4, :], exp_sum[:, b, :]).then_inc(S["inv_sum"], 1)
                    dve.wait_ge(S["inv_sum"], L * PER["inv_sum"] + a + 1)
                    dve.scalar_tensor_tensor(ratio[:, b:b + 1], exp_sum[:, b, 0:1], neg_lam[:], inv_sum[:, a % 4, 1:2],
                                             ALU.mult, ALU.mult).then_inc(S["lam_ratio"], 1)
                    dve.wait_ge(S["lam_ratio"], L * PER["lam_ratio"] + a + 1)
                    e = expo[b]
                    n = (t + 1) * P
                    dve.scalar_tensor_tensor(e[:, 0, 0:n], e[:, 1, 0:n], ratio[:, b:b + 1], e[:, 0, 0:n], ALU.mult, ALU.add)\
                        .then_inc(S["p_ready"], 1)

                def low_probs(t, hi=pt_hi, lo=pt_lo):
                    for b in range(0, t + 1, 4):
                        r = low_ring()
                        n = min(4, t + 1 - b)
                        dve.tensor_tensor(lo[:, b:b + n, :], banks[:, TR_BANKS[r % 2], 0:n * P].rearrange("p (b n) -> p b n", n=P),
                                          hi[:, b:b + n, :].bitcast(F32), ALU.subtract).then_inc(S["tr_free"], 1)

                def diff_take(a):
                    if 0 <= a < DIFF_UNITS:
                        dve.wait_ge(S["pv_done"], L * PER["pv_done"] + a + 1)
                        if a >= 2:
                            dve.wait_ge(S["o_out"], L * PER["o_out"] + a - 1)
                        take_output(d_sum[a % 2][:], banks[:, O_BANK, :], P)

                def take_output(dst, bank, width):
                    dve.tensor_reduce(dst, bank[:, 0:2 * width].rearrange("p (c d) -> p d c", c=2), AX_X, ALU.add).then_inc(S["o_free"], 1)

                def diff_maxima(a):
                    if 0 <= a < DIFF_UNITS:
                        for m in range(2):
                            negated_max(2 * a + m, a, m, tile_of(a))

                for a in DIFF_STEPS:
                    diff_rotate(a + T - 1)
                    diff_take(a - 2)
                    if a % T:
                        diff_maxima(a)
                    else:
                        for u in diff_transposes(a)[:1]:
                            diff_low(u)
                    if 0 <= a - 1 < DIFF_UNITS:
                        low_probs(tile_of(a - 1))
                    for u in diff_transposes(a)[0 if a % T else 1:]:
                        diff_low(u)
                    if a % T == 0:
                        diff_maxima(a)
                    if 0 <= a < DIFF_UNITS:
                        combine(a)

                def mla_latents(u):
                    t = tile_of(u)
                    z = banks[:, z_bank(Z_MLA + u), 0:MLA_COLS]
                    dve.wait_ge(S["m_sq"], L * PER["m_sq"] + u + 1)
                    zr = z[:, Q_RANK + KV_RANK:MLA_COLS].rearrange("p (s d) -> p s d", s=2)
                    if u >= 1:
                        dve.wait_ge(S["m_krope"], L * PER["m_krope"] + u)
                    dve.tensor_tensor(mk_a[:], zr, cos_m[:, t, :].unsqueeze(1).to_broadcast([P, 2, 16]), ALU.mult)
                    dve.tensor_tensor(mk_b[:], zr[:, ::-1, :], sin_m[:, t], ALU.mult).then_inc(S["m_kab"], 1)
                    dve.wait_ge(S["m_rstd"], L * PER["m_rstd"] + u + 1)
                    if u >= 1:
                        dve.wait_ge(S["tr_done"], L * PER["tr_done"] + ring[0])
                    dve.tensor_scalar(cn[:, 0:2, :].rearrange("p b n -> p (b n)"), z[:, 0:Q_RANK], m_rs[:, u % 2, 0:1], None, ALU.mult)
                    dve.tensor_scalar(cn[:, 2, :], z[:, Q_RANK:Q_RANK + KV_RANK], m_rs[:, u % 2, 1:2], None, ALU.mult)\
                        .then_inc(S["z_free"], 1)

                def mla_low_latents():
                    r = low_ring()
                    dve.tensor_tensor(ct_lo[:].rearrange("p b n -> p (b n)"), banks[:, TR_BANKS[r % 2], 0:3 * P],
                                      ct_hi[:].rearrange("p b n -> p (b n)").bitcast(F32), ALU.subtract).then_inc(S["tr_free"], 1)

                def mla_up(u):
                    t = tile_of(u)
                    dve.wait_ge(S["m_nope"], L * PER["m_nope"] + u + 1)
                    qb = banks[:, 2 * (u % 2), 0:MLA_HEADS * MLA_QK].rearrange("p (h d) -> p h d", h=MLA_HEADS)
                    kvb = banks[:, 2 * (u % 2) + 1, :].rearrange("p (h d) -> p h d", h=MLA_HEADS)
                    qr = qb[:, :, NOPE:].rearrange("p h (s d) -> p h s d", s=2)
                    if u >= 1:
                        dve.wait_ge(S["m_qrope"], L * PER["m_qrope"] + u)
                    dve.tensor_tensor(mq_a[:], qr, cos_m[:, t, :].unsqueeze(1).unsqueeze(1).to_broadcast([P, MLA_HEADS, 2, 16]), ALU.mult)
                    dve.tensor_tensor(mq_b[:], qr[:, :, ::-1, :], sin_m[:, t].unsqueeze(1).to_broadcast([P, MLA_HEADS, 2, 16]),
                                      ALU.mult).then_inc(S["m_qab"], 1)
                    dve.tensor_tensor(m_v[:, t, :, 1, :], kvb[:, :, NOPE:], m_v[:, t, :, 0, :].bitcast(F32), ALU.subtract).then_inc(S["u_free"], 1)

                def mla_low(u):
                    t = tile_of(u)
                    r = low_ring()
                    bank = banks[0:MLA_QK, TR_BANKS[r % 2], :]
                    dve.scalar_tensor_tensor(mq_lo[:, tokens(t)], bank[:, 0:P], MLA_SCALE, mq_hi[:, tokens(t)].bitcast(F32),
                                             ALU.mult, ALU.subtract)
                    dve.tensor_tensor(mk_lo[:, tokens(t)], bank[:, P:2 * P], mk_hi[:, tokens(t)].bitcast(F32), ALU.subtract)\
                        .then_inc(S["tr_free"], 1)

                def mla_sum(a):
                    if 0 <= a < MLA_UNITS:
                        dve.wait_ge(S["s_exp"], L * PER["s_exp"] + 2 * DIFF_UNITS + a + 1)
                        if a >= 4:
                            dve.wait_ge(S["o_out"], L * PER["o_out"] + DIFF_UNITS + a - 3)
                        dve.reciprocal(inv_sum[:, a % 4, 0:1], exp_sum[:, a % 2, 0:1]).then_inc(S["inv_sum"], 1)

                def mla_take(a):
                    if 0 <= a < MLA_UNITS:
                        dve.wait_ge(S["pv_done"], L * PER["pv_done"] + DIFF_UNITS + a + 1)
                        dve.wait_ge(S["o_out"], L * PER["o_out"] + DIFF_UNITS + a - 1)
                        take_output(m_sum[a % 2][:], banks[:, o_bank(a), :], MLA_V)

                for u in range(T + 1):
                    if u >= 1:
                        mla_low_latents()
                    if u < T:
                        mla_latents(u)
                    if u >= 1:
                        mla_up(u - 1)
                for a in MLA_STEPS:
                    if 0 <= a < MLA_UNITS and a % T:
                        negated_max(2 * DIFF_UNITS + a, a, 0, tile_of(a))
                    if 0 <= a - 1 < MLA_UNITS:
                        low_probs(tile_of(a - 1), mpt_hi[(a - 1) % 2], mpt_lo[(a - 1) % 2])
                    if a + T < MLA_UNITS:
                        mla_low(a + T)
                    if 0 <= a < MLA_UNITS and a % T == 0:
                        negated_max(2 * DIFF_UNITS + a, a, 0, tile_of(a))
                    mla_take(a - 3)
                    mla_sum(a - 1)

                def ret_rotate(n):
                    t = n % T
                    dve.wait_ge(S["v_hi"], L * PER["v_hi"] + ROPE_RET + n + 1)
                    bank = banks[:, Z_BANK, :]
                    if n >= 2:
                        dve.wait_ge(S["rope_sum"], L * PER["rope_sum"] + ROPE_RET + n - 1)
                    rotate(bank[:, 0:2 * P], r_ab[n % 2][0], r_ab[n % 2][1], t).then_inc(S["rope_ab"], 1)
                    dve.tensor_tensor(rv_lo[n % 3][:], bank[:, 2 * P:3 * P], rv_hi[n % 3][:].bitcast(F32), ALU.subtract)\
                        .then_inc(S["z_free"], 1)

                def rs_count(n):
                    return n - n // T

                def ret_low(n):
                    r = low_ring()
                    dve.tensor_tensor(rt_lo[n % 2][:].rearrange("p b n -> p (b n)"), banks[:, TR_BANKS[r % 2], 0:3 * P],
                                      rt_hi[n % 2][:].rearrange("p b n -> p (b n)").bitcast(F32), ALU.subtract).then_inc(S["tr_free"], 1)

                def ret_inner(n):
                    p = n // T
                    if n == 0:
                        dve.wait_ge(S["ret_in"], L * PER["ret_in"] + PER["ret_in"])
                    dve.wait_ge(S["ri_done"], L * PER["ri_done"] + n + 1)
                    if n >= 1:
                        dve.wait_ge(S["r_atlo"], L * PER["r_atlo"] + n)
                    dve.tensor_tensor(r_at[:].rearrange("p (j n) -> p j n", j=2), banks[:, 0:2, 0:P], decay[:, p, :].rearrange("p (j n) -> p j n", j=2), ALU.mult).then_inc(S["r_at"], 1)
                    if n % T < T - 1:
                        i = rs_count(n)
                        dve.wait_ge(S["rs_done"], L * PER["rs_done"] + i + 1)
                        if i:
                            dve.wait_ge(S["r_sthi"], L * PER["r_sthi"] + i)
                            dve.wait_ge(S["r_stlo"], L * PER["r_stlo"] + i)
                        if n % T == 0:
                            st = dve.tensor_copy(r_st[:], banks[:, RET_STATE, 0:P])
                        else:
                            st = dve.scalar_tensor_tensor(r_st[:], r_st[:], cd[:, p:p + 1], banks[:, RET_STATE, 0:P], ALU.mult, ALU.add)
                        st.then_inc(S["r_st"], 1)

                def ret_moments(n):
                    b = n % 2
                    dve.wait_ge(S["ro_done"], L * PER["ro_done"] + n + 1)
                    for j in range(2):
                        st = dve.bn_stats(bn[:, b, j, :], banks[:, RET_OUT[j], 0:64])
                    st.then_inc(S["r_bn"], 1)
                    dve.wait_ge(S["r_bn"], L * PER["r_bn"] + n + 1)
                    dve.sem_inc(S["passed"], 1)
                    for j in range(2):
                        st = dve.bn_aggr(mv[:, b, j, :], bn[:, b, j, :])
                    st.then_inc(S["r_mv"], 1)

                def ret_normed(n):
                    b = n % 2
                    dve.wait_ge(S["r_rstd"], L * PER["r_rstd"] + n + 1)
                    if n >= 2:
                        dve.wait_ge(S["r_gw"], L * PER["r_gw"] + n - 1)
                    for j in range(2):
                        st = dve.tensor_scalar(r_norm[b][:, 64 * j:64 * j + 64], banks[:, RET_OUT[j], 0:64],
                                               mv[:, b, j, 0:1], r_rs[:, b, j:j + 1], ALU.subtract, ALU.mult)
                    st.then_inc(S["r_on"], 1)

                for n in range(RET_UNITS + 3):
                    if 2 <= n < RET_UNITS + 2:
                        ret_inner(n - 2)
                    if n >= 3:
                        ret_normed(n - 3)
                    if 1 <= n <= RET_UNITS:
                        ret_low(n - 1)
                    if n < RET_UNITS:
                        ret_rotate(n)
                    if 2 <= n < RET_UNITS + 2:
                        ret_moments(n - 2)

                for half in range(2):
                    low_rows(half, None)
                dve.wait_ge(S["x_back"], L * PER["x_back"] + 16)
                for q in range(2 * T):
                    c, t = q // T, q % T
                    cols = slice(c * 512, (c + 1) * 512)
                    dve.wait_ge(S["out_done"], L * PER["out_done"] + q + 1)
                    dve.tensor_tensor(X[:, t, cols], X[:, t, cols], banks[:, q % 4, :], ALU.add).then_inc(S["out_add"], 1)
                dve.wait_ge(S["out_add"], L * PER["out_add"] + 2 * T)
                norm_rows(1, ffn_gain)

                with dve.Fori(0, GROUPS) as g:
                    for v in range(4):
                        m, half = v // 2, v % 2
                        dve.wait_ge(S["f_silu"], L * PER["f_silu"] + g * 4 + (v + 1))
                        if v >= 2:
                            dve.wait_ge(S["f_act"], L * PER["f_act"] + g * 4 + (v - 1))
                        dve.tensor_tensor(f_prod[v % 2][:], banks[:, 2 * (v % 2) + 1, :], f_gate[v % 2][:], ALU.mult)\
                            .then_inc(S["f_mul"], 1)
                        dve.wait_ge(S["f_ahi"], L * PER["f_ahi"] + g * 4 + (v + 1))
                        dve.tensor_tensor(act_lo[:, m, tokens(4 * half, 4)], f_prod[v % 2][:],
                                          act_hi[:, m, tokens(4 * half, 4)].bitcast(F32), ALU.subtract).then_inc(S["f_act"], 1)
                    for q in range(2 * T):
                        t, c = q // 2, q % 2
                        cols = slice(c * 512, (c + 1) * 512)
                        dve.wait_ge(S["fd_done"], L * PER["fd_done"] + g * 2 * T + (q + 1 + D_CREDIT))
                        dve.tensor_tensor(X[:, t, cols], X[:, t, cols], banks[:, 4 + q % 4, :], ALU.add).then_inc(S["d_add"], 1)
                    dve.wait_ge(S["d_add"], L * PER["d_add"] + g * 2 * T + (2 * T + ADD_CREDIT))

            dve.wait_ge(S["final_in"], 16)
            for t in range(T):
                dve.wait_ge(S["f_rstd"], t // 4 + 1)
                if t >= 4:
                    dve.wait_ge(S[f"y_out{t % 4}"], 16)
                dve.scalar_tensor_tensor(rows[:, t % 4, :], X[:, t, :], row_rstd[:, t:t + 1], final_gain[:], ALU.mult, ALU.mult)\
                    .then_inc(S["y_ready"], 1)

        @block.gpsimd
        def _(pool):
            pool.memset(minus_half, -0.5).then_inc(S["half_ok"], 1)
            pool.wait_ge(S["half_ok"], 1)

            def inverse_root(out_, in_):
                return pool.tensor_tensor(out_, in_, minus_half[:, 0:in_.shape[1]], ALU.pow)

            with pool.Fori(0, DEPTH) as L:

                def inverse_roots(norm):
                    for half in range(2):
                        i = 2 * norm + half
                        cols = slice(4 * half, 4 * half + 4)
                        if norm:
                            pool.wait_ge(S["n_xn"], L * PER["n_xn"] + T)
                        pool.wait_ge(S["n_sq"], L * PER["n_sq"] + norm * T + 4 * half + 4)
                        pool.sem_inc(S["passed"], 1)
                        pool.tensor_scalar(row_ms[:, cols], row_ss[:, cols], 1.0 / D, NORM_EPS, ALU.mult, ALU.add).then_inc(S["n_ms"], 1)
                        pool.wait_ge(S["n_ms"], L * PER["n_ms"] + i + 1)
                        inverse_root(row_rstd[:, cols], row_ms[:, cols]).then_inc(S["n_rstd"], 1)

                def weights(chunk, parts=range(PARTS)):
                    if chunk == CH_UKV:
                        pool.wait_ge(S["w_hi"], L * PER["w_hi"] + PARTS * (chunk + 1))
                        pool.tensor_tensor(w_uq[1][:], w_uq[2][:], w_uq[0][:].bitcast(F32), ALU.subtract)
                        pool.tensor_tensor(w_ukv[1][:], w_ukv[2][:], w_ukv[0][:].bitcast(F32), ALU.subtract).then_inc(S["w_lo"], 1)
                        return
                    w = (w_diff[chunk % 2] if chunk < CH_MLA else w_mla if chunk == CH_MLA else
                         w_ret[chunk % 2] if chunk < CH_OUT else w_o[chunk % 2])
                    step = KD // PARTS
                    for i in parts:
                        pool.wait_ge(S["w_hi"], L * PER["w_hi"] + PARTS * chunk + i + 1)
                        k = slice(i * step, (i + 1) * step)
                        st = pool.tensor_tensor(w[1][:, k, :], w[2][:, k, :], w[0][:, k, :].bitcast(F32), ALU.subtract)
                        if i == PARTS - 1:
                            st.then_inc(S["w_lo"], 1)

                inverse_roots(0)
                weights(0)

                def rotation(n, a, b, dst, copies):
                    pool.wait_ge(S["rope_ab"], L * PER["rope_ab"] + n + 1)
                    a, b = (x[:].rearrange("p v s d -> p v (s d)").unsqueeze(2).to_broadcast([P, 4, copies, 64]) for x in (a, b))
                    return pool.tensor_tensor(dst[:] if copies > 1 else dst[:].unsqueeze(2), a, b, ALU.add)

                def diff_rotation(u):
                    if not 0 <= u < DIFF_UNITS:
                        return
                    if u >= 2:
                        pool.wait_ge(S["tr_done"], L * PER["tr_done"] + qk_ring[u - 2])
                    rotation(u, rope_a[u % 2], rope_b[u % 2], qk_rot[u % 2], 2).then_inc(S["rope_sum"], 1)

                def diff_root(a):
                    if not 0 <= a < DIFF_UNITS:
                        return
                    b = slice(a % 2, a % 2 + 1)
                    pool.wait_ge(S["o_sq"], L * PER["o_sq"] + a + 1)
                    pool.sem_inc(S["passed"], 1)
                    pool.tensor_scalar(o_ms[:, b], o_ss[:, b], 1.0 / (2 * DIFF_DIM), SUBLN_EPS, ALU.mult, ALU.add).then_inc(S["o_ms"], 1)
                    pool.wait_ge(S["o_ms"], L * PER["o_ms"] + 3 * a + 1)
                    inverse_root(o_rs[:, b], o_ms[:, b]).then_inc(S["o_ms"], 1)
                    pool.wait_ge(S["o_ms"], L * PER["o_ms"] + 3 * a + 2)
                    pool.tensor_tensor(o_rr[:, b], o_rs[:, b], inv_sum[:, a % 4, 0:1], ALU.mult).then_inc(S["o_ms"], 1)
                    if a >= 2:
                        pool.wait_ge(S[f"mix_out{a % 2}"], L * PER[f"mix_out{a % 2}"] + 16 * (a // 2))
                    pool.wait_ge(S["o_ms"], L * PER["o_ms"] + 3 * a + 3)
                    pool.tensor_tensor(d_mx[a % 2][:], d_sum[a % 2][:], o_rr[:, b].to_broadcast([P, P]), ALU.mult).then_inc(S["o_rr"], 1)
                    pool.wait_ge(S["o_rr"], L * PER["o_rr"] + a + 1)
                    pool.tensor_tensor(d_mx[a % 2][:], d_mx[a % 2][:], subln[:], ALU.mult).then_inc(S["o_out"], 1)

                for a in DIFF_STEPS:
                    diff_rotation(a + T - 1)
                    diff_root(a - 2)
                    if a < DIFF_UNITS and a // T + 2 < CH_UKV and 3 <= a % T < 3 + PARTS:
                        weights(a // T + 2, [a % T - 3])
                    elif a == (CH_UKV - 2) * T + 1:
                        pool.wait_ge(S["w_in1"], L * PER["w_in1"] + 16 * 10)
                        pool.sem_inc(S["passed"], 1)
                        for k in range(2):
                            pool.tensor_scalar(w_uq[2][:, k, :], w_uq[2][:, k, :], q_gain[:, k:k + 1], None, ALU.mult)
                        pool.tensor_scalar(w_ukv[2][:], w_ukv[2][:], kv_gain[:], None, ALU.mult).then_inc(S["w_gain"], 1)
                    elif a == (CH_UKV - 2) * T + 3:
                        weights(CH_UKV)

                def mla_roots(t):
                    u = T - 1 - t
                    b = u % 2
                    pool.wait_ge(S["m_sq"], L * PER["m_sq"] + u + 1)
                    pool.sem_inc(S["passed"], 1)
                    pool.tensor_scalar(m_msq[:, b, 0:1], m_ss[:, b, 0:1], 1.0 / Q_RANK, NORM_EPS, ALU.mult, ALU.add)
                    pool.tensor_scalar(m_msq[:, b, 1:2], m_ss[:, b, 1:2], 1.0 / KV_RANK, NORM_EPS, ALU.mult, ALU.add).then_inc(S["m_ms"], 2)
                    pool.wait_ge(S["m_ms"], L * PER["m_ms"] + 2 * u + 2)
                    inverse_root(m_rs[:, b, :], m_msq[:, b, :]).then_inc(S["m_rstd"], 1)
                    pool.wait_ge(S["m_kab"], L * PER["m_kab"] + u + 1)
                    if u == 0:
                        pool.wait_ge(S["pv_done"], L * PER["pv_done"] + DIFF_HEADS * T)
                        pool.wait_ge(S["mix_out0"], L * PER["mix_out0"] + 16 * DIFF_HEADS * T // 2)
                        pool.wait_ge(S["mix_out1"], L * PER["mix_out1"] + 16 * DIFF_HEADS * T // 2)
                    pool.tensor_tensor(m_k[:, t, :, NOPE:], mk_a[:].rearrange("p s d -> p (s d)").unsqueeze(1).to_broadcast([P, MLA_HEADS, ROPE]),
                                       mk_b[:].rearrange("p s d -> p (s d)").unsqueeze(1).to_broadcast([P, MLA_HEADS, ROPE]), ALU.add)\
                        .then_inc(S["m_krope"], 1)

                def mla_q_rotation(t):
                    u = T - 1 - t
                    pool.wait_ge(S["m_qab"], L * PER["m_qab"] + u + 1)
                    pool.tensor_tensor(m_q[:, t, :, NOPE:], mq_a[:].rearrange("p h s d -> p h (s d)"), mq_b[:].rearrange("p h s d -> p h (s d)"),
                                       ALU.add).then_inc(S["m_qrope"], 1)

                for s in range(T + 1):
                    if s < T:
                        mla_roots(T - 1 - s)
                    if s >= 1:
                        mla_q_rotation(T - s)
                for a in range(MLA_UNITS):
                    pool.wait_ge(S["inv_sum"], L * PER["inv_sum"] + DIFF_UNITS + a + 1)
                    pool.wait_ge(S[f"mix_out{a % 2}"], L * PER[f"mix_out{a % 2}"] + 16 * ((DIFF_UNITS + a) // 2))
                    pool.wait_ge(S["o_free"], L * PER["o_free"] + DIFF_UNITS + a + 1)
                    pool.tensor_tensor(m_mx[a % 2][:], m_sum[a % 2][:], inv_sum[:, a % 4, 0:1].to_broadcast([P, MLA_V]), ALU.mult)\
                        .then_inc(S["o_out"], 1)
                    if T <= a < T + PARTS:
                        weights(CH_RET, [a - T])

                def rs_count(n):
                    return n - n // T

                def ret_scaled(n):
                    b = n % 2
                    if n == 0:
                        pool.wait_ge(S["pv_done"], L * PER["pv_done"] + ATT_UNITS)
                    if n >= 2:
                        pool.wait_ge(S["tr_done"], L * PER["tr_done"] + ret_ring + n - 1)
                        pool.wait_ge(S["r_kzhi"], L * PER["r_kzhi"] + n - 1)
                    rotation(ROPE_RET + n, r_ab[b][0], r_ab[b][1], r_rot[b], 1).then_inc(S["rope_sum"], 1)
                    pool.wait_ge(S["rope_sum"], L * PER["rope_sum"] + ROPE_RET + n + 1)
                    pool.tensor_tensor(r_xzt[b][:], r_rot[b][:], xz[:, n // T, :].unsqueeze(2).to_broadcast([P, 4, 64]), ALU.mult)\
                        .then_inc(S["r_xz"], 1)

                def ret_low_k(n):
                    b = n % 2
                    pool.wait_ge(S["r_kzhi"], L * PER["r_kzhi"] + n + 1)
                    pool.tensor_tensor(rk_lo[b][:], r_xzt[b][:, 2:4, :].rearrange("p a d -> p (a d)"), rk_hi[b][:].bitcast(F32), ALU.subtract)\
                        .then_inc(S["r_kzlo"], 1)

                def ret_inner(n):
                    pool.wait_ge(S["r_athi"], L * PER["r_athi"] + n + 1)
                    pool.tensor_tensor(r_at_lo[:], r_at[:], r_at_hi[:].bitcast(F32), ALU.subtract).then_inc(S["r_atlo"], 1)
                    if n % T < T - 1:
                        i = rs_count(n)
                        pool.wait_ge(S["r_sthi"], L * PER["r_sthi"] + i + 1)
                        b = n % T % 2
                        pool.tensor_tensor(r_st_lo[b][:], r_st[:], r_st_hi[b][:].bitcast(F32), ALU.subtract).then_inc(S["r_stlo"], 1)

                def ret_root(n):
                    b = n % 2
                    pool.wait_ge(S["r_mv"], L * PER["r_mv"] + n + 1)
                    pool.sem_inc(S["passed"], 1)
                    pool.tensor_scalar(r_ms[:, b, :], mv[:, b, :, 1], GN_EPS, None, ALU.add).then_inc(S["r_ms"], 1)
                    pool.wait_ge(S["r_ms"], L * PER["r_ms"] + n + 1)
                    inverse_root(r_rs[:, b, :], r_ms[:, b, :]).then_inc(S["r_rstd"], 1)

                def ret_finish(n):
                    b, p = n % 2, n // T
                    pool.wait_ge(S["r_on"], L * PER["r_on"] + n + 1)
                    cols = slice(p * P, (p + 1) * P)
                    if n == 0:
                        pool.wait_ge(S["ret_in"], L * PER["ret_in"] + PER["ret_in"])
                    if n >= 2:
                        pool.wait_ge(S[f"mix_out{b}"], L * PER[f"mix_out{b}"] + 16 * (ATT_UNITS // 2 + n // 2))
                    pool.tensor_tensor(r_mx[b][:], r_norm[b][:], gn_w[:, cols], ALU.mult).then_inc(S["r_gw"], 1)
                    pool.wait_ge(S["r_gw"], L * PER["r_gw"] + n + 1)
                    pool.tensor_tensor(r_mx[b][:], r_mx[b][:], gn_b[:, cols], ALU.add).then_inc(S["r_gb"], 1)
                    pool.wait_ge(S["r_gb"], L * PER["r_gb"] + n + 1)
                    pool.tensor_tensor(r_mx[b][:], r_mx[b][:], r_gate[n % 3][:], ALU.mult).then_inc(S["r_mx"], 1)

                ret_ring = RING - 2 * 2 * KD - 2 * T
                for n in range(RET_UNITS + 3):
                    if 2 <= n < RET_UNITS + 2:
                        ret_inner(n - 2)
                    if 1 <= n <= RET_UNITS:
                        ret_low_k(n - 1)
                    if n >= 3:
                        ret_finish(n - 3)
                    if n < RET_UNITS:
                        ret_scaled(n)
                    if 2 <= n < RET_UNITS + 2:
                        ret_root(n - 2)
                    if 2 <= n < 2 + PARTS:
                        weights(CH_RET + 1, [n - 2])
                    if T + 2 <= n < T + 2 + PARTS:
                        weights(CH_OUT, [n - T - 2])
                weights(CH_OUT + 1)
                inverse_roots(1)

                with pool.Fori(0, GROUPS) as g:
                    for i, w in enumerate((w_gu[0], w_gu[1], w_dn)):
                        pool.wait_ge(S["f_hi"], L * PER["f_hi"] + g * 3 + (i + 1))
                        pool.tensor_tensor(w[1][:], w[2][:], w[0][:].bitcast(F32), ALU.subtract).then_inc(S["f_lo"], 1)

            for half in range(2):
                cols = slice(4 * half, 4 * half + 4)
                pool.wait_ge(S["f_sq"], 4 * half + 4)
                pool.tensor_scalar(row_ms[:, cols], row_ss[:, cols], 1.0 / D, NORM_EPS, ALU.mult, ALU.add).then_inc(S["f_ms"], 1)
                pool.wait_ge(S["f_ms"], half + 1)
                inverse_root(row_rstd[:, cols], row_ms[:, cols]).then_inc(S["f_rstd"], 1)


_INS = ["x", "positions", "attn_norm", "w_in", "diff_lam_q1", "diff_lam_k1", "diff_lam_q2", "diff_lam_k2", "diff_subln",
        "mla_q_norm", "mla_w_uq", "mla_kv_norm", "mla_w_ukv", "ret_gn_w", "ret_gn_b", "w_out", "ffn_norm", "w_gate",
        "w_up", "w_down", "final_norm"]
_OUTS = [((1, SEQ, D), "float32")]


def kernel(**inputs):
    import numpy as _np
    import concourse.bacc as _bacc
    from concourse import mybir as _mybir
    from concourse.bass_utils import run_bass_kernel_spmd as _run

    nc = _bacc.Bacc("TRN2", target_bir_lowering=False, num_devices=1)
    arrays, args = {}, []
    for name in _INS:
        a = _np.ascontiguousarray(inputs[name])
        arrays[f"in_{name}_dram"] = a
        args.append(nc.dram_tensor(f"in_{name}_dram", a.shape, _mybir.dt.from_np(a.dtype), kind="ExternalInput").ap())
    for i, (shape, dtype) in enumerate(_OUTS):
        dt = _mybir.dt.from_np(_np.dtype(dtype))
        args.append(nc.dram_tensor(f"out_{i}_dram", shape, dt, kind="ExternalOutput").ap())
    hybrid_block_kernel(nc, *args)
    r = _run(nc, [arrays], core_ids=[0])
    got = tuple(r.results[0][f"out_{i}_dram"] for i in range(len(_OUTS)))
    return got[0]
```

```python
import math
from contextlib import ExitStack

import numpy as np

import concourse.bass as bass
from concourse import mybir

F32 = mybir.dt.float32
F32R = mybir.dt.float32r
I32 = mybir.dt.int32
ALU = mybir.AluOpType
ACT = mybir.ActivationFunctionType
AX_X = mybir.AxisListType.X

P = 128
DEPTH = 2
SEQ = 1024
D = 1024
T = SEQ // P
KD = D // P
DESC = range(T - 1, -1, -1)

DIFF_HEADS, DIFF_DIM = 4, 64
MLA_HEADS, NOPE, ROPE, MLA_V = 4, 64, 32, 64
MLA_QK = NOPE + ROPE
Q_RANK, KV_RANK = 256, 128
RET_HEADS, RET_DIM = 4, 64
RET_PAIRS = RET_HEADS // 2
FFN = 2816
GROUP = 256
GROUPS = FFN // GROUP
GM = GROUP // P

DIFF_W = DIFF_HEADS * 2 * DIFF_DIM
RET_W = RET_HEADS * RET_DIM
COL_DQ, COL_DK, COL_DV = 0, DIFF_W, 2 * DIFF_W
COL_MLA = 3 * DIFF_W
MLA_COLS = Q_RANK + KV_RANK + ROPE
COL_RET = COL_MLA + MLA_COLS
MIX_MLA = DIFF_W
MIX_RET = DIFF_W + MLA_HEADS * MLA_V

NORM_EPS, SUBLN_EPS, GN_EPS = 1e-6, 1e-5, 1e-6
DIFF_SCALE = DIFF_DIM ** -0.5
MLA_SCALE = MLA_QK ** -0.5
NEG = -1e30

CH_DIFF, CH_MLA, CH_UKV, CH_RET, CH_OUT, CHUNKS = 0, 4, 5, 6, 8, 10
Z_MLA, Z_RET, Z_UNITS = 4 * T, 5 * T, 7 * T
ROPE_RET = 4 * T
ATT_UNITS = DIFF_HEADS * T + MLA_HEADS * T


def groups_of_four(t):
    return (t + 4) // 4


PT_RINGS = sum(groups_of_four(t) for t in range(T))
RING = 2 * KD + 4 * (T + PT_RINGS) + (T + 4 * (T + PT_RINGS)) + 2 * T + 2 * 2 * KD

PARTS = 4
V_SLOTS = T + 2


def diff_transposes(a):
    return [u for u in (a + T - 1,) if 0 <= u < DIFF_HEADS * T]


DIFF_STEPS = range(-T, DIFF_HEADS * T + 2)


def diff_rings():
    ring, after = 2 * KD, {}
    for a in DIFF_STEPS:
        if 0 <= a - 1 < DIFF_HEADS * T:
            ring += groups_of_four(T - 1 - (a - 1) % T)
        for u in diff_transposes(a):
            ring += 1
            after[u] = ring
    return after


PER = dict(
    params_in=16 * 8, ret_in=16 * 3, x_saved=16, x_back0=16, x_back1=16, mix_in=16,
    w_in0=16 * (3 + 3 + 1 + 4 + 4 + 1), w_in1=16 * (3 + 3 + 4 + 1), w_gain=1, w_hi=PARTS * CHUNKS, w_lo=CHUNKS,
    lam=5, n_sq=2 * T, n_ms=5, n_rstd=5, n_xn=2 * T, tr_done=RING, tr_hi=RING, tr_free=RING,
    z_done=Z_UNITS, z_free=Z_UNITS, rope_ab=6 * T, rope_sum=6 * T, v_hi=6 * T,
    s_done=2 * DIFF_HEADS * T + MLA_HEADS * T, s_max=2 * DIFF_HEADS * T + MLA_HEADS * T,
    s_exp=2 * DIFF_HEADS * T + MLA_HEADS * T,
    inv_sum=ATT_UNITS, lam_ratio=DIFF_HEADS * T, p_ready=DIFF_HEADS * T, pv_done=ATT_UNITS, o_free=ATT_UNITS,
    o_sq=DIFF_HEADS * T, o_ms=3 * DIFF_HEADS * T, o_rr=DIFF_HEADS * T, o_out=ATT_UNITS,
    mix_out0=8 * ATT_UNITS, mix_out1=8 * ATT_UNITS,
    m_sq=T, m_sq2=T, m_ms=2 * T, m_rstd=T, m_kab=T, m_krope=T, u_done=T, m_nope=T, m_vhi=T, m_qab=T, u_free=T,
    m_qrope=T, m_cn=T,
    r_vlo=2 * T, r_take=2 * T, r_xz=2 * T, r_kzhi=2 * T, r_kzlo=2 * T, ri_done=2 * T, r_at=2 * T, r_athi=2 * T, r_atlo=2 * T,
    ro_done=2 * T, rs_done=2 * (T - 1), r_st=2 * (T - 1), r_sthi=2 * (T - 1), r_stlo=2 * (T - 1),
    r_bn=2 * T, r_mv=2 * T, r_ms=2 * T, r_rstd=2 * T, r_on=2 * T, r_gw=2 * T, r_gb=2 * T, r_mx=2 * T,
    out_done=2 * T, out_add=2 * T,
    fg_in0=32 * GROUPS, fg_in1=32 * GROUPS, fd_in=16 * GROUPS, f_hi=3 * GROUPS, f_lo=3 * GROUPS,
    gu_done=4 * GROUPS, f_silu=4 * GROUPS, f_mul=4 * GROUPS, f_ahi=4 * GROUPS, f_act=4 * GROUPS,
    fd_done=2 * T * GROUPS, d_add=2 * T * GROUPS,
)
GU_CREDIT, D_CREDIT, ADD_CREDIT = 1, 1, 2 * T

C_IDENT, C_MASK, C_XZ, C_CD, C_INVF, C_LAM = 0, P, 2 * P, 2 * P + 8, 2 * P + 10, 2 * P + 58
C_COLS = C_LAM + 2 * DEPTH


def constants():
    c = np.zeros((P, C_COLS), np.float32)
    c[:, C_IDENT:C_IDENT + P] = np.eye(P)
    c[:, C_MASK:C_MASK + P] = np.triu(np.full((P, P), NEG), 1)
    log_gamma = np.log1p(-np.exp2(-5.0 - np.arange(RET_HEADS, dtype=np.float32))).astype(np.float32)
    pos = np.arange(P, dtype=np.float32)
    xi = np.exp((pos[:, None] + 1.0) * log_gamma[None, :])
    zeta = np.exp((P - 1.0 - pos)[:, None] * log_gamma[None, :]) * RET_DIM ** -0.5
    for p in range(RET_PAIRS):
        c[:, C_XZ + 4 * p:C_XZ + 4 * p + 2] = xi[:, 2 * p:2 * p + 2]
        c[:, C_XZ + 4 * p + 2:C_XZ + 4 * p + 4] = zeta[:, 2 * p:2 * p + 2]
        c[:64, C_CD + p] = np.exp(P * log_gamma[2 * p])
        c[64:, C_CD + p] = np.exp(P * log_gamma[2 * p + 1])
    for at, dim in ((0, DIFF_DIM), (32, ROPE)):
        freq = np.float32(1.0) / (np.float32(10000.0) ** (np.arange(0, dim, 2, dtype=np.float32) / np.float32(dim)))
        c[:, C_INVF + at:C_INVF + at + dim // 2] = freq
    for layer in range(DEPTH):
        init = 0.8 - 0.6 * math.exp(-0.3 * layer)
        c[:, C_LAM + 2 * layer:C_LAM + 2 * layer + 2] = (init, 1.0 - init)
    rel = pos[None, :] - pos[:, None]
    decay = np.where(rel[:, None, :] >= 0, np.exp(np.maximum(rel, 0.0)[:, None, :] * log_gamma[None, :, None]), 0.0)
    return c, (decay * RET_DIM ** -0.5).astype(np.float32).reshape(P, RET_HEADS * P)


def hybrid_block_kernel(nc, x, positions, attn_norm, w_in, diff_lam_q1, diff_lam_k1, diff_lam_q2, diff_lam_k2,
                        diff_subln, mla_q_norm, mla_w_uq, mla_kv_norm, mla_w_ukv, ret_gn_w, ret_gn_b, w_out,
                        ffn_norm, w_gate, w_up, w_down, final_norm, out):
    const_np, decay_np = constants()
    const_dram = nc.inline_tensor(const_np, name="const_table").ap()
    decay_dram = nc.inline_tensor(decay_np, name="decay_table").ap()
    mixed_dram = nc.dram_tensor("mixed_scratch", (SEQ, D), F32, kind="Internal").ap()
    x_dram = nc.dram_tensor("x_scratch", (SEQ, D), F32, kind="Internal").ap()

    base = 16512
    KB = 1024
    HT, WSLOT, XREG, EREG, MREG, CREG = 0, 64 * KB, 128 * KB, 160 * KB, 176 * KB, 200 * KB

    def sb(name, shape, dt, at):
        return nc.alloc_sbuf_tensor_at(name, shape, dt, offset=base + at)

    ht_hi = sb("ht_hi", [P, KD, SEQ], F32R, HT)
    ht_lo = sb("ht_lo", [P, KD, SEQ], F32R, HT + 32 * KB)

    def weight(name, shape, at):
        size = 4 * int(np.prod(shape[1:]))
        return (sb(name + "_hi", shape, F32R, at), sb(name + "_lo", shape, F32R, at + size),
                sb(name + "_raw", shape, F32, at + size))

    slots = [WSLOT, WSLOT + 32 * KB]
    w_diff = [weight(f"w_diff{i}", [P, KD, 3 * P], slots[i]) for i in range(2)]
    w_mla = weight("w_mla", [P, KD, MLA_COLS], slots[0])
    w_uq = weight("w_uq", [P, Q_RANK // P, MLA_HEADS * MLA_QK], slots[1])
    w_ukv = weight("w_ukv", [P, MLA_HEADS * (NOPE + MLA_V)], slots[1] + 8 * KB)
    w_ret = weight("w_ret", [P, KD, 4 * P], slots[0])
    w_o = [weight(f"w_o{i}", [P, KD, 512], slots[i]) for i in range(2)]
    w_gu = [weight(f"w_gu{m}", [P, 2, KD, P], slots[0] + 16 * KB * m) for m in range(2)]
    w_dn = weight("w_dn", [P, GM, D], slots[1])

    X = sb("X", [P, T, D], F32, XREG)
    mixed_rows = sb("mixed_rows", [P, T, D], F32, XREG)
    dq_hi = sb("dq_hi", [P, 2, SEQ], F32R, XREG)
    dq_lo = sb("dq_lo", [P, 2, SEQ], F32R, XREG + 8 * KB)
    dk = sb("dk", [P, 2, SEQ], F32R, XREG + 16 * KB)
    dv = [sb(f"dv{i}", [P, 2, P], F32R, XREG + (24 + i) * KB if i < T else MREG + (18 + i - T) * KB) for i in range(V_SLOTS)]
    mq_hi = sb("mq_hi", [MLA_QK, SEQ], F32R, XREG)
    mq_lo = sb("mq_lo", [MLA_QK, SEQ], F32R, XREG + 4 * KB)
    mk_hi = sb("mk_hi", [MLA_QK, SEQ], F32R, XREG + 8 * KB)
    mk_lo = sb("mk_lo", [MLA_QK, SEQ], F32R, XREG + 12 * KB)
    m_v = sb("m_v", [P, T, MLA_HEADS, 2, MLA_V], F32R, XREG + 16 * KB)

    pt_hi = sb("pt_hi", [P, T, P], F32R, EREG)
    pt_lo = sb("pt_lo", [P, T, P], F32R, EREG + 4 * KB)
    expo = [sb("expo0", [P, 2, SEQ], F32, EREG + 8 * KB), sb("expo1", [P, 2, SEQ], F32, MREG)]
    mexpo = [sb(f"mexpo{i}", [P, SEQ], F32, EREG + (8 + 4 * i) * KB) for i in range(2)]
    mpt_hi = [pt_hi, sb("mpt_hi1", [P, T, P], F32R, slots[1])]
    mpt_lo = [pt_lo, sb("mpt_lo1", [P, T, P], F32R, slots[1] + 4 * KB)]
    rope_a = [sb(f"rope_a{i}", [P, 4, 2, 32], F32, MREG + (8 + i) * KB) for i in range(2)]
    rope_b = [sb(f"rope_b{i}", [P, 4, 2, 32], F32, MREG + (10 + i) * KB) for i in range(2)]
    qk_rot = [sb(f"qk_rot{i}", [P, 4, 2, 64], F32, MREG + (12 + 2 * i) * KB) for i in range(2)]
    d_mx = [sb(f"d_mx{i}", [P, P], F32, MREG + 16 * KB + 512 * i) for i in range(2)]
    d_sum = [sb(f"d_sum{i}", [P, P], F32, MREG + 22 * KB + 512 * i) for i in range(2)]
    m_sum = [sb(f"m_sum{i}", [P, MLA_V], F32, slots[1] + 8 * KB + 256 * i) for i in range(2)]
    square_out = sb("square_out", [P, P], F32, MREG + 17 * KB)
    m_q = sb("m_q", [P, T, MLA_HEADS, MLA_QK], F32, MREG)
    m_k = sb("m_k", [P, T, MLA_HEADS, MLA_QK], F32, MREG + 12 * KB)
    m_z = [sb(f"m_z{u}", [P, MLA_COLS], F32, slots[1] + 16 * KB + 4 * MLA_COLS * u) for u in range(T)]
    cn = [sb(f"cn{i}", [P, 3, P], F32, EREG + 8 * KB * i) for i in range(2)]
    ct_hi = [sb(f"ct_hi{i}", [P, 3, P], F32R, EREG + 8 * KB * i + 1536) for i in range(2)]
    ct_lo = [sb(f"ct_lo{i}", [P, 3, P], F32R, EREG + 8 * KB * i + 3072) for i in range(2)]
    mk_a = sb("mk_a", [P, 2, 16], F32, EREG + 4608)
    mk_b = sb("mk_b", [P, 2, 16], F32, EREG + 4736)
    mq_a = sb("mq_a", [P, MLA_HEADS, 2, 16], F32, EREG + 5120)
    mq_b = sb("mq_b", [P, MLA_HEADS, 2, 16], F32, EREG + 5632)
    m_square = sb("m_square", [P, Q_RANK], F32, EREG + 6144)
    decay = sb("decay", [P, RET_PAIRS, 2 * P], F32, EREG)
    gn_w = sb("gn_w", [P, RET_W], F32, EREG + 2 * KB)
    gn_b = sb("gn_b", [P, RET_W], F32, EREG + 3 * KB)
    rt_hi = [sb(f"rt_hi{i}", [P, 3, P], F32R, HT + 12 * KB + 1536 * i) for i in range(3)]
    rt_lo = [sb(f"rt_lo{i}", [P, 3, P], F32R, HT + 17 * KB + 1536 * i) for i in range(3)]
    rk_hi = [sb(f"rk_hi{i}", [P, P], F32R, EREG + 10 * KB + 512 * i) for i in range(2)]
    rk_lo = [sb(f"rk_lo{i}", [P, P], F32R, EREG + 11 * KB + 512 * i) for i in range(2)]
    rv = [sb(f"rv{i}", [P, 2, 2, RET_DIM], F32R, HT + (22 + i) * KB) for i in range(5)]
    r_z = [sb(f"r_z{n}", [P, 4 * P], F32, slots[1] + (16 + 2 * n) * KB if n < T else
              slots[1] + (10 + 2 * (n - T)) * KB if n < T + 3 else MREG + 2 * (n - T - 3) * KB) for n in range(2 * T)]
    r_ab = [(sb(f"r_a{i}", [P, 4, 2, 32], F32, HT + (38 + 2 * i) * KB),
             sb(f"r_b{i}", [P, 4, 2, 32], F32, HT + (39 + 2 * i) * KB)) for i in range(3)]
    r_rot = [sb(f"r_rot{i}", [P, 4, 64], F32, HT + (32 + i) * KB) for i in range(3)]
    r_xzt = [sb(f"r_xzt{i}", [P, 4, 64], F32, HT + (35 + i) * KB) for i in range(3)]
    r_at = sb("r_at", [P, 2 * P], F32, MREG + 10 * KB)
    r_at_hi = [sb(f"r_at_hi{i}", [P, 2 * P], F32R, HT + (8 + i) * KB) for i in range(2)]
    r_at_lo = [sb(f"r_at_lo{i}", [P, 2 * P], F32R, HT + (10 + i) * KB) for i in range(2)]
    r_st = sb("r_st", [P, P], F32, MREG + 13 * KB)
    r_sum = [sb(f"r_sum{i}", [P, 2, RET_DIM], F32, MREG + 13 * KB + 512 + 512 * i) for i in range(2)]
    r_st2 = [sb(f"r_st2{i}", [P, 2, P], F32R, HT + (27 + i) * KB) for i in range(3)]
    r_gate = [sb(f"r_gate{i}", [P, P], F32, MREG + 17 * KB + 512 * i) for i in range(6)]
    r_norm = [sb(f"r_norm{i}", [P, P], F32, MREG + 20 * KB + 512 * i) for i in range(2)]
    r_mx = [sb(f"r_mx{i}", [P, P], F32, MREG + 21 * KB + 512 * i) for i in range(2)]
    rows, rows1 = sb("rows", [P, 4, D], F32, MREG), sb("rows1", [P, 4, D], F32, EREG)
    row_square = sb("row_square", [P, D], F32, MREG + 16 * KB)
    act_hi = sb("act_hi", [P, GM, SEQ], F32R, EREG)
    act_lo = sb("act_lo", [P, GM, SEQ], F32R, EREG + 8 * KB)
    f_gate = [sb(f"f_gate{i}", [P, 512], F32, MREG + 2 * i * KB) for i in range(2)]
    f_prod = [sb(f"f_prod{i}", [P, 512], F32, MREG + (4 + 2 * i) * KB) for i in range(2)]
    final_gain = sb("final_gain", [P, D], F32, MREG + 20 * KB)
    ang, turns, red, cosarg = (sb(n, [P, T, 48], F32, EREG + 1536 * i) for i, n in
                               enumerate(("ang", "turns", "red", "cosarg")))
    pos_int = sb("pos_int", [P, T], I32, EREG + 6144)
    pos_f = sb("pos_f", [P, T], F32, EREG + 6400)
    consts = sb("consts", [P, C_COLS], F32, EREG + 7 * KB)
    at = [CREG]

    def keep(name, shape, dt=F32):
        size = -(-4 * int(np.prod(shape[1:])) // 32) * 32
        at[0] += size
        return sb(name, shape, dt, at[0] - size)

    ident = keep("ident", [P, P])
    ident_r = keep("ident_r", [P, P], F32R)
    mask_r = keep("mask_r", [P, P], F32R)
    subln = keep("subln", [P, P])
    cos_d = keep("cos_d", [P, T, 32])
    sin_d = keep("sin_d", [P, T, 2, 32])
    cos_m = keep("cos_m", [P, T, 16])
    sin_m = keep("sin_m", [P, T, 2, 16])
    stats = keep("stats", [P, 148])
    taken = [0]

    def small(*shape):
        size = int(np.prod(shape))
        taken[0] += size
        cols = stats[:, taken[0] - size:taken[0]]
        if len(shape) == 1:
            return cols
        names = "abc"[:len(shape)]
        return cols.rearrange(f"p ({' '.join(names)}) -> p {' '.join(names)}", **dict(zip(names, shape)))

    xz = small(2, 4)
    cd = small(2)
    lam_const = small(2)
    m_mx = [keep(f"m_mx{i}", [P, MLA_V]) for i in range(2)]
    attn_gain = small(KD)
    ffn_gain = small(KD)
    q_gain = small(2)
    kv_gain = small(1)
    lam_sum = small(2)
    lam_exp = small(2)
    neg_lam = small(1)
    row_ss = small(T)
    row_ms = small(T)
    row_rstd = small(T)
    neg_max = small(2, 2)
    exp_sum = small(2, 2)
    inv_sum = small(4, 2)
    ratio = small(2)
    o_ss = small(2)
    o_ms = small(2)
    o_rs = small(2)
    o_rr = small(2)
    m_ss = small(2, 2)
    m_msq = small(2, 2)
    m_rs = small(2, 2)
    bn = small(2, 2, 6)
    mv = small(2, 2, 2)
    r_rs = small(2, 2)
    r_ms = small(2, 2)
    minus_half = small(4)
    assert taken[0] <= 148, taken[0]
    assert base + at[0] <= nc.sbuf_usable_end, at[0] - CREG
    lam_vec = sb("lam_vec", [P, 4, DIFF_DIM], F32, MREG + 20 * KB)
    lam_prod = sb("lam_prod", [P, DIFF_DIM], F32, MREG + 21 * KB)

    ctx = ExitStack()
    with ctx:
        ctx.enter_context(nc.allow_non_contiguous_dma(reason="columns of gains and positions, a few KB"))
        banks = ctx.enter_context(nc.psum_tensor("banks", [P, 8, 512], F32))
        S = {name: ctx.enter_context(nc.semaphore(name)) for name in PER}
        S |= {name: ctx.enter_context(nc.semaphore(name)) for name in
              ("passed", "const_in", "x_in0", "x_in1", "pos_in", "tab_dve", "tab_act", "ident_ok", "half_ok", "final_in", "f_sq", "f_ms", "f_rstd", "f_scaled", "y_pool", "y_dve",
                 "y_out0", "y_out1", "y_out2", "y_out3")}

        SCORE = [banks[:, 0:2, :].rearrange("p b n -> p (b n)"), banks[:, 2:4, :].rearrange("p b n -> p (b n)")]
        Z_BANK, O_BANK = 4, 7

        def z_bank(u):
            return O_BANK if u < T and u % 2 else Z_BANK

        TR_BANKS = (5, 6)
        NORM_BANKS = (4, 5, 6, 7)
        RET_INNER, RET_STATE, RET_OUT = (0, 1), 7, (2, 3)

        def tokens(t, n=1):
            return slice(t * P, (t + n) * P)

        def tile_of(unit):
            return T - 1 - unit % T

        DIFF_UNITS = DIFF_HEADS * T
        qk_ring = diff_rings()
        MLA_UNITS = MLA_HEADS * T
        MLA_STEPS = range(MLA_UNITS + 3)

        RET_UNITS = RET_PAIRS * T
        ret_unit_at = {(7 if n < T else 13) + n: n for n in range(RET_UNITS)}
        ROUND_RET = (0, 17)

        FINAL_POOL = 4

        def slot(chunk):
            return 0 if chunk == CH_RET + 1 else chunk % 2

        block = ctx.enter_context(nc.Block())

        @block.sync
        def _(sp):
            sp.dma_start(consts[:], const_dram).then_inc(S["const_in"], 16)
            sp.dma_start(ident[:], const_dram[:, C_IDENT:C_IDENT + P]).then_inc(S["const_in"], 16)
            sp.dma_start(xz[:], const_dram[:, C_XZ:C_XZ + 8]).then_inc(S["const_in"], 16)
            sp.dma_start(cd[:], const_dram[:, C_CD:C_CD + 2]).then_inc(S["const_in"], 16)
            sp.dma_start(pos_int[:], positions.rearrange("b (t p) -> p (b t)", p=P)).then_inc(S["pos_in"], 16)
            for half in range(2):
                tiles = slice(4 * half, 4 * half + 4)
                sp.dma_start(X[:, tiles, :], x[0].rearrange("(t p) d -> p t d", p=P)[:, tiles, :]).then_inc(S[f"x_in{half}"], 16)
            const2 = const_dram[:, C_LAM:C_LAM + 2 * DEPTH].rearrange("p (l c) -> l p c", l=DEPTH)
            mixed = mixed_dram.rearrange("(t p) d -> t p d", p=P)

            with sp.Fori(0, DEPTH) as L:

                def arrives(dst, src, name):
                    sp.dma_start(dst, src).then_inc(S[name], 16)

                arrives(attn_gain[:], attn_norm[L].rearrange("(k p) -> p k", p=P), "params_in")
                arrives(lam_const[:], const2[L], "params_in")
                for i, v in enumerate((diff_lam_q1, diff_lam_k1, diff_lam_q2, diff_lam_k2)):
                    arrives(lam_vec[:, i, :], v[L].partition_broadcast(P), "params_in")
                arrives(subln[:], diff_subln[L].partition_broadcast(P), "params_in")
                arrives(ffn_gain[:], ffn_norm[L].rearrange("(k p) -> p k", p=P), "params_in")

                def load_columns(chunk, w, starts, width):
                    src = w_in[L].rearrange("(k p) n -> p k n", p=P)
                    for i, start in enumerate(starts):
                        arrives(w[:, :, i * width:(i + 1) * width], src[:, :, start:start + width],
                                f"w_in{slot(chunk)}")

                def load_diff(h):
                    load_columns(h, w_diff[h % 2][2], [c + h * P for c in (COL_DQ, COL_DK, COL_DV)], P)

                def load_ret(p):
                    load_columns(CH_RET + p, w_ret[2], [COL_RET + i * RET_W + p * P for i in range(4)], P)

                def load_out(c):
                    arrives(w_o[c][2][:], w_out[L].rearrange("(k p) n -> p k n", p=P)[:, :, c * 512:(c + 1) * 512],
                            f"w_in{c}")

                sp.wait_ge(S["gu_done"], L * PER["gu_done"] + GU_CREDIT)
                load_diff(0)
                sp.wait_ge(S["fd_done"], L * PER["fd_done"] + D_CREDIT)
                load_diff(1)
                sp.wait_ge(S["x_in0"], 16)
                sp.wait_ge(S["x_in1"], 16)
                sp.wait_ge(S["d_add"], L * PER["d_add"] + ADD_CREDIT)
                arrives(x_dram.rearrange("(t p) d -> p t d", p=P), X[:], "x_saved")

                def next_chunk(h):
                    sp.wait_ge(S["z_done"], L * PER["z_done"] + T * (h + 1))
                    if h + 2 < DIFF_HEADS:
                        load_diff(h + 2)
                    elif h + 2 == CH_MLA:
                        arrives(w_mla[2][:], w_in[L].rearrange("(k p) n -> p k n", p=P)[:, :, COL_MLA:COL_MLA + MLA_COLS],
                                "w_in0")
                    elif h + 2 == CH_UKV:
                        arrives(q_gain[:], mla_q_norm[L].rearrange("(k p) -> p k", p=P), "w_in1")
                        arrives(w_uq[2][:], mla_w_uq[L].rearrange("(k p) n -> p k n", p=P), "w_in1")
                        arrives(kv_gain[:], mla_kv_norm[L].rearrange("(k p) -> p k", p=P), "w_in1")
                        arrives(w_ukv[2][:], mla_w_ukv[L], "w_in1")

                def store_mixed(ready, n, t, col, width, tile, unit):
                    sp.wait_ge(S[ready], L * PER[ready] + n)
                    arrives(mixed[t][:, col:col + width], tile, f"mix_out{unit % 2}")

                next_chunk(0)
                for h in range(DIFF_HEADS):
                    for t in DESC:
                        a = h * T + (T - 1 - t)
                        store_mixed("o_out", a + 1, t, h * P, P, d_mx[a % 2][:], a)
                        if t == 2 and h + 1 < DIFF_HEADS:
                            next_chunk(h + 1)
                sp.wait_ge(S["z_done"], L * PER["z_done"] + Z_MLA + T)
                load_ret(0)
                for h in range(MLA_HEADS):
                    for t in DESC:
                        a = DIFF_HEADS * T + h * T + (T - 1 - t)
                        store_mixed("o_out", a + 1, t, MIX_MLA + h * MLA_V, MLA_V, m_mx[a % 2][:], a)
                        if h * T + T - 1 - t == 9:
                            sp.wait_ge(S["z_done"], L * PER["z_done"] + Z_RET + T)
                            load_ret(1)
                        if h * T + T - 1 - t == 25:
                            sp.wait_ge(S["z_done"], L * PER["z_done"] + Z_UNITS)
                            load_out(0)
                sp.wait_ge(S["pv_done"], L * PER["pv_done"] + ATT_UNITS)
                arrives(decay[:], decay_dram.rearrange("p (a n) -> p a n", a=RET_PAIRS), "ret_in")
                arrives(gn_w[:], ret_gn_w[L].partition_broadcast(P), "ret_in")
                arrives(gn_b[:], ret_gn_b[L].partition_broadcast(P), "ret_in")
                sp.wait_ge(S["mix_out0"], L * PER["mix_out0"] + PER["mix_out0"])
                sp.wait_ge(S["mix_out1"], L * PER["mix_out1"] + PER["mix_out1"])
                arrives(mixed_rows[:, :, 0:MIX_RET], mixed_dram.rearrange("(t p) d -> p t d", p=P)[:, :, 0:MIX_RET], "mix_in")
                sp.wait_ge(S["v_hi"], L * PER["v_hi"] + ROPE_RET + T + 3)
                sp.wait_ge(S["r_vlo"], L * PER["r_vlo"] + T + 3)
                sp.wait_ge(S["rope_ab"], L * PER["rope_ab"] + ROPE_RET + T + 3)
                load_out(1)
                sp.wait_ge(S["x_saved"], L * PER["x_saved"] + 16)
                for half in range(2):
                    sp.wait_ge(S["tr_done"], L * PER["tr_done"] + RING - 2 * 2 * KD + (half + 1) * KD)
                    arrives(X[:, 4 * half:4 * half + 4, :], x_dram.rearrange("(t p) d -> p t d", p=P)[:, 4 * half:4 * half + 4, :],
                            f"x_back{half}")

                wgv = w_gate[L].rearrange("(k p) n -> p k n", p=P)
                wuv = w_up[L].rearrange("(k p) n -> p k n", p=P)
                wdv = w_down[L].rearrange("(g k p) n -> g p k n", p=P, k=GM)

                def load_gu(g, m):
                    arrives(w_gu[m][2][:, 0], wgv[:, :, bass.ds(g * GROUP + m * P, P)], f"fg_in{m}")
                    arrives(w_gu[m][2][:, 1], wuv[:, :, bass.ds(g * GROUP + m * P, P)], f"fg_in{m}")

                sp.wait_ge(S["out_done"], L * PER["out_done"] + T)
                load_gu(0, 0)
                load_gu(0, 1)
                sp.wait_ge(S["out_done"], L * PER["out_done"] + 2 * T)
                arrives(w_dn[2][:], wdv[0], "fd_in")
                with sp.Fori(1, GROUPS) as g:
                    for m in range(GM):
                        sp.wait_ge(S["gu_done"], L * PER["gu_done"] + g * 4 + (2 * (m + 1) - 4 + GU_CREDIT))
                        load_gu(g, m)
                    sp.wait_ge(S["fd_done"], L * PER["fd_done"] + g * 2 * T + D_CREDIT)
                    arrives(w_dn[2][:], wdv[g], "fd_in")

            sp.wait_ge(S["gu_done"], DEPTH * PER["gu_done"] + GU_CREDIT)
            sp.dma_start(final_gain[:], final_norm.partition_broadcast(P)).then_inc(S["final_in"], 16)
            for t in range(T):
                if t < FINAL_POOL:
                    sp.wait_ge(S["y_pool"], t + 1)
                else:
                    sp.wait_ge(S["y_dve"], t + 1 - FINAL_POOL)
                sp.dma_start(out[0].rearrange("(t p) d -> t p d", p=P)[t], X[:, t, :]).then_inc(S[f"y_out{t % 4}"], 16)
            for i in range(4):
                sp.wait_ge(S[f"y_out{i}"], 16 * T // 4)

        @block.tensor
        def _(pe):
            pe.wait_ge(S["const_in"], 64)
            pe.wait_ge(S["ident_ok"], 2)
            pe.sem_inc(S["gu_done"], GU_CREDIT)
            pe.sem_inc(S["fd_done"], D_CREDIT)

            def products(bank, pairs, first=True, last=True):
                mm = None
                for i, (lhsT, rhs) in enumerate(pairs):
                    mm = pe.matmul(bank, lhsT, rhs, start=first and i == 0, stop=last and i == len(pairs) - 1)
                return mm

            def split(a, b):
                return [(a[0], b[0]), (a[0], b[1]), (a[1], b[0])]

            with pe.Fori(0, DEPTH) as L:
                ring, freed = [0], [0]

                def ring_empty():
                    if ring[0] > freed[0]:
                        pe.wait_ge(S["tr_free"], L * PER["tr_free"] + ring[0])
                    freed[0] = ring[0]

                def take_ring(n_banks=2):
                    r = ring[0]
                    if r - n_banks + 1 > freed[0]:
                        pe.wait_ge(S["tr_free"], L * PER["tr_free"] + r - n_banks + 1)
                    ring[0] += 1
                    return banks[:, (TR_BANKS if n_banks == 2 else NORM_BANKS)[r % n_banks], :]

                def transpose_rows(tiles, ready, count, blocks=range(KD)):
                    pe.wait_ge(S[ready], L * PER[ready] + count)
                    for k in blocks:
                        bank = take_ring(4)
                        for j in range(4):
                            tr = pe.transpose(bank[:, tokens(j)], tiles[:, j, tokens(k)], ident[:])
                        tr.then_inc(S["tr_done"], 1)

                def project(u, t, chunk, w, n, parts=(0, 1)):
                    if 0 in parts:
                        pe.wait_ge(S["w_hi"], L * PER["w_hi"] + PARTS * (chunk + 1))
                        pe.wait_ge(S["w_lo"], L * PER["w_lo"] + chunk + 1)
                        if u > T:
                            pe.wait_ge(S["z_free"], L * PER["z_free"] + u)
                        elif u >= 2:
                            pe.wait_ge(S["z_free"], L * PER["z_free"] + u - 1)
                    bank = banks[:, z_bank(u), 0:n]
                    for part in parts:
                        pairs = [pair for k in range(part * KD // 2, (part + 1) * KD // 2) for pair in
                                 split((ht_hi[:, k, tokens(t)], ht_lo[:, k, tokens(t)]), (w[0][:, k, :], w[1][:, k, :]))]
                        mm = products(bank, pairs, first=part == 0, last=part == 1)
                    if 1 in parts:
                        mm.then_inc(S["z_done"], 1)

                transpose_rows(rows, "n_xn", 4)
                transpose_rows(rows1, "n_xn", 8)
                ring_empty()

                def diff_project(u, part):
                    if 0 <= u < DIFF_UNITS:
                        project(u, tile_of(u), u // T, w_diff[u // T % 2], 3 * P, (part,))
                    elif Z_MLA <= u < Z_MLA + T:
                        project(u, tile_of(u), CH_MLA, w_mla, MLA_COLS, (part,))

                def diff_transpose(u):
                    pe.wait_ge(S["rope_sum"], L * PER["rope_sum"] + u + 1)
                    bank = take_ring()
                    for v in range(4):
                        tr = pe.transpose(bank[:, tokens(v)], qk_rot[u % 2][:, v].rearrange("p c d -> p (c d)"), ident[:])
                    tr.then_inc(S["tr_done"], 1)
                    assert qk_ring[u] == ring[0]

                def diff_scores(a):
                    t = tile_of(a)
                    if a % T == 0:
                        pe.wait_ge(S["tr_free"], L * PER["tr_free"] + qk_ring[a + T - 1])
                    for m in range(2):
                        j = 2 * a + m
                        if j >= 2:
                            pe.wait_ge(S["s_exp"], L * PER["s_exp"] + j - 1)
                        for c in range(0, (t + 1) * P, 512):
                            n = min(512, (t + 1) * P - c)
                            diagonal = c + n == (t + 1) * P
                            keys = dk[:, m, c:c + n]
                            mm = products(SCORE[m][:, c:c + n], [(dq_hi[:, m, tokens(t)], keys), (dq_lo[:, m, tokens(t)], keys)],
                                          last=not diagonal)
                        mm = pe.matmul(SCORE[m][:, tokens(t)], ident_r[:], mask_r[:], start=False, stop=True)
                        mm.then_inc(S["s_done"], 1)

                def weighted(bank, hi, lo, v, width):
                    for kb, v_kb in enumerate(v):
                        pe.matmul(bank[:, 0:2 * width], hi[:, kb, :], v_kb.rearrange("p c d -> p (c d)"), start=kb == 0, stop=False)
                        mm = pe.matmul(bank[:, 0:width], lo[:, kb, :], v_kb[:, 0, :], start=False, stop=kb == len(v) - 1)
                    mm.then_inc(S["pv_done"], 1)

                def transpose_probs(tile, t):
                    for b in range(0, t + 1, 4):
                        bank = take_ring()
                        for kb in range(b, min(b + 4, t + 1)):
                            tr = pe.transpose(bank[:, tokens(kb - b)], tile[:, tokens(kb)], ident[:])
                        tr.then_inc(S["tr_done"], 1)

                def diff_probs(a):
                    if 0 <= a < DIFF_UNITS:
                        pe.wait_ge(S["p_ready"], L * PER["p_ready"] + a + 1)
                        transpose_probs(expo[a % 2][:, 0, :], tile_of(a))
                        p_ring[a] = ring[0]

                p_ring = {}

                def diff_output(a):
                    if not 0 <= a < DIFF_UNITS:
                        return
                    t = tile_of(a)
                    if a >= 1:
                        pe.wait_ge(S["o_free"], L * PER["o_free"] + a)
                    if p_ring[a] > freed[0]:
                        pe.wait_ge(S["tr_free"], L * PER["tr_free"] + p_ring[a])
                        freed[0] = p_ring[a]
                    weighted(banks[:, O_BANK, :], pt_hi, pt_lo,
                             [dv[(a // T * T + T - 1 - kb) % V_SLOTS][:] for kb in range(t + 1)], P)

                for a in DIFF_STEPS:
                    if 0 <= a < DIFF_UNITS and a % T:
                        diff_scores(a)
                    diff_project(a + T, 0)
                    diff_probs(a - 1)
                    if a % T:
                        diff_project(a + T, 1)
                    for u in diff_transposes(a):
                        diff_transpose(u)
                    if a % T == 0:
                        diff_project(a + T, 1)
                    if a >= T:
                        pe.wait_ge(S["z_free"], L * PER["z_free"] + min(DIFF_UNITS, a + T - 1))
                    diff_output(a - 1)
                    if a % T == 0 and 0 <= a < DIFF_UNITS:
                        diff_scores(a)

                def mla_transpose_latents(u):
                    pe.wait_ge(S["m_cn"], L * PER["m_cn"] + u + 1)
                    bank = take_ring()
                    for b in range(3):
                        tr = pe.transpose(bank[:, tokens(b)], cn[u % 2][:, b, :], ident[:])
                    tr.then_inc(S["tr_done"], 1)
                    ct_ring[u] = ring[0]

                ct_ring = {}

                def mla_up(u):
                    pe.wait_ge(S["w_hi"], L * PER["w_hi"] + CH_UKV + 1)
                    pe.wait_ge(S["w_lo"], L * PER["w_lo"] + CH_UKV + 1)
                    if u >= 2:
                        pe.wait_ge(S["u_free"], L * PER["u_free"] + u - 1)
                        pe.wait_ge(S["m_nope"], L * PER["m_nope"] + u - 1)
                    if u == 0:
                        pe.wait_ge(S["s_exp"], L * PER["s_exp"] + 2 * DIFF_HEADS * T)
                    pe.wait_ge(S["tr_free"], L * PER["tr_free"] + ct_ring[u])
                    hi, lo = ct_hi[u % 2], ct_lo[u % 2]
                    pairs = [pair for k in range(2) for pair in
                             split((hi[:, k, :], lo[:, k, :]), (w_uq[0][:, k, :], w_uq[1][:, k, :]))]
                    products(banks[:, 2 * (u % 2), 0:MLA_HEADS * MLA_QK], pairs)
                    products(banks[:, 2 * (u % 2) + 1, :], split((hi[:, 2, :], lo[:, 2, :]), (w_ukv[0][:], w_ukv[1][:])))\
                        .then_inc(S["u_done"], 1)

                def mla_transpose(u):
                    h, t = u // T, tile_of(u)
                    if h == 0:
                        pe.wait_ge(S["m_qrope"], L * PER["m_qrope"] + u + 1)
                        pe.wait_ge(S["m_krope"], L * PER["m_krope"] + u + 1)
                        pe.wait_ge(S["m_nope"], L * PER["m_nope"] + u + 1)
                    bank = take_ring()
                    pe.transpose(bank[0:MLA_QK, 0:P], m_q[:, t, h, :], ident[:])
                    pe.transpose(bank[0:MLA_QK, P:2 * P], m_k[:, t, h, :], ident[:]).then_inc(S["tr_done"], 1)
                    mqk_ring[u] = ring[0]

                mqk_ring, mp_ring = {}, {}

                def mla_scores(a):
                    t = tile_of(a)
                    j = 2 * DIFF_UNITS + a
                    if a % T == 0:
                        pe.wait_ge(S["tr_free"], L * PER["tr_free"] + mqk_ring[a + T - 1])
                    pe.wait_ge(S["s_exp"], L * PER["s_exp"] + j - 1)
                    for c in range(0, (t + 1) * P, 512):
                        n = min(512, (t + 1) * P - c)
                        products(SCORE[j % 2][:, c:c + n],
                                 split((mq_hi[:, tokens(t)], mq_lo[:, tokens(t)]), (mk_hi[:, c:c + n], mk_lo[:, c:c + n])),
                                 last=c + n != (t + 1) * P)
                    pe.matmul(SCORE[j % 2][:, tokens(t)], ident_r[:], mask_r[:], start=False, stop=True)\
                        .then_inc(S["s_done"], 1)

                def mla_probs(a):
                    if 0 <= a < MLA_UNITS:
                        pe.wait_ge(S["s_exp"], L * PER["s_exp"] + 2 * DIFF_UNITS + a + 1)
                        transpose_probs(mexpo[a % 2], tile_of(a))
                        mp_ring[a] = ring[0]

                def mla_output(a):
                    if not 0 <= a < MLA_UNITS:
                        return
                    h, t = a // T, tile_of(a)
                    pe.wait_ge(S["o_free"], L * PER["o_free"] + DIFF_UNITS + a)
                    if mp_ring[a] > freed[0]:
                        pe.wait_ge(S["tr_free"], L * PER["tr_free"] + mp_ring[a])
                        freed[0] = mp_ring[a]
                    weighted(banks[:, O_BANK, :], mpt_hi[a % 2], mpt_lo[a % 2], [m_v[:, kb, h] for kb in range(t + 1)], MLA_V)

                for u in range(T + 4):
                    if u >= 4:
                        mla_transpose(u - 4)
                    if 1 <= u <= T:
                        mla_transpose_latents(u - 1)
                    if 2 <= u < T + 2:
                        mla_up(u - 2)
                pe.wait_ge(S["u_free"], L * PER["u_free"] + T)
                pe.wait_ge(S["m_nope"], L * PER["m_nope"] + T)
                def ret_project(a, part):
                    if a in ret_unit_at:
                        n = ret_unit_at[a]
                        project(Z_RET + n, n % T, CH_RET + n // T, w_ret, 4 * P, (part,))

                for a in MLA_STEPS:
                    if a < MLA_UNITS and a % T:
                        mla_scores(a)
                    ret_project(a, 0)
                    mla_probs(a - 1)
                    ret_project(a, 1)
                    mla_output(a - 2)
                    if a < MLA_UNITS and a % T == 0:
                        mla_scores(a)
                    if a + T < MLA_UNITS:
                        mla_transpose(a + T)

                def ret_transpose(p, t):
                    n = p * T + t
                    pe.wait_ge(S["r_xz"], L * PER["r_xz"] + n + 1)
                    bank = take_ring()
                    pe.transpose(bank[:, tokens(0)], r_rot[n % 3][:, 0:2, :].rearrange("p a d -> p (a d)"), ident[:])
                    pe.transpose(bank[:, tokens(1)], r_rot[n % 3][:, 2:4, :].rearrange("p a d -> p (a d)"), ident[:])
                    pe.transpose(bank[:, tokens(2)], r_xzt[n % 3][:, 0:2, :].rearrange("p a d -> p (a d)"), ident[:])\
                        .then_inc(S["tr_done"], 1)
                    ret_ready[n] = ring[0]

                ret_ready = {}

                def ret_inner(p, t):
                    n = p * T + t
                    pe.wait_ge(S["tr_free"], L * PER["tr_free"] + ret_ready[n])
                    if n >= 1:
                        pe.wait_ge(S["r_at"], L * PER["r_at"] + n)
                    hi, lo = rt_hi[n % 3], rt_lo[n % 3]
                    for j in range(2):
                        at_ = slice(64 * j, 64 * j + 64)
                        mm = products(banks[:, RET_INNER[j], 0:P], split((hi[at_, 1, :], lo[at_, 1, :]), (hi[at_, 0, :], lo[at_, 0, :])))
                    mm.then_inc(S["ri_done"], 1)
                    if t < T - 1:
                        n_s = p * (T - 1) + t
                        pe.wait_ge(S["r_kzhi"], L * PER["r_kzhi"] + n + 1)
                        pe.wait_ge(S["r_kzlo"], L * PER["r_kzlo"] + n + 1)
                        pe.wait_ge(S["r_vlo"], L * PER["r_vlo"] + n + 1)
                        if n_s >= 1:
                            pe.wait_ge(S["r_st"], L * PER["r_st"] + n_s)
                        products(banks[:, RET_STATE, 0:P], split((rk_hi[n % 2][:], rk_lo[n % 2][:]), (rv[n % 5][:, :, 0, :], rv[n % 5][:, :, 1, :])))\
                            .then_inc(S["rs_done"], 1)

                def ret_output(p, t):
                    n = p * T + t
                    pe.wait_ge(S["r_athi"], L * PER["r_athi"] + n + 1)
                    pe.wait_ge(S["r_atlo"], L * PER["r_atlo"] + n + 1)
                    pe.wait_ge(S["r_vlo"], L * PER["r_vlo"] + n + 1)
                    if n >= 1:
                        pe.wait_ge(S["r_take"], L * PER["r_take"] + n)
                    if t >= 1:
                        pe.wait_ge(S["r_sthi"], L * PER["r_sthi"] + p * (T - 1) + t)
                        pe.wait_ge(S["r_stlo"], L * PER["r_stlo"] + p * (T - 1) + t)
                    for j in range(2):
                        at_ = slice(64 * j, 64 * j + 64)
                        operands = [(r_at_hi[n % 2][:, tokens(j)], r_at_lo[n % 2][:, tokens(j)], rv[n % 5][:, j])]
                        if t >= 1:
                            operands.append((rt_hi[n % 3][at_, 2, :], rt_lo[n % 3][at_, 2, :], r_st2[(p * (T - 1) + t - 1) % 3][at_, :, at_]))
                        for i, (hi, lo, sides) in enumerate(operands):
                            pe.matmul(banks[:, RET_OUT[j], 0:P].rearrange("p (c d) -> p c d", c=2), hi, sides, start=i == 0, stop=False)
                            mm = pe.matmul(banks[:, RET_OUT[j], 0:64], lo, sides[:, 0, :], start=False, stop=i == len(operands) - 1)
                    mm.then_inc(S["ro_done"], 1)

                pe.wait_ge(S["s_exp"], L * PER["s_exp"] + PER["s_exp"])
                pe.wait_ge(S["o_free"], L * PER["o_free"] + PER["o_free"])
                for n in range(1, RET_UNITS + 3):
                    if n <= RET_UNITS:
                        ret_transpose((n - 1) // T, (n - 1) % T)
                    if 2 <= n < RET_UNITS + 2:
                        ret_inner((n - 2) // T, (n - 2) % T)
                    if n >= 3:
                        ret_output((n - 3) // T, (n - 3) % T)

                pe.wait_ge(S["z_free"], L * PER["z_free"] + Z_UNITS)
                ring_empty()
                pe.wait_ge(S["mix_in"], L * PER["mix_in"] + 16)
                transpose_rows(mixed_rows[:, 0:4, :], "r_mx", T + 4)
                transpose_rows(mixed_rows[:, 4:8, :], "r_mx", 2 * T)
                ring_empty()
                pe.wait_ge(S["r_take"], L * PER["r_take"] + 2 * T)
                for c in range(2):
                    pe.wait_ge(S["w_hi"], L * PER["w_hi"] + CH_OUT + c + 1)
                    pe.wait_ge(S["w_lo"], L * PER["w_lo"] + CH_OUT + c + 1)
                    for t in range(T):
                        q = c * T + t
                        if q >= 4:
                            pe.wait_ge(S["out_add"], L * PER["out_add"] + q - 3)
                        pairs = [pair for k in range(KD) for pair in
                                 split((ht_hi[:, k, tokens(t)], ht_lo[:, k, tokens(t)]), (w_o[c][0][:, k, :], w_o[c][1][:, k, :]))]
                        products(banks[:, q % 4, :], pairs).then_inc(S["out_done"], 1)
                        if q in (2 * T - 3, 2 * T - 2):
                            transpose_rows(rows, "n_xn", T + 4, range(4) if q == 2 * T - 3 else range(4, KD))
                transpose_rows(rows1, "n_xn", 2 * T)
                assert ring[0] == RING
                pe.wait_ge(S["tr_free"], L * PER["tr_free"] + RING)
                pe.wait_ge(S["out_add"], L * PER["out_add"] + 2 * T)
                pe.sem_inc(S["passed"], 1)

                with pe.Fori(0, GROUPS) as g:
                    for m in range(GM):
                        pe.wait_ge(S["f_hi"], L * PER["f_hi"] + g * 3 + (m + 1))
                        pe.wait_ge(S["f_lo"], L * PER["f_lo"] + g * 3 + (m + 1))
                        for half in range(2):
                            v = 2 * m + half
                            if v >= 2:
                                pe.wait_ge(S["f_mul"], L * PER["f_mul"] + g * 4 + (v - 1))
                            for gate_or_up in range(2):
                                pairs = []
                                for k in range(KD):
                                    w = (w_gu[m][0][:, gate_or_up, k, :], w_gu[m][1][:, gate_or_up, k, :])
                                    h_ = (ht_hi[:, k, tokens(4 * half, 4)], ht_lo[:, k, tokens(4 * half, 4)])
                                    pairs += split(w, h_)
                                mm = products(banks[:, 2 * (v % 2) + gate_or_up, :], pairs)
                            mm.then_inc(S["gu_done"], 1)
                    pe.wait_ge(S["f_hi"], L * PER["f_hi"] + g * 3 + 3)
                    pe.wait_ge(S["f_lo"], L * PER["f_lo"] + g * 3 + 3)
                    for t in range(T):
                        if t % 4 == 0:
                            pe.wait_ge(S["f_act"], L * PER["f_act"] + g * 4 + (3 + t // 4))
                        for c in range(2):
                            q = 2 * t + c
                            pe.wait_ge(S["d_add"], L * PER["d_add"] + g * 2 * T + (q - 3 + ADD_CREDIT))
                            pairs = [pair for m in range(GM) for pair in
                                     split((act_hi[:, m, tokens(t)], act_lo[:, m, tokens(t)]),
                                           (w_dn[0][:, m, c * 512:(c + 1) * 512], w_dn[1][:, m, c * 512:(c + 1) * 512]))]
                            products(banks[:, 4 + q % 4, :], pairs).then_inc(S["fd_done"], 1)

        @block.scalar
        def _(act):
            act.wait_ge(S["tab_dve"], 11)
            act.activation(sin_d[:, :, 1, :], red[:, :, 0:32], ACT.Sin)
            act.activation(sin_d[:, :, 0, :], red[:, :, 0:32], ACT.Sin, scale=-1.0)
            act.activation(sin_m[:, :, 1, :], red[:, :, 32:48], ACT.Sin)
            act.activation(sin_m[:, :, 0, :], red[:, :, 32:48], ACT.Sin, scale=-1.0)
            act.activation(cos_d[:], cosarg[:, :, 0:32], ACT.Sin)
            act.activation(cos_m[:], cosarg[:, :, 32:48], ACT.Sin).then_inc(S["tab_act"], 1)

            with act.Fori(0, DEPTH) as L:
                ring = [0]

                def round_ring():
                    ring[0] += 1
                    act.wait_ge(S["tr_done"], L * PER["tr_done"] + ring[0])
                    return ring[0] - 1

                def round_weights(chunk, n_in, parts, whole=PARTS):
                    act.wait_ge(S[f"w_in{slot(chunk)}"], L * PER[f"w_in{slot(chunk)}"] + n_in)
                    for hi, raw in parts:
                        act.activation(hi, raw, ACT.Copy).then_inc(S["w_hi"], PARTS // whole)

                def square_rows(norm, t, ready, n):
                    act.wait_ge(S[ready], L * PER[ready] + n)
                    if norm * T + t:
                        act.wait_ge(S["n_sq"], L * PER["n_sq"] + norm * T + t)
                    act.activation(row_square[:], X[:, t, :], ACT.Square, accum_out=row_ss[:, t:t + 1])\
                        .then_inc(S["n_sq"], 1)

                def high_rows(half, gain, blocks=range(KD)):
                    for k in blocks:
                        r = round_ring()
                        act.activation(ht_hi[:, k, tokens(4 * half, 4)], banks[:, NORM_BANKS[r % 4], :], ACT.Copy,
                                       scale=gain[:, k:k + 1] if gain is not None else 1.0).then_inc(S["tr_hi"], 1)

                def weights(chunk, parts=range(PARTS)):
                    if chunk < CH_MLA:
                        w, n = w_diff[chunk % 2], 3 * (chunk // 2 + 1)
                    elif chunk == CH_MLA:
                        w, n = w_mla, 7
                    elif chunk == CH_UKV:
                        act.wait_ge(S["w_gain"], L * PER["w_gain"] + 1)
                        return round_weights(chunk, 16 * 10, [(w_uq[0][:], w_uq[2][:]), (w_ukv[0][:], w_ukv[2][:])], 2)
                    elif chunk < CH_OUT:
                        w, n = w_ret, (11, 15)[chunk % 2]
                    else:
                        w, n = w_o[chunk % 2], (16, 11)[chunk % 2]
                    step = KD // PARTS
                    round_weights(chunk, 16 * n, [(w[0][:, i * step:(i + 1) * step, :], w[2][:, i * step:(i + 1) * step, :])
                                                  for i in parts])

                for t in range(T):
                    if t % 4 == 0:
                        act.wait_ge(S[f"x_in{t // 4}"], 16)
                    square_rows(0, t, "d_add", 2 * (t + 1))
                act.wait_ge(S["params_in"], L * PER["params_in"] + PER["params_in"])
                high_rows(0, attn_gain)
                weights(0)
                high_rows(1, attn_gain)
                act.wait_ge(S["lam"], L * PER["lam"] + 2)
                act.activation(lam_exp[:], lam_sum[:], ACT.Exp).then_inc(S["lam"], 1)

                def diff_v(u):
                    if Z_MLA <= u < Z_MLA + T:
                        act.wait_ge(S["z_done"], L * PER["z_done"] + u + 1)
                        act.activation(m_z[u - Z_MLA][:], banks[:, z_bank(u), 0:MLA_COLS], ACT.Copy).then_inc(S["z_free"], 1)
                    if 0 <= u < DIFF_UNITS:
                        act.wait_ge(S["z_done"], L * PER["z_done"] + u + 1)
                        if u >= V_SLOTS:
                            act.wait_ge(S["pv_done"], L * PER["pv_done"] + u - V_SLOTS + 1)
                        act.activation(dv[u % V_SLOTS][:, 0, :], banks[:, z_bank(u), 2 * P:3 * P], ACT.Copy).then_inc(S["v_hi"], 1)

                def diff_qk(u):
                    t = tile_of(u)
                    r = round_ring()
                    bank = banks[:, TR_BANKS[r % 2], :].rearrange("p (a m n) -> p a m n", a=2, m=2)
                    act.activation(dq_hi[:, :, tokens(t)], bank[:, 0], ACT.Copy, scale=DIFF_SCALE)
                    act.activation(dk[:, :, tokens(t)], bank[:, 1], ACT.Copy).then_inc(S["tr_hi"], 1)

                def exponentials(j, dst, a, m, t):
                    act.wait_ge(S["s_max"], L * PER["s_max"] + j + 1)
                    act.activation(dst, SCORE[j % 2][:, 0:(t + 1) * P], ACT.Exp, bias=neg_max[:, a % 2, m:m + 1],
                                   accum_out=exp_sum[:, a % 2, m:m + 1]).then_inc(S["s_exp"], 1)

                def high_probs(a, t, hi=pt_hi, behind=0):
                    for b in range(0, t + 1, 4):
                        r = round_ring()
                        n = min(4, t + 1 - b)
                        if a >= 1:
                            act.wait_ge(S["pv_done"], L * PER["pv_done"] + a - behind)
                        act.activation(hi[:, b:b + n, :], banks[:, TR_BANKS[r % 2], 0:n * P].rearrange("p (b n) -> p b n", n=P),
                                       ACT.Copy).then_inc(S["tr_hi"], 1)

                def diff_square(a):
                    if not 0 <= a < DIFF_UNITS:
                        return
                    act.wait_ge(S["o_free"], L * PER["o_free"] + a + 1)
                    if a >= 1:
                        act.wait_ge(S["o_sq"], L * PER["o_sq"] + a)
                    act.activation(square_out[:], d_sum[a % 2][:], ACT.Square, scale=inv_sum[:, a % 4, 0:1],
                                   accum_out=o_ss[:, a % 2:a % 2 + 1]).then_inc(S["o_sq"], 1)

                def diff_exponentials(a):
                    if 0 <= a < DIFF_UNITS:
                        for m in range(2):
                            if a >= 2:
                                act.wait_ge(S["pv_done"], L * PER["pv_done"] + a - 1)
                            exponentials(2 * a + m, expo[a % 2][:, m, 0:(tile_of(a) + 1) * P], a, m, tile_of(a))

                act.wait_ge(S["x_saved"], L * PER["x_saved"] + 16)
                for a in DIFF_STEPS:
                    if 0 <= a - 1 < DIFF_UNITS:
                        high_probs(a - 1, tile_of(a - 1))
                    if a % T:
                        diff_exponentials(a)
                        diff_v(a + T)
                    for u in diff_transposes(a):
                        diff_qk(u)
                    if a % T == 0:
                        diff_v(a + T)
                    diff_square(a - 2)
                    if a % T == 0:
                        diff_exponentials(a)
                    if a < DIFF_UNITS and 3 <= a % T < 3 + PARTS:
                        if a // T + 2 < CH_UKV:
                            weights(a // T + 2, [a % T - 3])
                        elif a % T == 3:
                            weights(CH_UKV)

                def mla_squares(u):
                    z = m_z[u][:]
                    if u == 0:
                        act.wait_ge(S["z_free"], L * PER["z_free"] + Z_MLA + T)
                        act.wait_ge(S["pv_done"], L * PER["pv_done"] + DIFF_HEADS * T)
                    else:
                        act.wait_ge(S["m_sq"], L * PER["m_sq"] + u)
                    act.activation(m_square[:], z[:, 0:Q_RANK], ACT.Square, accum_out=m_ss[:, u % 2, 0:1]).then_inc(S["m_sq2"], 1)
                    act.wait_ge(S["m_sq2"], L * PER["m_sq2"] + u + 1)
                    act.activation(m_square[:, 0:KV_RANK], z[:, Q_RANK:Q_RANK + KV_RANK], ACT.Square,
                                   accum_out=m_ss[:, u % 2, 1:2]).then_inc(S["m_sq"], 1)

                def mla_high(u):
                    r = round_ring()
                    if u >= 2:
                        act.wait_ge(S["u_done"], L * PER["u_done"] + u - 1)
                    act.activation(ct_hi[u % 2][:].rearrange("p b n -> p (b n)"), banks[:, TR_BANKS[r % 2], 0:3 * P], ACT.Copy).then_inc(S["tr_hi"], 1)

                def mla_up(u):
                    t = tile_of(u)
                    act.wait_ge(S["u_done"], L * PER["u_done"] + u + 1)
                    if u == 0:
                        act.wait_ge(S["mix_out0"], L * PER["mix_out0"] + 16 * DIFF_HEADS * T // 2)
                        act.wait_ge(S["mix_out1"], L * PER["mix_out1"] + 16 * DIFF_HEADS * T // 2)
                    qb = banks[:, 2 * (u % 2), 0:MLA_HEADS * MLA_QK].rearrange("p (h d) -> p h d", h=MLA_HEADS)
                    kvb = banks[:, 2 * (u % 2) + 1, :].rearrange("p (h d) -> p h d", h=MLA_HEADS)
                    act.activation(m_v[:, t, :, 0, :], kvb[:, :, NOPE:], ACT.Copy).then_inc(S["m_vhi"], 1)
                    act.activation(m_q[:, t, :, 0:NOPE], qb[:, :, 0:NOPE], ACT.Copy)
                    act.activation(m_k[:, t, :, 0:NOPE], kvb[:, :, 0:NOPE], ACT.Copy).then_inc(S["m_nope"], 1)

                def mla_qk(u):
                    t = tile_of(u)
                    r = round_ring()
                    bank = banks[0:MLA_QK, TR_BANKS[r % 2], :]
                    act.activation(mq_hi[:, tokens(t)], bank[:, 0:P], ACT.Copy, scale=MLA_SCALE)
                    act.activation(mk_hi[:, tokens(t)], bank[:, P:2 * P], ACT.Copy).then_inc(S["tr_hi"], 1)

                for u in range(T + 4):
                    if u < T:
                        mla_squares(u)
                    if u >= 4:
                        mla_qk(u - 4)
                    if 1 <= u <= T:
                        mla_high(u - 1)
                    if 2 <= u < T + 2:
                        mla_up(u - 2)
                def ret_gate_and_v(n):
                    if n >= 6:
                        act.wait_ge(S["r_mx"], L * PER["r_mx"] + n - 5)
                    if n >= 5:
                        act.wait_ge(S["ro_done"], L * PER["ro_done"] + n - 4)
                    if n == 0:
                        act.wait_ge(S["z_free"], L * PER["z_free"] + Z_UNITS)
                    act.activation(rv[n % 5][:, :, 0, :], r_z[n][:, 2 * P:3 * P].rearrange("p (j d) -> p j d", j=2), ACT.Copy).then_inc(S["v_hi"], 1)
                    act.activation(r_gate[n % 6][:], r_z[n][:, 3 * P:4 * P], ACT.Silu)

                def ret_scaled(n):
                    act.wait_ge(S["rope_sum"], L * PER["rope_sum"] + ROPE_RET + n + 1)
                    if n >= 3:
                        act.wait_ge(S["tr_done"], L * PER["tr_done"] + ret_ring + n - 2)
                        act.wait_ge(S["r_kzlo"], L * PER["r_kzlo"] + n - 2)
                    for i in range(4):
                        st = act.activation(r_xzt[n % 3][:, i, :], r_rot[n % 3][:, i, :], ACT.Copy, scale=xz[:, n // T, i:i + 1])
                    st.then_inc(S["r_xz"], 1)

                ret_ring = RING - 2 * 2 * KD - 2 * T

                def ret_high_k(n):
                    act.wait_ge(S["r_xz"], L * PER["r_xz"] + n + 1)
                    if n >= 2:
                        act.wait_ge(S["ri_done"], L * PER["ri_done"] + n - 1)
                        if rs_count(n - 1):
                            act.wait_ge(S["rs_done"], L * PER["rs_done"] + rs_count(n - 1))
                    act.activation(rk_hi[n % 2][:], r_xzt[n % 3][:, 2:4, :].rearrange("p a d -> p (a d)"), ACT.Copy)\
                        .then_inc(S["r_kzhi"], 1)

                def rs_count(n):
                    return n - n // T

                def ret_high(n):
                    r = round_ring()
                    if n >= 3:
                        act.wait_ge(S["ro_done"], L * PER["ro_done"] + n - 2)
                    act.activation(rt_hi[n % 3][:].rearrange("p b n -> p (b n)"), banks[:, TR_BANKS[r % 2], 0:3 * P], ACT.Copy)\
                        .then_inc(S["tr_hi"], 1)

                def ret_inner(n):
                    act.wait_ge(S["r_at"], L * PER["r_at"] + n + 1)
                    if n >= 2:
                        act.wait_ge(S["ro_done"], L * PER["ro_done"] + n - 1)
                    act.activation(r_at_hi[n % 2][:], r_at[:], ACT.Copy).then_inc(S["r_athi"], 1)
                    if n % T < T - 1:
                        i = rs_count(n)
                        act.wait_ge(S["r_st"], L * PER["r_st"] + i + 1)
                        act.activation(r_st2[i % 3][:, 0, :], r_st[:], ACT.Copy).then_inc(S["r_sthi"], 1)

                for a in MLA_STEPS:
                    if 0 <= a - 1 < MLA_UNITS:
                        high_probs(DIFF_UNITS + a - 1, tile_of(a - 1), mpt_hi[(a - 1) % 2], 1)
                    if 0 <= a < MLA_UNITS:
                        exponentials(2 * DIFF_UNITS + a, mexpo[a % 2][:, 0:(tile_of(a) + 1) * P], a, 0, tile_of(a))
                    if a in ret_unit_at:
                        n = ret_unit_at[a]
                        act.wait_ge(S["z_done"], L * PER["z_done"] + Z_RET + n + 1)
                        act.activation(r_z[n][:], banks[:, Z_BANK, :], ACT.Copy).then_inc(S["z_free"], 1)
                    if a + T < MLA_UNITS:
                        mla_qk(a + T)
                    for p in range(RET_PAIRS):
                        if 0 <= a - ROUND_RET[p] < PARTS:
                            weights(CH_RET + p, [a - ROUND_RET[p]])
                    if a > MLA_UNITS:
                        n = a - MLA_UNITS - 1
                        ret_gate_and_v(n)
                        ret_scaled(n)

                for n in range(1, RET_UNITS + 2):
                    if 1 <= n <= RET_UNITS:
                        ret_high_k(n - 1)
                        ret_high(n - 1)
                    if n >= 2:
                        ret_inner(n - 2)
                    if n + 1 < RET_UNITS:
                        ret_gate_and_v(n + 1)
                        ret_scaled(n + 1)
                    if 2 <= n < 2 + PARTS:
                        weights(CH_OUT, [n - 2])
                weights(CH_OUT + 1)

                high_rows(0, None)
                high_rows(1, None)
                for m in range(GM):
                    act.wait_ge(S[f"fg_in{m}"], L * PER[f"fg_in{m}"] + 32)
                    act.activation(w_gu[m][0][:], w_gu[m][2][:], ACT.Copy).then_inc(S["f_hi"], 1)
                for t in range(T):
                    square_rows(1, t, "out_add", T + t + 1)
                    if t in (T - 3, T - 2):
                        high_rows(0, ffn_gain, range(4) if t == T - 3 else range(4, KD))
                high_rows(1, ffn_gain)

                def activations(g):
                    act.wait_ge(S["fd_in"], L * PER["fd_in"] + g * 16 + 16)
                    act.activation(w_dn[0][:], w_dn[2][:], ACT.Copy).then_inc(S["f_hi"], 1)
                    for v in range(4):
                        m, half = v // 2, v % 2
                        act.wait_ge(S["gu_done"], L * PER["gu_done"] + g * 4 + (v + 1 + GU_CREDIT))
                        act.activation(f_gate[v % 2][:], banks[:, 2 * (v % 2), :], ACT.Silu).then_inc(S["f_silu"], 1)
                        act.wait_ge(S["f_mul"], L * PER["f_mul"] + g * 4 + (v + 1))
                        act.activation(act_hi[:, m, tokens(4 * half, 4)], f_prod[v % 2][:], ACT.Copy).then_inc(S["f_ahi"], 1)

                with act.Fori(0, GROUPS - 1) as g:
                    activations(g)
                    for m in range(GM):
                        act.wait_ge(S[f"fg_in{m}"], L * PER[f"fg_in{m}"] + g * 32 + 64)
                        act.activation(w_gu[m][0][:], w_gu[m][2][:], ACT.Copy).then_inc(S["f_hi"], 1)
                activations(GROUPS - 1)

            for t in range(T):
                act.wait_ge(S["d_add"], DEPTH * PER["d_add"] + 2 * (t + 1) - 2 * T + ADD_CREDIT)
                if t:
                    act.wait_ge(S["f_sq"], t)
                act.activation(row_square[:], X[:, t, :], ACT.Square, accum_out=row_ss[:, t:t + 1]).then_inc(S["f_sq"], 1)
                if 1 <= t <= FINAL_POOL:
                    act.wait_ge(S["f_rstd"], t)
                    act.activation(X[:, t - 1, :], X[:, t - 1, :], ACT.Copy, scale=row_rstd[:, t - 1:t]).then_inc(S["f_scaled"], 1)

        @block.vector
        def _(dve):
            dve.sem_inc(S["d_add"], ADD_CREDIT)
            tab = [0]

            def table_step(ins):
                tab[0] += 1
                ins.then_inc(S["tab_dve"], 1)
                dve.wait_ge(S["tab_dve"], tab[0])

            dve.wait_ge(S["const_in"], 64)
            dve.tensor_copy(ident_r[:], consts[:, C_IDENT:C_IDENT + P]).then_inc(S["ident_ok"], 1)
            dve.tensor_copy(mask_r[:], consts[:, C_MASK:C_MASK + P]).then_inc(S["ident_ok"], 1)
            dve.wait_ge(S["pos_in"], 16)
            table_step(dve.tensor_copy(pos_f[:], pos_int[:]))
            table_step(dve.tensor_tensor(ang[:], pos_f[:].unsqueeze(2).to_broadcast([P, T, 48]),
                                         consts[:, C_INVF:C_INVF + 48].unsqueeze(1).to_broadcast([P, T, 48]), ALU.mult))
            magic = 1.5 * 2.0 ** 23
            table_step(dve.tensor_scalar(turns[:], ang[:], 1.0 / (2 * math.pi), magic, ALU.mult, ALU.add))
            table_step(dve.tensor_scalar(turns[:], turns[:], magic, None, ALU.subtract))
            left = 2 * math.pi
            for bits in (5, 13, 30, 50):
                part = round(left * 2.0 ** bits) / 2.0 ** bits
                left -= part
                table_step(dve.scalar_tensor_tensor(red[:], turns[:], -part, ang[:] if bits == 5 else red[:], ALU.mult, ALU.add))
            top = float(np.nextafter(np.float32(math.pi), np.float32(0)))
            table_step(dve.tensor_scalar(red[:], red[:], top, -top, ALU.min, ALU.max))
            table_step(dve.scalar_tensor_tensor(cosarg[:], red[:], -1.0, red[:], ALU.mult, ALU.max))
            table_step(dve.tensor_scalar(cosarg[:], cosarg[:], -1.0, math.pi / 2, ALU.mult, ALU.add))
            dve.wait_ge(S["tab_act"], 1)

            with dve.Fori(0, DEPTH) as L:
                ring = [0]

                def low_ring():
                    ring[0] += 1
                    dve.wait_ge(S["tr_hi"], L * PER["tr_hi"] + ring[0])
                    return ring[0] - 1

                def scale_rows(tiles, roots):
                    for t in tiles:
                        dve.wait_ge(S["n_rstd"], L * PER["n_rstd"] + roots)
                        dve.tensor_scalar((rows, rows1)[t // 4][:, t % 4, :], X[:, t, :], row_rstd[:, t:t + 1], None, ALU.mult)\
                            .then_inc(S["n_xn"], 1)

                def low_rows(half, gain, blocks=range(KD)):
                    for k in blocks:
                        r = low_ring()
                        at_ = tokens(4 * half, 4)
                        bank = banks[:, NORM_BANKS[r % 4], :]
                        hi = ht_hi[:, k, at_].bitcast(F32)
                        if gain is None:
                            lo = dve.tensor_tensor(ht_lo[:, k, at_], bank, hi, ALU.subtract)
                        else:
                            lo = dve.scalar_tensor_tensor(ht_lo[:, k, at_], bank, gain[:, k:k + 1], hi, ALU.mult, ALU.subtract)
                        lo.then_inc(S["tr_free"], 1)

                dve.wait_ge(S["params_in"], L * PER["params_in"] + PER["params_in"])
                scale_rows(range(4), 1)
                low_rows(0, attn_gain, range(4))
                scale_rows(range(4, T), 2)
                low_rows(0, attn_gain, range(4, KD))
                low_rows(1, attn_gain)
                for m in range(2):
                    if m:
                        dve.wait_ge(S["lam"], L * PER["lam"] + 1)
                    dve.tensor_tensor_reduce(lam_prod[:], lam_vec[:, 2 * m, :], lam_vec[:, 2 * m + 1, :], 1.0, 0.0, ALU.mult,
                                             ALU.add, lam_sum[:, m:m + 1]).then_inc(S["lam"], 1)
                dve.wait_ge(S["lam"], L * PER["lam"] + 3)
                dve.tensor_tensor(neg_lam[:], lam_exp[:, 1:2], lam_exp[:, 0:1], ALU.subtract).then_inc(S["lam"], 1)
                dve.wait_ge(S["lam"], L * PER["lam"] + 4)
                dve.tensor_tensor(neg_lam[:], neg_lam[:], lam_const[:, 0:1], ALU.subtract)
                dve.tensor_scalar(subln[:], subln[:], lam_const[:, 1:2], None, ALU.mult).then_inc(S["lam"], 1)
                dve.wait_ge(S["lam"], L * PER["lam"] + 5)

                def rotate(z, a, b, t):
                    dve.tensor_tensor(a[:].rearrange("p v s d -> p (v s) d"), z.rearrange("p (v d) -> p v d", d=32),
                                      cos_d[:, t, :].unsqueeze(1).to_broadcast([P, 8, 32]), ALU.mult)
                    return dve.tensor_tensor(b[:], z.rearrange("p (v s d) -> p v s d", v=4, s=2)[:, :, ::-1, :],
                                             sin_d[:, t].unsqueeze(1).to_broadcast([P, 4, 2, 32]), ALU.mult)

                def diff_rotate(u):
                    if not 0 <= u < DIFF_UNITS:
                        return
                    bank = banks[:, z_bank(u), :]
                    dve.wait_ge(S["v_hi"], L * PER["v_hi"] + u + 1)
                    if u >= 2:
                        dve.wait_ge(S["rope_sum"], L * PER["rope_sum"] + u - 1)
                    rotate(bank[:, 0:2 * P], rope_a[u % 2], rope_b[u % 2], tile_of(u)).then_inc(S["rope_ab"], 1)
                    v = u % V_SLOTS
                    dve.tensor_tensor(dv[v][:, 1, :], bank[:, 2 * P:3 * P], dv[v][:, 0, :].bitcast(F32), ALU.subtract)\
                        .then_inc(S["z_free"], 1)

                def diff_low(u):
                    t = tile_of(u)
                    r = low_ring()
                    bank = banks[:, TR_BANKS[r % 2], :].rearrange("p (a m n) -> p a m n", a=2, m=2)
                    dve.scalar_tensor_tensor(dq_lo[:, :, tokens(t)], bank[:, 0], DIFF_SCALE, dq_hi[:, :, tokens(t)].bitcast(F32),
                                             ALU.mult, ALU.subtract)
                    low = dk[64:P, :, tokens(t)]
                    dve.tensor_tensor(low, bank[64:P, 1], low.bitcast(F32), ALU.subtract).then_inc(S["tr_free"], 1)

                def negated_max(j, a, m, t):
                    dve.wait_ge(S["s_done"], L * PER["s_done"] + j + 1)
                    dve.tensor_reduce(neg_max[:, a % 2, m:m + 1], SCORE[j % 2][:, 0:(t + 1) * P], AX_X, ALU.max, negate=True)\
                        .then_inc(S["s_max"], 1)

                def combine(a):
                    t = tile_of(a)
                    b = a % 2
                    dve.wait_ge(S["s_exp"], L * PER["s_exp"] + 2 * a + 2)
                    if a >= 4:
                        dve.wait_ge(S["o_out"], L * PER["o_out"] + a - 3)
                    dve.reciprocal(inv_sum[:, a % 4, :], exp_sum[:, b, :]).then_inc(S["inv_sum"], 1)
                    dve.wait_ge(S["inv_sum"], L * PER["inv_sum"] + a + 1)
                    dve.scalar_tensor_tensor(ratio[:, b:b + 1], exp_sum[:, b, 0:1], neg_lam[:], inv_sum[:, a % 4, 1:2],
                                             ALU.mult, ALU.mult).then_inc(S["lam_ratio"], 1)
                    dve.wait_ge(S["lam_ratio"], L * PER["lam_ratio"] + a + 1)
                    e = expo[b]
                    n = (t + 1) * P
                    dve.scalar_tensor_tensor(e[:, 0, 0:n], e[:, 1, 0:n], ratio[:, b:b + 1], e[:, 0, 0:n], ALU.mult, ALU.add)\
                        .then_inc(S["p_ready"], 1)

                def low_probs(t, hi=pt_hi, lo=pt_lo):
                    for b in range(0, t + 1, 4):
                        r = low_ring()
                        n = min(4, t + 1 - b)
                        dve.tensor_tensor(lo[:, b:b + n, :], banks[:, TR_BANKS[r % 2], 0:n * P].rearrange("p (b n) -> p b n", n=P),
                                          hi[:, b:b + n, :].bitcast(F32), ALU.subtract).then_inc(S["tr_free"], 1)

                def diff_take(a):
                    if 0 <= a < DIFF_UNITS:
                        dve.wait_ge(S["pv_done"], L * PER["pv_done"] + a + 1)
                        if a >= 2:
                            dve.wait_ge(S["o_out"], L * PER["o_out"] + a - 1)
                        take_output(d_sum[a % 2][:], banks[:, O_BANK, :], P)

                def take_output(dst, bank, width):
                    dve.tensor_reduce(dst, bank[:, 0:2 * width].rearrange("p (c d) -> p d c", c=2), AX_X, ALU.add).then_inc(S["o_free"], 1)

                def diff_maxima(a):
                    if 0 <= a < DIFF_UNITS:
                        for m in range(2):
                            negated_max(2 * a + m, a, m, tile_of(a))

                for a in DIFF_STEPS:
                    diff_take(a - 2)
                    if a % T:
                        diff_maxima(a)
                    if 0 <= a - 1 < DIFF_UNITS:
                        low_probs(tile_of(a - 1))
                    if a % T:
                        diff_rotate(a + T)
                    for u in diff_transposes(a):
                        diff_low(u)
                    if a % T == 0:
                        diff_rotate(a + T)
                    if a % T == 0:
                        diff_maxima(a)
                    if 0 <= a < DIFF_UNITS:
                        combine(a)

                def mla_latents(u):
                    t = tile_of(u)
                    z = m_z[u][:]
                    dve.wait_ge(S["m_sq"], L * PER["m_sq"] + u + 1)
                    zr = z[:, Q_RANK + KV_RANK:MLA_COLS].rearrange("p (s d) -> p s d", s=2)
                    if u >= 1:
                        dve.wait_ge(S["m_krope"], L * PER["m_krope"] + u)
                    dve.tensor_tensor(mk_a[:], zr, cos_m[:, t, :].unsqueeze(1).to_broadcast([P, 2, 16]), ALU.mult)
                    dve.tensor_tensor(mk_b[:], zr[:, ::-1, :], sin_m[:, t], ALU.mult).then_inc(S["m_kab"], 1)
                    dve.wait_ge(S["m_rstd"], L * PER["m_rstd"] + u + 1)
                    if u >= 2:
                        dve.wait_ge(S["tr_done"], L * PER["tr_done"] + ring[0])
                    dve.tensor_scalar(cn[u % 2][:, 0:2, :].rearrange("p b n -> p (b n)"), z[:, 0:Q_RANK], m_rs[:, u % 2, 0:1], None, ALU.mult)
                    dve.tensor_scalar(cn[u % 2][:, 2, :], z[:, Q_RANK:Q_RANK + KV_RANK], m_rs[:, u % 2, 1:2], None, ALU.mult)\
                        .then_inc(S["m_cn"], 1)

                def mla_low_latents(u):
                    r = low_ring()
                    dve.tensor_tensor(ct_lo[u % 2][:].rearrange("p b n -> p (b n)"), banks[:, TR_BANKS[r % 2], 0:3 * P],
                                      ct_hi[u % 2][:].rearrange("p b n -> p (b n)").bitcast(F32), ALU.subtract).then_inc(S["tr_free"], 1)

                def mla_up(u):
                    t = tile_of(u)
                    dve.wait_ge(S["m_nope"], L * PER["m_nope"] + u + 1)
                    qb = banks[:, 2 * (u % 2), 0:MLA_HEADS * MLA_QK].rearrange("p (h d) -> p h d", h=MLA_HEADS)
                    kvb = banks[:, 2 * (u % 2) + 1, :].rearrange("p (h d) -> p h d", h=MLA_HEADS)
                    qr = qb[:, :, NOPE:].rearrange("p h (s d) -> p h s d", s=2)
                    if u >= 1:
                        dve.wait_ge(S["m_qrope"], L * PER["m_qrope"] + u)
                    dve.tensor_tensor(mq_a[:], qr, cos_m[:, t, :].unsqueeze(1).unsqueeze(1).to_broadcast([P, MLA_HEADS, 2, 16]), ALU.mult)
                    dve.tensor_tensor(mq_b[:], qr[:, :, ::-1, :], sin_m[:, t].unsqueeze(1).to_broadcast([P, MLA_HEADS, 2, 16]),
                                      ALU.mult).then_inc(S["m_qab"], 1)
                    dve.tensor_tensor(m_v[:, t, :, 1, :], kvb[:, :, NOPE:], m_v[:, t, :, 0, :].bitcast(F32), ALU.subtract).then_inc(S["u_free"], 1)

                def mla_low(u):
                    t = tile_of(u)
                    r = low_ring()
                    bank = banks[0:MLA_QK, TR_BANKS[r % 2], :]
                    dve.scalar_tensor_tensor(mq_lo[:, tokens(t)], bank[:, 0:P], MLA_SCALE, mq_hi[:, tokens(t)].bitcast(F32),
                                             ALU.mult, ALU.subtract)
                    dve.tensor_tensor(mk_lo[:, tokens(t)], bank[:, P:2 * P], mk_hi[:, tokens(t)].bitcast(F32), ALU.subtract)\
                        .then_inc(S["tr_free"], 1)

                def mla_sum(a):
                    if 0 <= a < MLA_UNITS:
                        dve.wait_ge(S["s_exp"], L * PER["s_exp"] + 2 * DIFF_UNITS + a + 1)
                        if a >= 4:
                            dve.wait_ge(S["o_out"], L * PER["o_out"] + DIFF_UNITS + a - 3)
                        dve.reciprocal(inv_sum[:, a % 4, 0:1], exp_sum[:, a % 2, 0:1]).then_inc(S["inv_sum"], 1)

                def mla_take(a):
                    if 0 <= a < MLA_UNITS:
                        dve.wait_ge(S["pv_done"], L * PER["pv_done"] + DIFF_UNITS + a + 1)
                        dve.wait_ge(S["o_out"], L * PER["o_out"] + DIFF_UNITS + a - 1)
                        take_output(m_sum[a % 2][:], banks[:, O_BANK, :], MLA_V)

                for u in range(T + 4):
                    if u >= 4:
                        mla_low(u - 4)
                    if 1 <= u <= T:
                        mla_low_latents(u - 1)
                    if u < T:
                        mla_latents(u)
                    if 2 <= u < T + 2:
                        mla_up(u - 2)
                def ret_rotate(n):
                    if n == 0:
                        dve.wait_ge(S["z_free"], L * PER["z_free"] + Z_UNITS)
                    if n >= 3:
                        dve.wait_ge(S["rope_sum"], L * PER["rope_sum"] + ROPE_RET + n - 2)
                    rotate(r_z[n][:, 0:2 * P], r_ab[n % 3][0], r_ab[n % 3][1], n % T).then_inc(S["rope_ab"], 1)
                    dve.wait_ge(S["v_hi"], L * PER["v_hi"] + ROPE_RET + n + 1)
                    dve.tensor_tensor(rv[n % 5][:, :, 1, :], r_z[n][:, 2 * P:3 * P].rearrange("p (j d) -> p j d", j=2),
                                      rv[n % 5][:, :, 0, :].bitcast(F32), ALU.subtract).then_inc(S["r_vlo"], 1)
                    if n >= 3:
                        dve.wait_ge(S["tr_done"], L * PER["tr_done"] + ring[0])
                        dve.wait_ge(S["r_xz"], L * PER["r_xz"] + n - 2)
                    dve.wait_ge(S["rope_ab"], L * PER["rope_ab"] + ROPE_RET + n + 1)
                    dve.tensor_tensor(r_rot[n % 3][:], r_ab[n % 3][0][:].rearrange("p v s d -> p v (s d)"),
                                      r_ab[n % 3][1][:].rearrange("p v s d -> p v (s d)"), ALU.add).then_inc(S["rope_sum"], 1)

                def rs_count(n):
                    return n - n // T

                def ret_low(n):
                    r = low_ring()
                    dve.tensor_tensor(rt_lo[n % 3][:].rearrange("p b n -> p (b n)"), banks[:, TR_BANKS[r % 2], 0:3 * P],
                                      rt_hi[n % 3][:].rearrange("p b n -> p (b n)").bitcast(F32), ALU.subtract).then_inc(S["tr_free"], 1)

                def ret_inner(n):
                    p = n // T
                    if n == 0:
                        dve.wait_ge(S["ret_in"], L * PER["ret_in"] + PER["ret_in"])
                    dve.wait_ge(S["ri_done"], L * PER["ri_done"] + n + 1)
                    if n >= 1:
                        dve.wait_ge(S["r_atlo"], L * PER["r_atlo"] + n)
                    dve.tensor_tensor(r_at[:].rearrange("p (j n) -> p j n", j=2), banks[:, 0:2, 0:P], decay[:, p, :].rearrange("p (j n) -> p j n", j=2), ALU.mult).then_inc(S["r_at"], 1)
                    if n % T < T - 1:
                        i = rs_count(n)
                        dve.wait_ge(S["rs_done"], L * PER["rs_done"] + i + 1)
                        if i:
                            dve.wait_ge(S["r_sthi"], L * PER["r_sthi"] + i)
                            dve.wait_ge(S["r_stlo"], L * PER["r_stlo"] + i)
                        if n % T == 0:
                            st = dve.tensor_copy(r_st[:], banks[:, RET_STATE, 0:P])
                        else:
                            st = dve.scalar_tensor_tensor(r_st[:], r_st[:], cd[:, p:p + 1], banks[:, RET_STATE, 0:P], ALU.mult, ALU.add)
                        st.then_inc(S["r_st"], 1)

                def ret_moments(n):
                    b = n % 2
                    dve.wait_ge(S["ro_done"], L * PER["ro_done"] + n + 1)
                    if n >= 2:
                        dve.wait_ge(S["r_on"], L * PER["r_on"] + n - 1)
                    dve.tensor_reduce(r_sum[b][:], banks[:, RET_OUT[0]:RET_OUT[1] + 1, 0:P].rearrange("p j (c d) -> p j d c", c=2),
                                      AX_X, ALU.add).then_inc(S["r_take"], 1)
                    dve.wait_ge(S["r_take"], L * PER["r_take"] + n + 1)
                    for j in range(2):
                        st = dve.bn_stats(bn[:, b, j, :], r_sum[b][:, j, :])
                    st.then_inc(S["r_bn"], 1)
                    dve.wait_ge(S["r_bn"], L * PER["r_bn"] + n + 1)
                    dve.sem_inc(S["passed"], 1)
                    for j in range(2):
                        st = dve.bn_aggr(mv[:, b, j, :], bn[:, b, j, :])
                    st.then_inc(S["r_mv"], 1)

                def ret_normed(n):
                    b = n % 2
                    dve.wait_ge(S["r_rstd"], L * PER["r_rstd"] + n + 1)
                    if n >= 2:
                        dve.wait_ge(S["r_gw"], L * PER["r_gw"] + n - 1)
                    for j in range(2):
                        st = dve.tensor_scalar(r_norm[b][:, 64 * j:64 * j + 64], r_sum[b][:, j, :],
                                               mv[:, b, j, 0:1], r_rs[:, b, j:j + 1], ALU.subtract, ALU.mult)
                    st.then_inc(S["r_on"], 1)

                for a in MLA_STEPS:
                    mla_take(a - 3)
                    if a < MLA_UNITS and a % T:
                        negated_max(2 * DIFF_UNITS + a, a, 0, tile_of(a))
                    if 0 <= a - 1 < MLA_UNITS:
                        low_probs(tile_of(a - 1), mpt_hi[(a - 1) % 2], mpt_lo[(a - 1) % 2])
                    if a < MLA_UNITS and a % T == 0:
                        negated_max(2 * DIFF_UNITS + a, a, 0, tile_of(a))
                    if a + T < MLA_UNITS:
                        mla_low(a + T)
                    mla_sum(a - 1)
                    if a > MLA_UNITS:
                        ret_rotate(a - MLA_UNITS - 1)

                for n in range(1, RET_UNITS + 4):
                    if 1 <= n <= RET_UNITS:
                        ret_low(n - 1)
                    if 2 <= n < RET_UNITS + 2:
                        ret_inner(n - 2)
                    if n >= 4:
                        ret_normed(n - 4)
                    if n + 1 < RET_UNITS:
                        ret_rotate(n + 1)
                    if 3 <= n < RET_UNITS + 3:
                        ret_moments(n - 3)

                for half in range(2):
                    low_rows(half, None)
                for q in range(2 * T):
                    c, t = q // T, q % T
                    cols = slice(c * 512, (c + 1) * 512)
                    if q % 4 == 0 and q < T:
                        dve.wait_ge(S[f"x_back{q // 4}"], L * PER[f"x_back{q // 4}"] + 16)
                    dve.wait_ge(S["out_done"], L * PER["out_done"] + q + 1)
                    dve.tensor_tensor(X[:, t, cols], X[:, t, cols], banks[:, q % 4, :], ALU.add).then_inc(S["out_add"], 1)
                    if q == T + 4:
                        scale_rows(range(4), 3)
                    if q == 2 * T - 3:
                        low_rows(0, ffn_gain, range(4))
                    if q == 2 * T - 2:
                        low_rows(0, ffn_gain, range(4, KD))
                        scale_rows(range(4, T - 1), 4)
                    if q == 2 * T - 1:
                        scale_rows([T - 1], 5)
                dve.wait_ge(S["out_add"], L * PER["out_add"] + 2 * T)
                low_rows(1, ffn_gain)

                with dve.Fori(0, GROUPS) as g:
                    for v in range(4):
                        m, half = v // 2, v % 2
                        dve.wait_ge(S["f_silu"], L * PER["f_silu"] + g * 4 + (v + 1))
                        if v >= 2:
                            dve.wait_ge(S["f_act"], L * PER["f_act"] + g * 4 + (v - 1))
                        dve.tensor_tensor(f_prod[v % 2][:], banks[:, 2 * (v % 2) + 1, :], f_gate[v % 2][:], ALU.mult)\
                            .then_inc(S["f_mul"], 1)
                        dve.wait_ge(S["f_ahi"], L * PER["f_ahi"] + g * 4 + (v + 1))
                        dve.tensor_tensor(act_lo[:, m, tokens(4 * half, 4)], f_prod[v % 2][:],
                                          act_hi[:, m, tokens(4 * half, 4)].bitcast(F32), ALU.subtract).then_inc(S["f_act"], 1)
                    for q in range(2 * T):
                        t, c = q // 2, q % 2
                        cols = slice(c * 512, (c + 1) * 512)
                        dve.wait_ge(S["fd_done"], L * PER["fd_done"] + g * 2 * T + (q + 1 + D_CREDIT))
                        dve.tensor_tensor(X[:, t, cols], X[:, t, cols], banks[:, 4 + q % 4, :], ALU.add).then_inc(S["d_add"], 1)
                    dve.wait_ge(S["d_add"], L * PER["d_add"] + g * 2 * T + (2 * T + ADD_CREDIT))

            dve.wait_ge(S["final_in"], 16)
            for t in range(FINAL_POOL, T):
                dve.wait_ge(S["f_rstd"], t + 1)
                dve.scalar_tensor_tensor(X[:, t, :], X[:, t, :], row_rstd[:, t:t + 1], final_gain[:], ALU.mult, ALU.mult)\
                    .then_inc(S["y_dve"], 1)

        @block.gpsimd
        def _(pool):
            pool.memset(minus_half, -0.5).then_inc(S["half_ok"], 1)
            pool.wait_ge(S["half_ok"], 1)

            def inverse_root(out_, in_):
                return pool.tensor_tensor(out_, in_, minus_half[:, 0:in_.shape[1]], ALU.pow)

            with pool.Fori(0, DEPTH) as L:

                def inverse_roots(norm, groups, done):
                    for i, (start, end) in enumerate(groups):
                        cols = slice(start, end)
                        if norm:
                            pool.wait_ge(S["n_xn"], L * PER["n_xn"] + T)
                        pool.wait_ge(S["n_sq"], L * PER["n_sq"] + norm * T + end)
                        pool.sem_inc(S["passed"], 1)
                        pool.tensor_scalar(row_ms[:, cols], row_ss[:, cols], 1.0 / D, NORM_EPS, ALU.mult, ALU.add).then_inc(S["n_ms"], 1)
                        pool.wait_ge(S["n_ms"], L * PER["n_ms"] + done + i + 1)
                        inverse_root(row_rstd[:, cols], row_ms[:, cols]).then_inc(S["n_rstd"], 1)

                def weights(chunk, parts=range(PARTS)):
                    if chunk == CH_UKV:
                        pool.wait_ge(S["w_hi"], L * PER["w_hi"] + PARTS * (chunk + 1))
                        pool.tensor_tensor(w_uq[1][:], w_uq[2][:], w_uq[0][:].bitcast(F32), ALU.subtract)
                        pool.tensor_tensor(w_ukv[1][:], w_ukv[2][:], w_ukv[0][:].bitcast(F32), ALU.subtract).then_inc(S["w_lo"], 1)
                        return
                    w = (w_diff[chunk % 2] if chunk < CH_MLA else w_mla if chunk == CH_MLA else
                         w_ret if chunk < CH_OUT else w_o[chunk % 2])
                    step = KD // PARTS
                    for i in parts:
                        pool.wait_ge(S["w_hi"], L * PER["w_hi"] + PARTS * chunk + i + 1)
                        k = slice(i * step, (i + 1) * step)
                        st = pool.tensor_tensor(w[1][:, k, :], w[2][:, k, :], w[0][:, k, :].bitcast(F32), ALU.subtract)
                        if i == PARTS - 1:
                            st.then_inc(S["w_lo"], 1)

                inverse_roots(0, [(0, 4), (4, T)], 0)
                weights(0)

                def rotation(n, a, b, dst, copies):
                    pool.wait_ge(S["rope_ab"], L * PER["rope_ab"] + n + 1)
                    a, b = (x[:].rearrange("p v s d -> p v (s d)").unsqueeze(2).to_broadcast([P, 4, copies, 64]) for x in (a, b))
                    return pool.tensor_tensor(dst[:] if copies > 1 else dst[:].unsqueeze(2), a, b, ALU.add)

                def diff_rotation(u):
                    if not 0 <= u < DIFF_UNITS:
                        return
                    if u >= 2:
                        pool.wait_ge(S["tr_done"], L * PER["tr_done"] + qk_ring[u - 2])
                    rotation(u, rope_a[u % 2], rope_b[u % 2], qk_rot[u % 2], 2).then_inc(S["rope_sum"], 1)

                def diff_root(a):
                    if not 0 <= a < DIFF_UNITS:
                        return
                    b = slice(a % 2, a % 2 + 1)
                    pool.wait_ge(S["o_sq"], L * PER["o_sq"] + a + 1)
                    pool.sem_inc(S["passed"], 1)
                    pool.tensor_scalar(o_ms[:, b], o_ss[:, b], 1.0 / (2 * DIFF_DIM), SUBLN_EPS, ALU.mult, ALU.add).then_inc(S["o_ms"], 1)
                    pool.wait_ge(S["o_ms"], L * PER["o_ms"] + 3 * a + 1)
                    inverse_root(o_rs[:, b], o_ms[:, b]).then_inc(S["o_ms"], 1)
                    pool.wait_ge(S["o_ms"], L * PER["o_ms"] + 3 * a + 2)
                    pool.tensor_tensor(o_rr[:, b], o_rs[:, b], inv_sum[:, a % 4, 0:1], ALU.mult).then_inc(S["o_ms"], 1)
                    if a >= 2:
                        pool.wait_ge(S[f"mix_out{a % 2}"], L * PER[f"mix_out{a % 2}"] + 16 * (a // 2))
                    pool.wait_ge(S["o_ms"], L * PER["o_ms"] + 3 * a + 3)
                    pool.tensor_tensor(d_mx[a % 2][:], d_sum[a % 2][:], o_rr[:, b].to_broadcast([P, P]), ALU.mult).then_inc(S["o_rr"], 1)
                    pool.wait_ge(S["o_rr"], L * PER["o_rr"] + a + 1)
                    pool.tensor_tensor(d_mx[a % 2][:], d_mx[a % 2][:], subln[:], ALU.mult).then_inc(S["o_out"], 1)

                for a in DIFF_STEPS:
                    diff_rotation(a + T)
                    diff_root(a - 2)
                    if a < DIFF_UNITS and a // T + 2 < CH_UKV and 3 <= a % T < 3 + PARTS:
                        weights(a // T + 2, [a % T - 3])
                    elif a == (CH_UKV - 2) * T + 1:
                        pool.wait_ge(S["w_in1"], L * PER["w_in1"] + 16 * 10)
                        pool.sem_inc(S["passed"], 1)
                        for k in range(2):
                            pool.tensor_scalar(w_uq[2][:, k, :], w_uq[2][:, k, :], q_gain[:, k:k + 1], None, ALU.mult)
                        pool.tensor_scalar(w_ukv[2][:], w_ukv[2][:], kv_gain[:], None, ALU.mult).then_inc(S["w_gain"], 1)
                    elif a == (CH_UKV - 2) * T + 3:
                        weights(CH_UKV)

                def mla_roots(t):
                    u = T - 1 - t
                    b = u % 2
                    pool.wait_ge(S["m_sq"], L * PER["m_sq"] + u + 1)
                    pool.sem_inc(S["passed"], 1)
                    pool.tensor_scalar(m_msq[:, b, 0:1], m_ss[:, b, 0:1], 1.0 / Q_RANK, NORM_EPS, ALU.mult, ALU.add)
                    pool.tensor_scalar(m_msq[:, b, 1:2], m_ss[:, b, 1:2], 1.0 / KV_RANK, NORM_EPS, ALU.mult, ALU.add).then_inc(S["m_ms"], 2)
                    pool.wait_ge(S["m_ms"], L * PER["m_ms"] + 2 * u + 2)
                    inverse_root(m_rs[:, b, :], m_msq[:, b, :]).then_inc(S["m_rstd"], 1)
                    pool.wait_ge(S["m_kab"], L * PER["m_kab"] + u + 1)
                    if u == 0:
                        pool.wait_ge(S["pv_done"], L * PER["pv_done"] + DIFF_HEADS * T)
                        pool.wait_ge(S["mix_out0"], L * PER["mix_out0"] + 16 * DIFF_HEADS * T // 2)
                        pool.wait_ge(S["mix_out1"], L * PER["mix_out1"] + 16 * DIFF_HEADS * T // 2)
                    pool.tensor_tensor(m_k[:, t, :, NOPE:], mk_a[:].rearrange("p s d -> p (s d)").unsqueeze(1).to_broadcast([P, MLA_HEADS, ROPE]),
                                       mk_b[:].rearrange("p s d -> p (s d)").unsqueeze(1).to_broadcast([P, MLA_HEADS, ROPE]), ALU.add)\
                        .then_inc(S["m_krope"], 1)

                def mla_q_rotation(t):
                    u = T - 1 - t
                    pool.wait_ge(S["m_qab"], L * PER["m_qab"] + u + 1)
                    pool.tensor_tensor(m_q[:, t, :, NOPE:], mq_a[:].rearrange("p h s d -> p h (s d)"), mq_b[:].rearrange("p h s d -> p h (s d)"),
                                       ALU.add).then_inc(S["m_qrope"], 1)

                for u in range(T + 2):
                    if u < T:
                        mla_roots(tile_of(u))
                    if u >= 2:
                        mla_q_rotation(tile_of(u - 2))
                for step in range(MLA_UNITS + 3):
                    a = step - 3
                    if a >= 0:
                        pool.wait_ge(S["inv_sum"], L * PER["inv_sum"] + DIFF_UNITS + a + 1)
                        pool.wait_ge(S[f"mix_out{a % 2}"], L * PER[f"mix_out{a % 2}"] + 16 * ((DIFF_UNITS + a) // 2))
                        pool.wait_ge(S["o_free"], L * PER["o_free"] + DIFF_UNITS + a + 1)
                        pool.tensor_tensor(m_mx[a % 2][:], m_sum[a % 2][:], inv_sum[:, a % 4, 0:1].to_broadcast([P, MLA_V]), ALU.mult)\
                            .then_inc(S["o_out"], 1)
                    for p in range(RET_PAIRS):
                        if 0 <= step - ROUND_RET[p] < PARTS:
                            weights(CH_RET + p, [step - ROUND_RET[p]])

                def rs_count(n):
                    return n - n // T

                def ret_low_k(n):
                    b = n % 2
                    pool.wait_ge(S["r_kzhi"], L * PER["r_kzhi"] + n + 1)
                    pool.tensor_tensor(rk_lo[b][:], r_xzt[n % 3][:, 2:4, :].rearrange("p a d -> p (a d)"), rk_hi[b][:].bitcast(F32), ALU.subtract)\
                        .then_inc(S["r_kzlo"], 1)

                def ret_inner(n):
                    pool.wait_ge(S["r_athi"], L * PER["r_athi"] + n + 1)
                    pool.tensor_tensor(r_at_lo[n % 2][:], r_at[:], r_at_hi[n % 2][:].bitcast(F32), ALU.subtract).then_inc(S["r_atlo"], 1)
                    if n % T < T - 1:
                        i = rs_count(n)
                        pool.wait_ge(S["r_sthi"], L * PER["r_sthi"] + i + 1)
                        b = i % 3
                        pool.tensor_tensor(r_st2[b][:, 1, :], r_st[:], r_st2[b][:, 0, :].bitcast(F32), ALU.subtract).then_inc(S["r_stlo"], 1)

                def ret_root(n):
                    b = n % 2
                    pool.wait_ge(S["r_mv"], L * PER["r_mv"] + n + 1)
                    pool.sem_inc(S["passed"], 1)
                    pool.tensor_scalar(r_ms[:, b, :], mv[:, b, :, 1], GN_EPS, None, ALU.add).then_inc(S["r_ms"], 1)
                    pool.wait_ge(S["r_ms"], L * PER["r_ms"] + n + 1)
                    inverse_root(r_rs[:, b, :], r_ms[:, b, :]).then_inc(S["r_rstd"], 1)

                def ret_finish(n):
                    b, p = n % 2, n // T
                    pool.wait_ge(S["r_on"], L * PER["r_on"] + n + 1)
                    cols = slice(p * P, (p + 1) * P)
                    if n == 0:
                        pool.wait_ge(S["ret_in"], L * PER["ret_in"] + PER["ret_in"])
                    pool.tensor_tensor(r_mx[b][:], r_norm[b][:], gn_w[:, cols], ALU.mult).then_inc(S["r_gw"], 1)
                    pool.wait_ge(S["r_gw"], L * PER["r_gw"] + n + 1)
                    pool.tensor_tensor(r_mx[b][:], r_mx[b][:], gn_b[:, cols], ALU.add).then_inc(S["r_gb"], 1)
                    pool.wait_ge(S["r_gb"], L * PER["r_gb"] + n + 1)
                    pool.tensor_tensor(mixed_rows[:, n % T, MIX_RET + p * P:MIX_RET + (p + 1) * P], r_mx[b][:], r_gate[n % 6][:], ALU.mult)\
                        .then_inc(S["r_mx"], 1)

                for n in range(RET_UNITS + 4):
                    if 1 <= n <= RET_UNITS:
                        ret_low_k(n - 1)
                    if 2 <= n < RET_UNITS + 2:
                        ret_inner(n - 2)
                    if n >= 4:
                        ret_finish(n - 4)
                    if 3 <= n < RET_UNITS + 3:
                        ret_root(n - 3)
                    if 2 <= n < 2 + PARTS:
                        weights(CH_OUT, [n - 2])
                weights(CH_OUT + 1)
                for m in range(GM):
                    pool.wait_ge(S["f_hi"], L * PER["f_hi"] + m + 1)
                    pool.tensor_tensor(w_gu[m][1][:], w_gu[m][2][:], w_gu[m][0][:].bitcast(F32), ALU.subtract).then_inc(S["f_lo"], 1)
                inverse_roots(1, [(0, 4), (4, T - 1), (T - 1, T)], 2)

                with pool.Fori(0, GROUPS - 1) as g:
                    for i, w in enumerate((w_dn, w_gu[0], w_gu[1])):
                        pool.wait_ge(S["f_hi"], L * PER["f_hi"] + g * 3 + (i + 3))
                        pool.tensor_tensor(w[1][:], w[2][:], w[0][:].bitcast(F32), ALU.subtract).then_inc(S["f_lo"], 1)
                pool.wait_ge(S["f_hi"], L * PER["f_hi"] + PER["f_hi"])
                pool.tensor_tensor(w_dn[1][:], w_dn[2][:], w_dn[0][:].bitcast(F32), ALU.subtract).then_inc(S["f_lo"], 1)

            pool.wait_ge(S["final_in"], 16)
            for t in range(T):
                col = slice(t, t + 1)
                pool.wait_ge(S["f_sq"], t + 1)
                pool.tensor_scalar(row_ms[:, col], row_ss[:, col], 1.0 / D, NORM_EPS, ALU.mult, ALU.add).then_inc(S["f_ms"], 1)
                pool.wait_ge(S["f_ms"], t + 1)
                inverse_root(row_rstd[:, col], row_ms[:, col]).then_inc(S["f_rstd"], 1)
                if 1 <= t <= FINAL_POOL:
                    pool.wait_ge(S["f_scaled"], t)
                    pool.tensor_tensor(X[:, t - 1, :], X[:, t - 1, :], final_gain[:], ALU.mult).then_inc(S["y_pool"], 1)


_INS = ["x", "positions", "attn_norm", "w_in", "diff_lam_q1", "diff_lam_k1", "diff_lam_q2", "diff_lam_k2", "diff_subln",
        "mla_q_norm", "mla_w_uq", "mla_kv_norm", "mla_w_ukv", "ret_gn_w", "ret_gn_b", "w_out", "ffn_norm", "w_gate",
        "w_up", "w_down", "final_norm"]
_OUTS = [((1, SEQ, D), "float32")]


def kernel(**inputs):
    import numpy as _np
    import concourse.bacc as _bacc
    from concourse import mybir as _mybir
    from concourse.bass_utils import run_bass_kernel_spmd as _run

    nc = _bacc.Bacc("TRN2", target_bir_lowering=False, num_devices=1)
    arrays, args = {}, []
    for name in _INS:
        a = _np.ascontiguousarray(inputs[name])
        arrays[f"in_{name}_dram"] = a
        args.append(nc.dram_tensor(f"in_{name}_dram", a.shape, _mybir.dt.from_np(a.dtype), kind="ExternalInput").ap())
    for i, (shape, dtype) in enumerate(_OUTS):
        dt = _mybir.dt.from_np(_np.dtype(dtype))
        args.append(nc.dram_tensor(f"out_{i}_dram", shape, dt, kind="ExternalOutput").ap())
    hybrid_block_kernel(nc, *args)
    r = _run(nc, [arrays], core_ids=[0])
    got = tuple(r.results[0][f"out_{i}_dram"] for i in range(len(_OUTS)))
    return got[0]
```
